# Optimizing a Trainium2 kernel written in Bass

```python
import jax, jax.numpy as jnp
from jax import lax
import numpy as np

D_MODEL = 1024
BATCH = 1
SEQ = 256
DEPTH = 2

GRID_W = 64
CTX_LEN = 256
N_EVEN = (DEPTH + 1) // 2
N_ODD = DEPTH // 2
N_MOD = 6
EPS = 1e-6
D_CONV = D_MODEL // 2
CONV_W = 3
D_POOL = D_MODEL // 2
POOL_WINDOWS = (2, 4, 8, 16)
N_POOL_GROUPS = len(POOL_WINDOWS)
POOL_GROUP = D_POOL // N_POOL_GROUPS
D_MIX_IN = 3 * D_CONV + D_POOL
NA_HEADS = 16
NA_HEAD_DIM = D_MODEL // NA_HEADS
NA_ROWS = 8
NA_COLS = 16
D_FF = 2816
N_EXPERTS = 8
TOP_K = 2
D_FF_EXPERT = 3584

kernel_name = 'hybrid_conv_pool_natten_moe_dit'

def rmsnorm(x, g):
    x32 = x.astype(jnp.float32)
    y = x32 * lax.rsqrt(jnp.mean(x32 * x32, axis=-1, keepdims=True) + EPS)
    return (y * g.astype(jnp.float32)).astype(x.dtype)

def modulate(h, shift, scale):
    return h * (1 + scale) + shift

def adaln(cond, w, b):
    m = jax.nn.silu(cond) @ w + b
    return m.reshape(m.shape[:-1] + (N_MOD, D_MODEL))

def short_conv(z, w):
    L = z.shape[1]
    pad = CONV_W // 2
    zp = jnp.pad(z, ((0, 0), (pad, CONV_W - 1 - pad), (0, 0)))
    out = zp[:, 0:L] * w[0]
    for k in range(1, CONV_W):
        out = out + zp[:, k:k + L] * w[k]
    return out

def multiscale_pool(p, w_grp, scale):
    B_, L, _ = p.shape
    p32 = p.astype(jnp.float32)
    csum = jnp.concatenate([jnp.zeros_like(p32[:, :1]), jnp.cumsum(p32, axis=1)], axis=1)
    t = np.arange(L)
    pooled = []
    for g, win in enumerate(POOL_WINDOWS):
        lo = np.maximum(t - win // 2, 0)
        hi = np.minimum(t + (win - 1 - win // 2), L - 1)
        cs = csum[..., g * POOL_GROUP:(g + 1) * POOL_GROUP]
        cnt = (hi - lo + 1).astype(np.float32)[None, :, None]
        pooled.append((cs[:, hi + 1] - cs[:, lo]) / cnt)
    pooled = jnp.stack(pooled, axis=2).astype(p.dtype)
    diff = pooled - p.reshape(B_, L, N_POOL_GROUPS, POOL_GROUP)
    y = jnp.einsum('blgc,gcd->blgd', diff, w_grp)
    return y.reshape(B_, L, D_POOL) * scale

def conv_pool_mixer(h, w_in, conv_w, pool_w, pool_scale, w_out):
    u = h @ w_in
    gate_b, gate_c, val, pin = jnp.split(u, [D_CONV, 2 * D_CONV, 3 * D_CONV], axis=-1)
    y_conv = gate_b * short_conv(gate_c * val, conv_w)
    y_pool = multiscale_pool(pin, pool_w, pool_scale)
    return jnp.concatenate([y_conv, y_pool], axis=-1) @ w_out

def _heads(t):
    return t.reshape(t.shape[0], t.shape[1], NA_HEADS, NA_HEAD_DIM)

def neighbourhood_attention(q, k, v, kc, vc, rpb):
    B_, L, H, dh = q.shape
    rows = L // GRID_W
    kr = min(NA_ROWS, rows)
    scale = dh ** -0.5
    qg = q.reshape(B_, rows, GRID_W, H, dh)
    kg = k.reshape(B_, rows, GRID_W, H, dh)
    vg = v.reshape(B_, rows, GRID_W, H, dh)
    jcol = np.arange(GRID_W)
    col_start = np.clip(jcol - NA_COLS // 2, 0, GRID_W - NA_COLS)
    col_idx = col_start[:, None] + np.arange(NA_COLS)[None, :]
    dc_idx = col_idx - jcol[:, None] + (NA_COLS - 1)
    rpb_c = rpb[:, :, dc_idx]
    n_loc = kr * NA_COLS

    def row_block(r):
        q_r = lax.dynamic_index_in_dim(qg, r, axis=1, keepdims=False)
        start = jnp.clip(r - NA_ROWS // 2, 0, rows - kr)
        k_band = lax.dynamic_slice_in_dim(kg, start, kr, axis=1)
        v_band = lax.dynamic_slice_in_dim(vg, start, kr, axis=1)
        k_win = k_band[:, :, col_idx]
        v_win = v_band[:, :, col_idx]
        dr_idx = start + jnp.arange(kr) - r + (NA_ROWS - 1)
        bias = jnp.take(rpb_c, dr_idx, axis=1).transpose(0, 2, 1, 3)
        s_loc = jnp.einsum('bjhd,brjchd->bhjrc', q_r, k_win).astype(jnp.float32) * scale + bias
        s_ctx = jnp.einsum('bjhd,bnhd->bhjn', q_r, kc).astype(jnp.float32) * scale
        logits = jnp.concatenate([s_loc.reshape(B_, H, GRID_W, n_loc), s_ctx], axis=-1)
        p = jax.nn.softmax(logits, axis=-1).astype(v.dtype)
        p_loc = p[..., :n_loc].reshape(B_, H, GRID_W, kr, NA_COLS)
        p_ctx = p[..., n_loc:]
        return (jnp.einsum('bhjrc,brjchd->bjhd', p_loc, v_win)
                + jnp.einsum('bhjn,bnhd->bjhd', p_ctx, vc))

    out = lax.map(row_block, jnp.arange(rows))
    return out.transpose(1, 0, 2, 3, 4).reshape(B_, L, H * dh)

def context_attention(qc, kc, vc):
    B_, N, H, dh = qc.shape
    s = jnp.einsum('bmhd,bnhd->bhmn', qc, kc).astype(jnp.float32) * (dh ** -0.5)
    p = jax.nn.softmax(s, axis=-1).astype(vc.dtype)
    return jnp.einsum('bhmn,bnhd->bmhd', p, vc).reshape(B_, N, H * dh)

def swiglu(h, w_gate, w_up, w_down):
    return (jax.nn.silu(h @ w_gate) * (h @ w_up)) @ w_down

def moe_swiglu(h, w_router, we_gate, we_up, we_down):
    shp = h.shape
    t = h.reshape(-1, D_MODEL)
    logits = (t @ w_router).astype(jnp.float32)
    top_v, top_i = lax.top_k(logits, TOP_K)
    gates = jax.nn.softmax(top_v, axis=-1)
    comb = jnp.sum(jax.nn.one_hot(top_i, N_EXPERTS, dtype=jnp.float32) * gates[..., None], axis=1).astype(h.dtype)
    out = jnp.zeros_like(t)
    for e in range(N_EXPERTS):
        out = out + comb[:, e:e + 1] * swiglu(t, we_gate[e], we_up[e], we_down[e])
    return out.reshape(shp)

def channel_mix(layer, h, w_ff_gate, w_ff_up, w_ff_down, w_router, we_gate, we_up, we_down):
    j = layer // 2
    if layer % 2 == 0:
        return swiglu(h, w_ff_gate[j], w_ff_up[j], w_ff_down[j])
    return moe_swiglu(h, w_router[j], we_gate[j], we_up[j], we_down[j])

def setup_inputs(seed: int = 0) -> dict:
    key = jax.random.key(seed)
    ks = iter(jax.random.split(key, 32))
    D = D_MODEL

    def nrm(shape, scale):
        return jax.random.normal(next(ks), shape, jnp.float32) * scale

    return {
        'x': nrm((BATCH, SEQ, D), 1.0),
        'c': nrm((BATCH, D), 1.0),
        'ctx': nrm((BATCH, CTX_LEN, D), 1.0),
        'c_ctx': nrm((D,), 1.0),
        'w_mod': nrm((DEPTH, D, N_MOD * D), 0.5 * D ** -0.5),
        'b_mod': nrm((DEPTH, N_MOD * D), 0.02),
        'g_mix': 1.0 + nrm((DEPTH, D), 0.05),
        'g_ffn': 1.0 + nrm((DEPTH, D), 0.05),
        'g_final': 1.0 + nrm((D,), 0.05),
        'w_in_ab': nrm((N_EVEN, D, D_MIX_IN), D ** -0.5),
        'conv_w': nrm((N_EVEN, CONV_W, D_CONV), CONV_W ** -0.5),
        'pool_w': nrm((N_EVEN, N_POOL_GROUPS, POOL_GROUP, POOL_GROUP), POOL_GROUP ** -0.5),
        'pool_scale': 1.0 + nrm((N_EVEN, D_POOL), 0.1),
        'w_out_ab': nrm((N_EVEN, D_CONV + D_POOL, D), (D_CONV + D_POOL) ** -0.5),
        'w_ff_gate': nrm((N_EVEN, D, D_FF), D ** -0.5),
        'w_ff_up': nrm((N_EVEN, D, D_FF), D ** -0.5),
        'w_ff_down': nrm((N_EVEN, D_FF, D), D_FF ** -0.5),
        'w_qkv': nrm((N_ODD, D, 3 * D), D ** -0.5),
        'rpb': nrm((N_ODD, NA_HEADS, 2 * NA_ROWS - 1, 2 * NA_COLS - 1), 0.1),
        'w_out_na': nrm((N_ODD, D, D), D ** -0.5),
        'w_router': nrm((N_ODD, D, N_EXPERTS), D ** -0.5),
        'we_gate': nrm((N_ODD, N_EXPERTS, D, D_FF_EXPERT), D ** -0.5),
        'we_up': nrm((N_ODD, N_EXPERTS, D, D_FF_EXPERT), D ** -0.5),
        'we_down': nrm((N_ODD, N_EXPERTS, D_FF_EXPERT, D), D_FF_EXPERT ** -0.5),
    }

def reference(x, c, ctx, c_ctx, w_mod, b_mod, g_mix, g_ffn, g_final, w_in_ab, conv_w, pool_w, pool_scale,
              w_out_ab, w_ff_gate, w_ff_up, w_ff_down, w_qkv, rpb, w_out_na, w_router, we_gate, we_up, we_down):
    h_lat, h_ctx = x, ctx
    for i in range(DEPTH):
        last = i == DEPTH - 1
        j = i // 2
        m_lat = adaln(c, w_mod[i], b_mod[i])[:, :, None, :]
        m_ctx = adaln(c_ctx, w_mod[i], b_mod[i])[None, :, None, :]
        a_lat = modulate(rmsnorm(h_lat, g_mix[i]), m_lat[:, 0], m_lat[:, 1])
        if i % 2 == 0:
            y_lat = conv_pool_mixer(a_lat, w_in_ab[j], conv_w[j], pool_w[j], pool_scale[j], w_out_ab[j])
        else:
            a_ctx = modulate(rmsnorm(h_ctx, g_mix[i]), m_ctx[:, 0], m_ctx[:, 1])
            q, k, v = (_heads(t) for t in jnp.split(a_lat @ w_qkv[j], 3, axis=-1))
            kc, vc = (_heads(t) for t in jnp.split(a_ctx @ w_qkv[j][:, D_MODEL:], 2, axis=-1))
            y_lat = neighbourhood_attention(q, k, v, kc, vc, rpb[j]) @ w_out_na[j]
        h_lat = h_lat + m_lat[:, 2] * y_lat
        f_lat = modulate(rmsnorm(h_lat, g_ffn[i]), m_lat[:, 3], m_lat[:, 4])
        h_lat = h_lat + m_lat[:, 5] * channel_mix(i, f_lat, w_ff_gate, w_ff_up, w_ff_down,
                                                  w_router, we_gate, we_up, we_down)
        if not last:
            if i % 2 == 0:
                a_ctx = modulate(rmsnorm(h_ctx, g_mix[i]), m_ctx[:, 0], m_ctx[:, 1])
                y_ctx = conv_pool_mixer(a_ctx, w_in_ab[j], conv_w[j], pool_w[j], pool_scale[j], w_out_ab[j])
            else:
                qc = _heads(a_ctx @ w_qkv[j][:, :D_MODEL])
                y_ctx = context_attention(qc, kc, vc) @ w_out_na[j]
            h_ctx = h_ctx + m_ctx[:, 2] * y_ctx
            f_ctx = modulate(rmsnorm(h_ctx, g_ffn[i]), m_ctx[:, 3], m_ctx[:, 4])
            h_ctx = h_ctx + m_ctx[:, 5] * channel_mix(i, f_ctx, w_ff_gate, w_ff_up, w_ff_down,
                                                      w_router, we_gate, we_up, we_down)
    return rmsnorm(h_lat, g_final)


_drawn_inputs = setup_inputs


def setup_inputs(seed=0):
    import zlib

    import numpy as np

    out = dict(_drawn_inputs(seed))
    spreads = {}
    factors = {}
    for name, (base, spread) in spreads.items():
        noise = np.random.default_rng([zlib.crc32(name.encode()), seed]).standard_normal(out[name].shape)
        drawn = base * np.exp(spread * noise) if base else spread * noise
        out[name] = __import__('jax').numpy.asarray(drawn.astype(out[name].dtype))
    for name, factor in factors.items():
        out[name] = (out[name] * factor).astype(out[name].dtype)
    return out
```

```python
from contextlib import ExitStack

import concourse.bass as bass
from concourse import mybir

F32 = mybir.dt.float32
F32R = mybir.dt.float32r
I32 = mybir.dt.int32
ALU = mybir.AluOpType
ACT = mybir.ActivationFunctionType
AXX = mybir.AxisListType.X

P = 128
D = 1024
KD = D // P
T = 256
TT = T // P
NS = 2
UC = 512
FS = 256
EPS = 1e-6
GRID = 64
HEADS, HD = 16, 64
WINR, WINC = 8, 16
DFF, DFE, NE, TOPK = 2816, 3584, 8, 2
STEPS0 = DFF // FS
STEPSE = DFE // FS
CAP = P
OVER = (TOPK * T) // (CAP + 1)
JOBS = NE + OVER
ZW = GRID * (GRID + 1)
NDR = 2 * WINR - 1
NDC = 2 * WINC - 1
C = 2
MODU = 6 * D // UC
WINDOWS = (2, 4, 8, 16)

GU_STREAM = 4 + 2 + STEPS0
GU_L1 = NS * GU_STREAM
GU_MOE = GU_L1 + 4 + 6 + 2
D_MOE = NS * STEPS0
SLOT_STREAM = (GU_STREAM - GU_STREAM // 2, GU_STREAM // 2)
DSLOT_STREAM = (STEPS0 - STEPS0 // 2, STEPS0 // 2)


def it0(i):
    return 0 if i is None else i


class Unit:

    def __init__(self, slot, n, uses, follows_same_slot):
        self.slot, self.n, self.uses = slot, n, uses
        self.before = n if follows_same_slot else n - 1


def gu0(s, k, i=0):
    return Unit(k % 2, s * GU_STREAM + i * 2 + k, s * SLOT_STREAM[k % 2] + i + (k // 2 + 1), k == 0)


def gu1(k, j=None, i=0):
    if j is None:
        return Unit(k % 2, GU_L1 + k, NS * SLOT_STREAM[k % 2] + k // 2 + 1, k == 0)
    base = GU_MOE - GU_L1
    return Unit(k % 2, j * STEPSE + i * 2 + (GU_MOE + k),
                j * (STEPSE // 2) + i + (NS * SLOT_STREAM[k % 2] + base // 2 + k // 2 + 1), False)


def d0(s, k, i=0):
    return Unit(k % 2, s * STEPS0 + i * 2 + k, s * DSLOT_STREAM[k % 2] + i + (k // 2 + 1), k == 0)


def d1(j, k, i=0):
    return Unit(k % 2, j * STEPSE + i * 2 + (D_MOE + k),
                j * (STEPSE // 2) + i + (NS * DSLOT_STREAM[k % 2] + k // 2 + 1), k == 0)


def backbone(nc, x, c, ctx_in, c_ctx, w_mod, b_mod, g_mix, g_ffn, g_final, w_in, conv_w, pool_w,
             pool_scale, w_out, w_gate, w_up, w_down, w_qkv, rpb, w_na, w_router, we_gate, we_up,
             we_down, out):
    stack = ExitStack()
    with stack:
        def sb(name, shape, dt=F32):
            return stack.enter_context(nc.sbuf_tensor(name, shape, dt))

        def ps(name, shape):
            return stack.enter_context(nc.psum_tensor(name, shape, F32))

        owned = {"act": [], "dve": [], "pe": [], "pool": []}

        def sem(name, owner=None):
            s = stack.enter_context(nc.semaphore(name))
            if owner:
                owned[owner].append(s)
            return s

        raw_gu = sb("raw_gu", [P, 2, KD, UC])
        hi_gu = sb("hi_gu", [P, 2, KD, UC], F32R)
        lo_gu = sb("lo_gu", [P, 2, KD, UC], F32R)
        raw_d = sb("raw_d", [P, 2, 2, D])
        hi_d = sb("hi_d", [P, 2, 2, D], F32R)
        lo_d = sb("lo_d", [P, 2, 2, D], F32R)
        h_all = sb("h_all", [P, NS, TT, D])
        scr = sb("scr", [P, 2 * KD, T])
        a_hi = sb("a_hi", [P, KD, T], F32R)
        a_lo = sb("a_lo", [P, KD, T], F32R)
        hT_hi = sb("hT_hi", [P, 2, T], F32R)
        hT_lo = sb("hT_lo", [P, 2, T], F32R)
        hnat = sb("hnat", [P, TT, FS])
        sg = sb("sg", [P, TT, FS])
        ident = sb("ident", [P, P])
        ones = sb("ones", [P, P])
        tri = sb("tri", [P, P])
        iota = sb("iota", [P, P])
        colsA = sb("colsA", [P, P])
        colsB = sb("colsB", [P, 32])
        sil = sb("sil", [P, NS, KD])
        modT = sb("modT", [P, 2, 6, KD, NS])
        gsT = sb("gsT", [P, 2, 2, KD, NS])
        wmask = sb("wmask", [P, GRID])
        edge = sb("edge", [P, 4, 16])
        poolw = sb("poolw", [P, 4, P])
        st = sb("st", [P, 24])
        wr = sb("wr", [P, KD, NE])
        low8 = sb("low8", [P, NE, NE])
        tables = poolw[:, 2:4, :].rearrange("p g c -> p (g c)")
        route = tables[:, 0:48].rearrange("p (a e) -> p a e", a=6)
        jobs = tables[:, 48:48 + 6 * JOBS].rearrange("p (a e) -> p a e", a=6)
        sel = tables[:, 128:128 + OVER * NE].rearrange("p (a e) -> p a e", a=OVER)
        cmp8 = tables[:, 160:160 + NE * NE].rearrange("p (a e) -> p a e", a=NE)
        small = sb("small", [P, 8, NE])
        jint = sb("jint", [P, 4], I32)

        xn = scr[:, 0:KD, :].rearrange("p k t -> p (k t)").rearrange("p (a d) -> p a d", a=TT)
        aT = scr[:, KD:2 * KD, :]
        aT_flat = aT.rearrange("p k t -> p (k t)")
        diag = xn[:, 0, :]
        grow = aT_flat[:, 0:D]
        q_all = aT
        k_lat = scr[:, 0:KD, :]
        k_ctx = h_all[:, 0, :, :].rearrange("p a d -> p (a d)").rearrange("p (k t) -> p k t", k=KD)
        v_all = raw_d[:, :, :, :].rearrange("p a b d -> p (a b) d")
        sl0 = raw_gu[:, 0, :, :].rearrange("p k n -> p (k n)")
        sl1 = raw_gu[:, 1, :, :].rearrange("p k n -> p (k n)")
        bias = sl0[:, 0:2048].rearrange("p (b i n) -> p b i n", b=2, i=4)
        prob = sl0[:, 2048:3072].rearrange("p (b n) -> p b n", b=2)
        probT = sl0[:, 3072:4096].rearrange("p (b n) -> p b n", b=2)
        o_nat = sl1[:, 0:2048].rearrange("p (a d) -> p a d", a=TT)
        q_cur = sl1[:, 2048:2560].rearrange("p (b n) -> p b n", b=2)
        k_cur = sl1[:, 2560:3584].rearrange("p (b n) -> p b n", b=2)
        xg = aT_flat[:, 0:KD * P].rearrange("p (k t) -> p k t", k=KD)
        ysb = aT_flat[:, D:2 * D]
        acc = h_all[:, 0, :, :]
        pick = hnat[:, :, 0:P]
        pickg = sg[:, :, 0:P]
        back = poolw[:, 0:2, :]
        ag_hi = a_hi[:, 0:KD // 2, :].rearrange("p k t -> p (k t)").rearrange("p (k t) -> p k t", k=KD)
        ag_lo = a_lo[:, 0:KD // 2, :].rearrange("p k t -> p (k t)").rearrange("p (k t) -> p k t", k=KD)
        zpad = hnat[0:120, 0, 0:2 * (GRID + 1)].rearrange("p (t w) -> p t w", t=2)
        zrep = raw_d[0:120, :, :, :].rearrange("p a b d -> p (a b d)")[:, 0:ZW // 2]
        iota_i = sg[:, 0, 0:P].bitcast(I32)
        rowsA = scr[:, 0, 0:P]
        rowsB = scr[:, 1, 0:P]

        pg = ps("pg", [P, 2, 512])
        ptr = ps("ptr", [P, 512])
        pm = ps("pm", [P, 512])
        py = ps("py", [P, 4, 512])

        zed = nc.dram_tensor("skewed_bias", [HEADS * NDR, ZW], F32, kind="Internal").ap()

        x_land = sem("x_land"); rows_land = sem("rows_land"); cst_land = sem("cst_land")
        rpb_land = sem("rpb_land"); z_land = sem("z_land"); bias_land = [sem("bias_land0"), sem("bias_land1")]
        ada_land = [sem("ada_land0"), sem("ada_land1")]
        gu_land = [sem("gu_land0"), sem("gu_land1")]
        d_land = [sem("d_land0"), sem("d_land1")]
        gf_land = sem("gf_land"); out_land = sem("out_land")
        consts = sem("consts"); act_pace = sem("act_pace"); p_self = sem("p_self")
        col_tr = sem("col_tr", "pe"); cols = sem("cols", "dve"); sil_done = sem("sil_done", "act")
        ada_mm = sem("ada_mm", "pe"); ada_ev = sem("ada_ev", "dve"); mods = sem("mods", "dve")
        z_rep = sem("z_rep", "dve")
        gu_hi = sem("gu_hi", "act"); gu_lo = sem("gu_lo", "dve"); gu_used = sem("gu_used", "pe")
        d_hi = sem("d_hi", "act"); d_lo = sem("d_lo", "dve"); d_used = sem("d_used", "pe")
        n_ss = sem("n_ss", "act"); n_ms = sem("n_ms", "dve"); n_sq = sem("n_sq", "act")
        n_xn = sem("n_xn", "dve"); n_tr = sem("n_tr", "pe"); n_a = sem("n_a", "dve")
        n_hi = sem("n_hi", "act"); n_lo = sem("n_lo", "dve")
        k_mm = sem("k_mm", "pe"); k_ev = sem("k_ev", "act")
        m_diff = sem("m_diff", "dve"); m_pool = sem("m_pool", "pe"); m_y = sem("m_y", "dve")
        m_hi = sem("m_hi", "act"); m_lo = sem("m_lo", "dve")
        g_dg = sem("g_dg", "dve"); g_mm = sem("g_mm", "pe"); g_ev = sem("g_ev", "act")
        res = sem("res", "dve")
        f_sil = sem("f_sil", "act"); f_h = sem("f_h", "dve")
        f_tr = sem("f_tr", "pe"); f_hi = sem("f_hi", "act"); f_lo = sem("f_lo", "dve")
        v_ev = sem("v_ev", "act")
        t_cur = sem("t_cur", "act"); t_qk = sem("t_qk", "pe"); t_s = sem("t_s", "dve")
        t_e = sem("t_e", "act"); t_tr = sem("t_tr", "pe"); t_pt = sem("t_pt", "act")
        t_pv = sem("t_pv", "pe"); t_o = sem("t_o", "dve"); t_bias = sem("t_bias", "pool")
        o_tr = sem("o_tr", "pe"); o_hi = sem("o_hi", "act"); o_lo = sem("o_lo", "dve")
        r_lg = sem("r_lg", "pe"); r_mx = sem("r_mx", "dve"); r_ex = sem("r_ex", "act")
        r_mask = sem("r_mask", "dve"); r_pos = sem("r_pos", "pe"); r_jobs = sem("r_jobs", "dve")
        j_pick = sem("j_pick", "dve"); j_gat = sem("j_gat", "pe"); j_xg = sem("j_xg", "dve")
        j_hi = sem("j_hi", "act"); j_lo = sem("j_lo", "dve"); j_bt = sem("j_bt", "pe")
        j_back = sem("j_back", "dve"); j_ysb = sem("j_ysb", "act")
        j_comb = sem("j_comb", "pe"); j_acc = sem("j_acc", "dve")
        fin = sem("fin", "dve")

        NORM_CTX, NORM_LAT, NORM_FFN, NORM_OUT = 4, 5, 6, 7
        RES_ATT, RES_MOE = 4, 5
        T_L1 = NS * 4

        def run_steps(eng, steps, step):
            step(0, None, True, True)
            loops = (steps - 3) // 2
            with eng.Fori(0, loops) as i:
                for n in (1, 2):
                    step(n, i, True, True)
            for n in range(1 + 2 * loops, steps):
                step(n, None, n + 2 < steps, n + 1 < steps)

        def credits(eng, name):
            for s_ in owned[name]:
                eng.sem_inc(s_, C)

        block = stack.enter_context(nc.Block())

        @block.sync
        def _(sp):
            for s, src in ((0, ctx_in), (1, x)):
                sp.dma_start(h_all[:, s, :, :], src[0].rearrange("(a p) d -> p a d", p=P)).then_inc(x_land, 16)
            rows = [(rowsA[0:96, :], b_mod.rearrange("l (m p) -> (l m) p", p=P)),
                    (rowsA[96:112, :], g_mix.rearrange("l (m p) -> (l m) p", p=P)),
                    (rowsA[112:128, :], g_ffn.rearrange("l (m p) -> (l m) p", p=P)),
                    (rowsB[0:12, :], conv_w[0].rearrange("k (m p) -> (k m) p", p=P)),
                    (rowsB[12:16, :], pool_scale[0].rearrange("(m p) -> m p", p=P)),
                    (rowsB[16:24, :], c_ctx.rearrange("(m p) -> m p", p=P)),
                    (rowsB[24:32, :], c[0].rearrange("(m p) -> m p", p=P))]
            for dst, src in rows:
                sp.dma_start(dst, src).then_inc(rows_land, 16)

            def load_mod(slot, src):
                sp.dma_start(raw_gu[:, slot, :, :], src).then_inc(ada_land[slot], 16)

            wm = [w_mod[l].rearrange("(k p) (j c) -> j p k c", p=P, c=UC) for l in range(2)]
            for slot in range(2):
                load_mod(slot, wm[0][slot])
            sp.dma_start(poolw[:, :, :], pool_w[0].rearrange("g c d -> c g d")).then_inc(cst_land, 16)
            sp.dma_start(wr[:, :, :], w_router[0].rearrange("(k p) e -> p k e", p=P)).then_inc(cst_land, 16)
            for l in range(2):
                with sp.Fori(1 - l, MODU // 2) as i:
                    for slot in range(2):
                        sp.wait_ge(ada_mm, i * 2 + (C + l * MODU + slot - 1))
                        load_mod(slot, wm[l][i * 2 + slot])
            sp.wait_ge(ada_mm, C + 2 * MODU)
            sp.wait_ge(z_land, 64)

            def load_gu(u, parts):
                sp.wait_ge(gu_lo, u.before * 2 + C)
                for dst, src in parts:
                    sp.dma_start(dst, src).then_inc(gu_land[u.slot], 16)

            def load_cols(u, w, unit):
                v = w[0].rearrange("(k p) n -> p k n", p=P)
                load_gu(u, [(raw_gu[:, u.slot, 4 * h:4 * h + 4, :],
                             v[:, 4 * h:4 * h + 4, unit * UC:(unit + 1) * UC]) for h in range(2)])

            def load_step(u, du, g_src, u_src, d_src):
                load_gu(u, [(raw_gu[:, u.slot, :, 0:FS], g_src), (raw_gu[:, u.slot, :, FS:2 * FS], u_src)])
                sp.wait_ge(d_lo, du.before + C)
                sp.dma_start(raw_d[:, du.slot, :, :], d_src).then_inc(d_land[du.slot], 16)

            gw = w_gate[0].rearrange("(k p) (j c) -> j p k c", p=P, c=FS)
            uw = w_up[0].rearrange("(k p) (j c) -> j p k c", p=P, c=FS)
            dw = w_down[0].rearrange("(j f p) n -> j p f n", p=P, f=2)
            with sp.Fori(0, NS) as s:
                for k in range(4):
                    load_cols(gu0(s, k), w_in, k)
                for k in range(2):
                    load_cols(gu0(s, 4 + k), w_out, k)
                load_step(gu0(s, 6), d0(s, 0), gw[0], uw[0], dw[0])
                with sp.Fori(0, (STEPS0 - 1) // 2) as i:
                    for k in (1, 2):
                        load_step(gu0(s, 6 + k, i), d0(s, k, i), gw[i * 2 + k], uw[i * 2 + k], dw[i * 2 + k])
            for n, unit in enumerate((2, 3, 4, 5, 0, 1, 2, 3, 4, 5)):
                load_cols(gu1(n), w_qkv, unit)

            zv = zed[:, WINC - 1:WINC - 1 + GRID * GRID].rearrange("r (j k) -> j r k", k=GRID)

            def load_bias(b, i=None):
                for par in range(2):
                    for qt in range(TT):
                        for r2 in range(2):
                            row = (2 * b + par) * NDR + WINR - 1 - (2 * qt + r2)
                            rows4 = zv[:, row:row + 4, :] if i is None else zv[:, bass.ds(i * (4 * NDR) + row, 4), :]
                            sp.dma_start(bias[64 * r2:64 * r2 + 64, b, 2 * par + qt, :]
                                         .rearrange("p (r k) -> p r k", k=GRID), rows4).then_inc(bias_land[b], 16)

            sp.wait_ge(gu_lo, C + 2 * (GU_L1 + 10))
            for b in range(2):
                load_bias(b)
            with sp.Fori(1, HEADS // 4) as i:
                for b in range(2):
                    sp.wait_ge(t_s, i * 8 + (C + 4 * b - 4))
                    load_bias(b, i)
            sp.wait_ge(o_tr, C + 4)
            for n in (10, 11):
                load_cols(gu1(n), w_na, n - 10)

            ge = we_gate[0].rearrange("e (k p) (j c) -> e j p k c", p=P, c=FS)
            ue = we_up[0].rearrange("e (k p) (j c) -> e j p k c", p=P, c=FS)
            de = we_down[0].rearrange("e (j f p) n -> e j p f n", p=P, f=2)

            def load_expert(j, e):
                load_step(gu1(0, j), d1(j, 0), ge[e, 0], ue[e, 0], de[e, 0])
                with sp.Fori(0, (STEPSE - 1) // 2) as i:
                    for k in (1, 2):
                        load_step(gu1(k, j, i), d1(j, k, i), ge[e, i * 2 + k], ue[e, i * 2 + k], de[e, i * 2 + k])
                k = STEPSE - 1
                load_step(gu1(k, j), d1(j, k), ge[e, k], ue[e, k], de[e, k])

            with sp.Fori(0, NE) as j:
                load_expert(j, j)
            sp.wait_ge(r_jobs, C + 1)
            over = sp.value_load(jint[0:1, 3:4], min_val=0, max_val=OVER)
            with sp.If(over > 0):
                with sp.Fori(0, over) as r:
                    e = sp.value_load(jint[0:1, bass.ds(r, 1)], min_val=0, max_val=NE - 1)
                    load_expert(r + NE, e)
            sp.wait_ge(g_dg, C + 6)
            gfin = sl0[:, 0:D]
            sp.dma_start(gfin, g_final.rearrange("(o d) -> o d", o=1).to_broadcast([P, D])).then_inc(gf_land, 16)
            for tt in range(TT):
                sp.wait_ge(fin, C + tt + 1)
                sp.dma_start(out[0].rearrange("(a p) d -> p a d", p=P)[:, tt, :], xn[:, tt, :]).then_inc(out_land, 16)
            sp.wait_ge(out_land, 16 * TT)

        @block.gpsimd
        def _(pool):
            credits(pool, "pool")
            pool.memset(ident[:, :], 0.0).then_inc(p_self, 1)
            pool.memset(ones[:, :], 1.0).then_inc(p_self, 1)
            pool.memset(tri[:, :], 1.0).then_inc(p_self, 1)
            pool.memset(wmask[:, :], 1.0).then_inc(p_self, 1)
            pool.memset(zpad[:, :, :], 0.0).then_inc(p_self, 1)
            pool.wait_ge(p_self, 5)
            pool.affine_select(out=ident[:, :], in_=ident[:, :], compare_op=ALU.not_equal, fill=1.0,
                               base=0, pattern=[[-1, P]], channel_multiplier=1).then_inc(consts, 1)
            pool.affine_select(out=tri[:, :], in_=tri[:, :], compare_op=ALU.is_gt, fill=0.0,
                               base=0, pattern=[[1, P]], channel_multiplier=-1).then_inc(consts, 1)
            pool.iota(iota_i[:, :], pattern=[[1, P]], base=0, channel_multiplier=0).then_inc(consts, 1)
            n = 5
            for r in range(2):
                lo, hi = 64 * r, 64 * r + 64
                for base, mult, step, cols_ in ((WINC // 2, -1, 1, (0, GRID - WINC)),
                                                (WINC // 2 - 1, 1, -1, (WINC, GRID))):
                    a, z = cols_
                    pool.wait_ge(p_self, n)
                    pool.affine_select(out=wmask[lo:hi, a:z], in_=wmask[lo:hi, a:z], compare_op=ALU.is_ge,
                                       fill=0.0, base=base + step * a, pattern=[[step, z - a]],
                                       channel_multiplier=mult).then_inc(p_self, 1)
                    n += 1
            pool.wait_ge(p_self, n)
            pool.tensor_scalar(wmask[:, :], wmask[:, :], -1.0, 1e30, ALU.add, ALU.mult).then_inc(p_self, 1)
            n += 1
            pool.wait_ge(p_self, n)
            for t in range(2):
                pool.dma_start(zpad[0:120, t, 0:NDC], rpb[0].rearrange("h a b -> (h a) b")[120 * t:120 * t + 120, :])\
                    .then_inc(rpb_land, 16)
            pool.wait_ge(rpb_land, 32)
            for t in range(2):
                for q in range(2):
                    if 2 * t + q:
                        pool.wait_ge(z_land, 16 * (2 * t + q))
                    half = ZW // 2
                    pool.tensor_copy(zrep.rearrange("p (j w) -> p j w", w=GRID + 1),
                                     zpad[0:120, t:t + 1, :].to_broadcast([120, GRID // 2, GRID + 1])).then_inc(p_self, 1)
                    n += 1
                    pool.wait_ge(p_self, n)
                    pool.dma_start(zed[120 * t:120 * t + 120, q * half:(q + 1) * half], zrep).then_inc(z_land, 16)
            with pool.Fori(0, HEADS // 4) as i:
                for b in range(2):
                    pool.wait_ge(bias_land[b], i * 128 + 128)
                    v = bias[:, b, :, :].rearrange("p i (r k) -> p (i r) k", k=GRID)
                    pool.tensor_tensor(v, v, wmask[:, None, :].to_broadcast([P, 16, GRID]), ALU.add).then_inc(t_bias, 1)

        @block.scalar
        def _(act):
            credits(act, "act")

            def hi_half(u, h):
                if h == 0:
                    act.wait_ge(gu_land[u.slot], u.uses * 32)
                    act.wait_ge(gu_used, u.before + C)
                act.activation(hi_gu[:, u.slot, 4 * h:4 * h + 4, :], raw_gu[:, u.slot, 4 * h:4 * h + 4, :],
                               ACT.Copy).then_inc(gu_hi, 1)

            def hi(u):
                hi_half(u, 0)
                hi_half(u, 1)

            def hi_down(u):
                act.wait_ge(d_land[u.slot], u.uses * 16)
                act.wait_ge(d_used, u.before + C)
                act.activation(hi_d[:, u.slot, :, :], raw_d[:, u.slot, :, :], ACT.Copy).then_inc(d_hi, 1)

            def norm_stats(k, h, x_rows):
                act.wait_ge(x_land, 32)
                act.sem_inc(act_pace, 1)
                for tt in range(TT):
                    act.activation(xn[:, tt, :], x_rows(tt), ACT.Square, accum_out=st[:, tt:tt + 1]).then_inc(n_ss, 1)
                act.wait_ge(n_ms, h)
                act.activation(st[:, 4:6], st[:, 2:4], ACT.Sqrt).then_inc(n_sq, 1)

            def norm(k, s):
                norm_stats(k, k + (C + 1), lambda tt: h_all[:, s, tt, :])
                for q in range(4):
                    act.wait_ge(n_a, k * 4 + (C + q + 1))
                    act.activation(a_hi[:, 2 * q:2 * q + 2, :], aT[:, 2 * q:2 * q + 2, :], ACT.Copy).then_inc(n_hi, 1)

            def evac_T(u, n, half, dst):
                if half:
                    act.wait_ge(gu_used, u.n + (C + 1))
                else:
                    act.wait_ge(k_mm, n + (C + 1))
                act.activation(dst, pg[:, half, :], ACT.Copy).then_inc(k_ev, 1)

            def gate_row(k):
                act.wait_ge(g_mm, k + (C + 1))
                act.activation(grow, pg[:, :, :].rearrange("p a n -> p (a n)"), ACT.Copy).then_inc(g_ev, 1)

            def swiglu(steps, tiles, q0, gu, du):
                def step(st_, i, ahead, ahead_d):
                    q = lambda n: (q0 + (st_ + n)) if i is None else (i * 2 + q0 + (st_ + n))
                    act.wait_ge(gu_used, gu(st_, it0(i)).n + (C + 1))
                    act.wait_ge(f_h, q(C))
                    for t in range(tiles):
                        b = t if tiles == 2 else st_ % 2
                        ins = act.activation(sg[:, t, :], pg[:, b, 0:FS], ACT.Silu)
                    ins.then_inc(f_sil, 1)
                    if ahead:
                        hi_half(gu(st_ + 2, it0(i)), 0)
                    act.wait_ge(f_tr, q(C + 1))
                    act.wait_ge(d_used, q(C))
                    n = tiles * P
                    act.activation(hT_hi[:, :, 0:n], ptr[:, 0:2 * n].rearrange("p (f t) -> p f t", f=2),
                                   ACT.Copy).then_inc(f_hi, 1)
                    if ahead:
                        hi_half(gu(st_ + 2, it0(i)), 1)
                    if ahead_d:
                        hi_down(du(st_ + 1, it0(i)))
                run_steps(act, steps, step)

            act.wait_ge(cols, C + 2)
            act.activation(sil[:, :, :], colsB[:, 16:32].rearrange("p (s k) -> p s k", s=NS), ACT.Silu).then_inc(sil_done, 1)

            with act.Fori(0, NS) as s:
                hi(gu0(s, 0))
                hi(gu0(s, 1))
                act.wait_ge(res, s * 2 + C)
                norm(s * 2, s)
                for k in range(4):
                    if k == 0:
                        act.wait_ge(n_lo, s * 8 + (C + 4))
                    for half in range(2):
                        m = 4 * k + 2 * half
                        evac_T(gu0(s, k), s * 4 + k, half, scr[:, m:m + 2, :].rearrange("p m t -> p (m t)"))
                    hi(gu0(s, k + 2))
                act.wait_ge(m_y, s + (C + 1))
                act.activation(a_hi[:, :, :], scr[:, 0:KD, :], ACT.Copy).then_inc(m_hi, 1)
                gate_row(s * 2)
                hi(gu0(s, 6))
                act.wait_ge(res, s * 2 + (C + 1))
                norm(s * 2 + 1, s)
                hi(gu0(s, 7))
                hi_down(d0(s, 0))
                gate_row(s * 2 + 1)
                swiglu(STEPS0, TT, s * STEPS0, lambda k, i: gu0(s, 6 + k, i), lambda k, i: d0(s, k, i))

            hi(gu1(0))
            hi(gu1(1))
            act.wait_ge(res, C + 4)
            norm(NORM_CTX, 0)
            for u in range(2):
                for half in range(2):
                    evac_T(gu1(u), T_L1 + u, half, k_ctx[:, 4 * u + 2 * half:4 * u + 2 * half + 2, :].rearrange("p m t -> p (m t)"))
                hi(gu1(u + 2))

            def evac_v(u, tile0):
                act.wait_ge(gu_used, C + u.n + 1)
                act.activation(v_all[:, tile0:tile0 + 2, :].rearrange("p a d -> p (a d)"),
                               py[:, :, :].rearrange("p a n -> p (a n)"), ACT.Copy).then_inc(v_ev, 1)

            act.wait_ge(d_lo, C + D_MOE)
            evac_v(gu1(3), 2)
            hi(gu1(4))
            hi(gu1(5))
            norm(NORM_LAT, 1)
            act.wait_ge(n_lo, C + 4 * (NORM_LAT + 1))
            for u in range(4):
                dst = (q_all, k_lat)[u // 2]
                for half in range(2):
                    m = 4 * (u % 2) + 2 * half
                    evac_T(gu1(4 + u), T_L1 + 2 + u, half, dst[:, m:m + 2, :].rearrange("p m t -> p (m t)"))
                hi(gu1(u + 6))
            evac_v(gu1(9), 0)
            act.wait_ge(gu_lo, C + 2 * (GU_L1 + 10))

            with act.Fori(0, HEADS // 4) as i:
                for b in range(2):
                    act.wait_ge(t_qk, i * 8 + (C + 4 * b))
                    act.wait_ge(k_ev, C + 2 * (T_L1 + 6))
                    act.sem_inc(act_pace, 1)
                    act.activation(q_cur[:, b, :], q_all[:, bass.ds(i * 2 + b, 1), :].rearrange("p o t -> p (o t)"), ACT.Copy)
                    act.activation(k_cur[:, b, 0:T], k_lat[:, bass.ds(i * 2 + b, 1), :].rearrange("p o t -> p (o t)"), ACT.Copy)
                    act.activation(k_cur[:, b, T:2 * T], k_ctx[:, bass.ds(i * 2 + b, 1), :].rearrange("p o t -> p (o t)"), ACT.Copy).then_inc(t_cur, 1)

                    def exps(it):
                        act.wait_ge(t_s, i * 8 + (C + 4 * b + it + 1))
                        act.activation(prob[:, it % 2, :], prob[:, it % 2, :], ACT.Exp, bias=st[:, 20 + it:21 + it],
                                       accum_out=st[:, 12 + it:13 + it]).then_inc(t_e, 1)

                    def turned(it):
                        act.wait_ge(t_tr, i * 8 + (C + 4 * b + it + 1))
                        act.wait_ge(t_pv, i * 8 + (C + 4 * b + it - 1))
                        act.activation(probT[:, it % 2, :], ptr[:, :], ACT.Copy).then_inc(t_pt, 1)

                    exps(0)
                    for it in range(1, 4):
                        exps(it)
                        turned(it - 1)
                    turned(3)
            for q in range(4):
                act.wait_ge(o_tr, C + q + 1)
                act.activation(a_hi[:, 2 * q:2 * q + 2, :].rearrange("p k t -> p (k t)"), py[:, q, :], ACT.Copy).then_inc(o_hi, 1)
            hi(gu1(10))
            hi(gu1(11))
            gate_row(RES_ATT)
            act.wait_ge(res, C + RES_ATT + 1)
            norm(NORM_FFN, 1)
            act.wait_ge(r_mx, C + 1)
            for tt in range(TT):
                act.activation(small[:, 2 + tt, :], small[:, tt, :], ACT.Exp, bias=st[:, 10 + tt:11 + tt]).then_inc(r_ex, 1)
            act.wait_ge(r_jobs, C + 1)
            over = act.value_load(jint[0:1, 3:4], min_val=0, max_val=OVER)
            with act.Fori(0, over + NE) as j:
                hi(gu1(0, j))
                hi(gu1(1, j))
                hi_down(d1(j, 0))
                act.wait_ge(j_xg, j + (C + 1))
                act.activation(ag_hi, xg, ACT.Copy).then_inc(j_hi, 1)
                swiglu(STEPSE, 1, j * STEPSE + D_MOE, lambda k, i: gu1(k, j, i), lambda k, i: d1(j, k, i))
                act.wait_ge(d_used, j * STEPSE + (D_MOE + STEPSE + C))
                act.wait_ge(j_comb, j * 2 + C)
                act.activation(ysb, py[:, 2:4, :].rearrange("p a n -> p (a n)"), ACT.Copy).then_inc(j_ysb, 1)
            gate_row(RES_MOE)
            act.wait_ge(res, C + RES_MOE + 1)
            norm_stats(NORM_OUT, C + NORM_OUT + 1, lambda tt: h_all[:, 1, tt, :])

        @block.vector
        def _(dve):
            credits(dve, "dve")
            dve.memset(low8[:, :, :], 0.0)
            dve.memset(edge[:, :, :], 1.0)
            dve.drain()
            for e in range(1, NE):
                dve.memset(low8[:, e, 0:e], 1.0)
            for g, w in enumerate(WINDOWS):
                for t in range(w // 2):
                    dve.memset(edge[:, g, t:t + 1], w / (t + w // 2))
                for t in range(w - 1 - w // 2):
                    dve.memset(edge[:, g, 15 - t:16 - t], w / (t + 1 + w // 2))
            dve.wait_ge(consts, 3)
            dve.tensor_copy(iota[:, :], iota_i[:, :])
            for n, (dst, rows_) in enumerate(((colsA, P), (colsB, 32))):
                dve.wait_ge(col_tr, C + n + 1)
                dve.tensor_copy(dst[:, :], (pm, ptr)[n][:, 0:rows_]).then_inc(cols, 1)

            def lo_half(u, h):
                dve.wait_ge(gu_hi, u.n * 2 + (C + h + 1))
                k = slice(4 * h, 4 * h + 4)
                dve.tensor_tensor(lo_gu[:, u.slot, k, :], raw_gu[:, u.slot, k, :],
                                  hi_gu[:, u.slot, k, :].bitcast(F32), ALU.subtract).then_inc(gu_lo, 1)

            def lo(u):
                lo_half(u, 0)
                lo_half(u, 1)

            def lo_down(u):
                dve.wait_ge(d_hi, u.n + (C + 1))
                dve.tensor_tensor(lo_d[:, u.slot, :, :], raw_d[:, u.slot, :, :], hi_d[:, u.slot, :, :].bitcast(F32),
                                  ALU.subtract).then_inc(d_lo, 1)

            def rstd(k):
                dve.wait_ge(n_ss, k * 2 + (C + 2))
                dve.tensor_scalar(st[:, 2:4], st[:, 0:2], 1.0 / D, EPS, ALU.mult, ALU.add).then_inc(n_ms, 1)
                dve.wait_ge(n_sq, k + (C + 1))
                dve.reciprocal(st[:, 6:8], st[:, 4:6])
                dve.drain()
                dve.tensor_tensor(st[:, 8:10], st[:, 6:8], st[:, 6:8], ALU.mult)
                dve.drain()
                dve.tensor_tensor(st[:, 8:10], st[:, 8:10], st[:, 2:4], ALU.mult)
                dve.drain()
                dve.tensor_scalar(st[:, 8:10], st[:, 8:10], -0.5, 1.5, ALU.mult, ALU.add)
                dve.drain()
                dve.tensor_tensor(st[:, 6:8], st[:, 6:8], st[:, 8:10], ALU.mult)
                dve.drain()

            def modulate(dst, src, l, half, kt, s):
                gs = gsT[:, l, half, kt, s:s + 1] if isinstance(s, int) else gsT[:, l, half, kt, bass.ds(s, 1)]
                sh = modT[:, l, 3 * half, kt, s:s + 1] if isinstance(s, int) else modT[:, l, 3 * half, kt, bass.ds(s, 1)]
                return dve.tensor_scalar(dst, src, gs, sh, ALU.mult, ALU.add)

            def norm(k, l, half, s):
                rstd(k)
                for tt in range(TT):
                    ins = dve.tensor_scalar(xn[:, tt, :], h_all[:, s, tt, :], st[:, 6 + tt:7 + tt], None, ALU.mult)
                ins.then_inc(n_xn, 1)
                for q in range(4):
                    dve.wait_ge(n_tr, k * 4 + (C + q + 1))
                    for kk in range(2):
                        ins = modulate(aT[:, 2 * q + kk, :], py[:, q, kk * T:kk * T + T], l, half, 2 * q + kk, s)
                    ins.then_inc(n_a, 1)
                for q in range(4):
                    dve.wait_ge(n_hi, k * 4 + (C + q + 1))
                    v = slice(2 * q, 2 * q + 2)
                    dve.tensor_tensor(a_lo[:, v, :], aT[:, v, :], a_hi[:, v, :].bitcast(F32), ALU.subtract).then_inc(n_lo, 1)

            def gate_diag(l, half, s):
                for kt in range(KD):
                    col = modT[:, l, 3 * half + 2, kt, s:s + 1] if isinstance(s, int) else modT[:, l, 3 * half + 2, kt, bass.ds(s, 1)]
                    ins = dve.tensor_scalar(diag[:, kt * P:kt * P + P], ident[:, :], col, None, ALU.mult)
                ins.then_inc(g_dg, 1)

            def residual(k, s, y=None, done=None):
                dve.wait_ge(g_ev, k + (C + 1))
                if done:
                    dve.wait_ge(*done)
                for tt in range(TT):
                    src = py[:, 2 * tt:2 * tt + 2, :].rearrange("p a n -> p (a n)") if y is None else y[:, tt, :]
                    dve.tensor_tensor(xn[:, tt, :], src, grow, ALU.mult)
                dve.drain()
                for tt in range(TT):
                    ins = dve.tensor_tensor(h_all[:, s, tt, :], h_all[:, s, tt, :], xn[:, tt, :], ALU.add)
                ins.then_inc(res, 1)

            def swiglu(steps, tiles, q0, gu, du):
                def step(st_, i, ahead, ahead_d):
                    q = lambda n: (q0 + (st_ + n)) if i is None else (i * 2 + q0 + (st_ + n))
                    dve.wait_ge(f_sil, q(C + 1))
                    dve.wait_ge(f_tr, q(C))
                    for t in range(tiles):
                        b = t if tiles == 2 else st_ % 2
                        ins = dve.tensor_tensor(hnat[:, t, :], pg[:, b, FS:2 * FS], sg[:, t, :], ALU.mult)
                    ins.then_inc(f_h, 1)
                    if ahead:
                        lo_half(gu(st_ + 2, it0(i)), 0)
                    dve.wait_ge(f_hi, q(C + 1))
                    n = tiles * P
                    dve.tensor_tensor(hT_lo[:, :, 0:n], ptr[:, 0:2 * n].rearrange("p (f t) -> p f t", f=2),
                                      hT_hi[:, :, 0:n].bitcast(F32), ALU.subtract).then_inc(f_lo, 1)
                    if ahead:
                        lo_half(gu(st_ + 2, it0(i)), 1)
                    if ahead_d:
                        lo_down(du(st_ + 1, it0(i)))
                run_steps(dve, steps, step)

            for l in range(2):
                mv = modT[:, l, :, :, :].rearrange("p i k s -> p (i k) s")
                with dve.Fori(0, MODU // 2) as i:
                    for slot in range(2):
                        dve.wait_ge(ada_mm, i * 2 + (C + l * MODU + slot + 1))
                        m4 = i * 8 + 4 * slot
                        bm = colsA[:, bass.ds(i * 8 + (l * 48 + 4 * slot), 4)]
                        dve.tensor_tensor(mv[:, bass.ds(m4, 4), :], (pm, ptr)[slot][:, 0:8].rearrange("p (m s) -> p m s", s=NS),
                                          bm[:, :, None].to_broadcast([P, 4, NS]), ALU.add).then_inc(ada_ev, 1)
            dve.drain()
            for l in range(2):
                for half in range(2):
                    g = colsA[:, 96 + 16 * half + 8 * l:96 + 16 * half + 8 * l + 8]
                    ins = dve.scalar_tensor_tensor(out=gsT[:, l, half, :, :], in0=modT[:, l, 3 * half + 1, :, :], scalar=1.0,
                                                   in1=g[:, :, None].to_broadcast([P, KD, NS]), op0=ALU.add, op1=ALU.mult)
            dve.drain()
            dve.wait_ge(z_land, 64)

            with dve.Fori(0, NS) as s:
                lo(gu0(s, 0))
                lo(gu0(s, 1))
                norm(s * 2, 0, 0, s)
                for k in range(2, 6):
                    lo(gu0(s, k))
                dve.wait_ge(k_ev, s * 8 + (C + 8))
                padA = hnat[:, :, :].rearrange("p a n -> p (a n)")
                padB = sg[:, :, :].rearrange("p a n -> p (a n)")
                for g, w in enumerate(WINDOWS):
                    if g:
                        dve.drain()
                    dve.memset(padA[:, 0:16], 0.0)
                    dve.memset(padA[:, 16 + T:32 + T], 0.0)
                    dve.tensor_copy(padA[:, 16:16 + T], scr[:, 12 + g, :])
                    dve.drain()
                    src, dst, n, back_, fwd = padA, padB, 1, 1, 0
                    lo_, hi_ = 0, T + 32
                    while n < w:
                        lo_, hi_ = lo_ + back_, hi_ - fwd
                        dve.tensor_tensor(dst[:, lo_:hi_], src[:, lo_ - back_:hi_ - back_], src[:, lo_ + fwd:hi_ + fwd], ALU.add)
                        dve.drain()
                        src, dst, n = dst, src, 2 * n
                        back_ = fwd = n // 2
                    for a, e in ((16, 0), (16 + T - 8, 8)):
                        dve.tensor_tensor(src[:, a:a + 8], src[:, a:a + 8], edge[:, g, e:e + 8], ALU.mult)
                    dve.drain()
                    ins = dve.scalar_tensor_tensor(out=scr[:, 12 + g, :], in0=src[:, 16:16 + T], scalar=1.0 / w,
                                                   in1=scr[:, 12 + g, :], op0=ALU.mult, op1=ALU.subtract)
                ins.then_inc(m_diff, 1)
                dve.tensor_tensor(scr[:, 4:8, :], scr[:, 4:8, :], scr[:, 8:12, :], ALU.mult)
                dve.drain()
                for m in range(4):
                    dve.tensor_scalar(scr[:, 8 + m, :], scr[:, 4 + m, :], colsB[:, 4 + m:5 + m], None, ALU.mult)
                dve.drain()
                for m in range(4):
                    dve.scalar_tensor_tensor(out=scr[:, 8 + m, 1:T], in0=scr[:, 4 + m, 0:T - 1], scalar=colsB[:, m:m + 1],
                                             in1=scr[:, 8 + m, 1:T], op0=ALU.mult, op1=ALU.add)
                dve.drain()
                for m in range(4):
                    dve.scalar_tensor_tensor(out=scr[:, 8 + m, 0:T - 1], in0=scr[:, 4 + m, 1:T], scalar=colsB[:, 8 + m:9 + m],
                                             in1=scr[:, 8 + m, 0:T - 1], op0=ALU.mult, op1=ALU.add)
                dve.drain()
                dve.tensor_tensor(scr[:, 0:4, :], scr[:, 0:4, :], scr[:, 8:12, :], ALU.mult)
                dve.wait_ge(m_pool, s + (C + 1))
                for g in range(4):
                    ins = dve.tensor_scalar(scr[:, 4 + g, :], pg[:, g // 2, (g % 2) * T:(g % 2) * T + T],
                                            colsB[:, 12 + g:13 + g], None, ALU.mult)
                ins.then_inc(m_y, 1)
                dve.wait_ge(m_hi, s + (C + 1))
                dve.tensor_tensor(a_lo[:, :, :], scr[:, 0:KD, :], a_hi[:, :, :].bitcast(F32), ALU.subtract).then_inc(m_lo, 1)
                dve.drain()
                gate_diag(0, 0, s)
                residual(s * 2, s, done=(gu_used, gu0(s, 5).n + (C + 1)))
                lo(gu0(s, 6))
                norm(s * 2 + 1, 0, 1, s)
                dve.drain()
                gate_diag(0, 1, s)
                lo(gu0(s, 7))
                lo_down(d0(s, 0))
                swiglu(STEPS0, TT, s * STEPS0, lambda k, i: gu0(s, 6 + k, i), lambda k, i: d0(s, k, i))
                residual(s * 2 + 1, s, done=(d_used, s * STEPS0 + (STEPS0 + C)))

            lo(gu1(0))
            lo(gu1(1))
            norm(NORM_CTX, 1, 0, 0)
            for n in range(2, 6):
                lo(gu1(n))
            norm(NORM_LAT, 1, 0, 1)
            for n in range(6, 10):
                lo(gu1(n))

            with dve.Fori(0, HEADS // 4) as i:
                for b in range(2):
                    def scores(it):
                        x_ = i * 8 + (C + 4 * b + it)
                        dve.wait_ge(t_qk, x_ + 1)
                        dve.wait_ge(t_tr, x_ - 1)
                        p_ = prob[:, it % 2, :]
                        dve.scalar_tensor_tensor(out=p_[:, 0:T], in0=pg[:, it % 2, 0:T], scalar=HD ** -0.5,
                                                 in1=bias[:, b, it, :], op0=ALU.mult, op1=ALU.add)
                        dve.tensor_scalar(p_[:, T:2 * T], pg[:, it % 2, T:2 * T], HD ** -0.5, None, ALU.mult)
                        dve.drain()
                        dve.tensor_reduce(st[:, 20 + it:21 + it], p_, AXX, ALU.max)
                        dve.drain()
                        dve.tensor_scalar(st[:, 20 + it:21 + it], st[:, 20 + it:21 + it], -1.0, None, ALU.mult).then_inc(t_s, 1)

                    def outs(it):
                        dve.wait_ge(t_pv, i * 8 + (C + 4 * b + it + 1))
                        dve.reciprocal(st[:, 16 + it:17 + it], st[:, 12 + it:13 + it])
                        dve.drain()
                        col = i * (4 * HD) + (2 * b + it // 2) * HD
                        dve.tensor_scalar(o_nat[:, it % 2, bass.ds(col, HD)], py[:, it, 0:HD], st[:, 16 + it:17 + it],
                                          None, ALU.mult).then_inc(t_o, 1)

                    dve.wait_ge(t_bias, i * 2 + (C + b + 1))
                    scores(0)
                    scores(1)
                    scores(2)
                    outs(0)
                    scores(3)
                    for it in range(1, 4):
                        outs(it)
            for q in range(4):
                dve.wait_ge(o_hi, C + q + 1)
                dve.tensor_tensor(a_lo[:, 2 * q:2 * q + 2, :].rearrange("p k t -> p (k t)"), py[:, q, :],
                                  a_hi[:, 2 * q:2 * q + 2, :].rearrange("p k t -> p (k t)").bitcast(F32), ALU.subtract).then_inc(o_lo, 1)
            gate_diag(1, 0, 1)
            lo(gu1(10))
            lo(gu1(11))
            residual(RES_ATT, 1, done=(gu_used, C + gu1(11).n + 1))
            norm(NORM_FFN, 1, 1, 1)

            dve.wait_ge(r_lg, C + 1)
            dve.tensor_copy(small[:, 0:2, :], pm[:, 0:2 * NE].rearrange("p (a e) -> p a e", a=TT))
            dve.memset(acc[:, :, :], 0.0)
            dve.drain()
            dve.tensor_reduce(st[:, 8:10], small[:, 0:2, :], AXX, ALU.max)
            dve.drain()
            dve.tensor_scalar(st[:, 10:12], st[:, 8:10], -1.0, None, ALU.mult).then_inc(r_mx, 1)
            for tt in range(TT):
                l_ = small[:, tt, :]
                other = l_[:, None, :].to_broadcast([P, NE, NE])
                own = l_[:, :, None].to_broadcast([P, NE, NE])
                dve.tensor_tensor(cmp8, other, own, ALU.is_equal)
                dve.drain()
                dve.tensor_tensor(cmp8, cmp8, low8[:, :, :], ALU.mult)
                dve.drain()
                dve.tensor_reduce(small[:, 4, :], cmp8, AXX, ALU.add)
                dve.drain()
                dve.tensor_tensor(cmp8, other, own, ALU.is_gt)
                dve.drain()
                dve.tensor_reduce(small[:, 5, :], cmp8, AXX, ALU.add)
                dve.drain()
                dve.tensor_tensor(small[:, 4, :], small[:, 4, :], small[:, 5, :], ALU.add)
                dve.drain()
                ins = dve.tensor_scalar(route[:, tt, :], small[:, 4, :], TOPK - 0.5, None, ALU.is_lt)
                dve.drain()
            dve.drain().then_inc(r_mask, 1)
            dve.wait_ge(r_ex, C + 2)
            for tt in range(TT):
                dve.tensor_tensor(small[:, 2 + tt, :], small[:, 2 + tt, :], route[:, tt, :], ALU.mult)
            dve.drain()
            dve.tensor_reduce(st[:, 12:14], small[:, 2:4, :], AXX, ALU.add)
            dve.drain()
            dve.reciprocal(st[:, 14:16], st[:, 12:14])
            dve.drain()
            for tt in range(TT):
                dve.tensor_scalar(route[:, 4 + tt, :], small[:, 2 + tt, :], st[:, 14 + tt:15 + tt], None, ALU.mult)
            dve.wait_ge(r_pos, C + 1)
            dve.tensor_copy(route[:, 2:4, :], pm[:, 32:48].rearrange("p (a e) -> p a e", a=TT))
            dve.tensor_scalar(small[:, 4, :], pm[:, 48:56], CAP + 0.5, None, ALU.is_gt)
            dve.drain()
            dve.tensor_tensor(cmp8, small[:, 4, :][:, None, :].to_broadcast([P, NE, NE]), low8[:, :, :], ALU.mult)
            dve.drain()
            dve.tensor_reduce(small[:, 5, :], cmp8, AXX, ALU.add)
            dve.tensor_reduce(st[:, 16:17], small[:, 4, :], AXX, ALU.add)
            dve.drain()
            for r in range(OVER):
                dve.scalar_tensor_tensor(out=sel[:, r, :], in0=small[:, 5, :], scalar=float(r), in1=small[:, 4, :],
                                         op0=ALU.is_equal, op1=ALU.mult)
            dve.tensor_copy(jobs[:, :, 0:NE], route)
            dve.drain()
            for r in range(OVER):
                dve.tensor_tensor(cmp8[:, 0:6, :], route, sel[:, r, :][:, None, :].to_broadcast([P, 6, NE]), ALU.mult)
                dve.drain()
                dve.tensor_reduce(jobs[:, :, NE + r], cmp8[:, 0:6, :], AXX, ALU.add)
                dve.drain()
                dve.tensor_scalar(jobs[:, 2:4, NE + r], jobs[:, 2:4, NE + r], -float(CAP), None, ALU.add)
            dve.tensor_tensor(cmp8[:, 0:OVER, :], sel, iota[:, 0:NE][:, None, :].to_broadcast([P, OVER, NE]), ALU.mult)
            dve.drain()
            dve.tensor_reduce(st[:, 17:17 + OVER], cmp8[:, 0:OVER, :], AXX, ALU.add)
            dve.drain()
            dve.tensor_copy(jint[:, 0:OVER], st[:, 17:17 + OVER])
            dve.tensor_copy(jint[:, 3:4], st[:, 16:17])
            dve.drain().then_inc(r_jobs, 1)
            dve.wait_ge(r_jobs, C + 1)
            over = dve.value_load(jint[0:1, 3:4], min_val=0, max_val=OVER)
            with dve.Fori(0, over + NE) as j:
                q0 = j * STEPSE + D_MOE
                dve.wait_ge(f_tr, q0 + C)
                for tt in range(TT):
                    dve.tensor_scalar(pick[:, tt, :], iota[:, :], jobs[:, 2 + tt, bass.ds(j, 1)],
                                      jobs[:, tt, bass.ds(j, 1)], ALU.is_equal, ALU.mult)
                dve.drain()
                for tt in range(TT):
                    ins = dve.tensor_scalar(pickg[:, tt, :], pick[:, tt, :], jobs[:, 4 + tt, bass.ds(j, 1)], None, ALU.mult)
                ins.then_inc(j_pick, 1)
                lo_half(gu1(0, j), 0)
                dve.wait_ge(j_gat, j + (C + 1))
                for kt in range(KD):
                    ins = modulate(xg[:, kt, :], py[:, kt // 4, (kt % 4) * P:(kt % 4) * P + P], 1, 1, kt, 1)
                ins.then_inc(j_xg, 1)
                dve.wait_ge(j_bt, j + (C + 1))
                dve.tensor_copy(back, ptr[:, 0:T].rearrange("p (a t) -> p a t", a=TT)).then_inc(j_back, 1)
                dve.wait_ge(j_hi, j + (C + 1))
                dve.tensor_tensor(ag_lo, xg, ag_hi.bitcast(F32), ALU.subtract).then_inc(j_lo, 1)
                lo_half(gu1(0, j), 1)
                lo(gu1(1, j))
                lo_down(d1(j, 0))
                swiglu(STEPSE, 1, q0, lambda k, i: gu1(k, j, i), lambda k, i: d1(j, k, i))
                for tt in range(TT):
                    dve.wait_ge(j_comb, j * 2 + (C + tt + 1))
                    dve.tensor_tensor(acc[:, tt, :], acc[:, tt, :], py[:, 0:2, :].rearrange("p a n -> p (a n)"), ALU.add).then_inc(j_acc, 1)
            dve.drain()
            gate_diag(1, 1, 1)
            residual(RES_MOE, 1, acc)
            rstd(NORM_OUT)
            dve.wait_ge(gf_land, 16)
            for tt in range(TT):
                dve.scalar_tensor_tensor(out=xn[:, tt, :], in0=h_all[:, 1, tt, :], scalar=st[:, 6 + tt:7 + tt],
                                         in1=sl0[:, 0:D], op0=ALU.mult, op1=ALU.mult).then_inc(fin, 1)

        @block.tensor
        def _(pe):
            credits(pe, "pe")
            pe.wait_ge(consts, 3)
            pe.wait_ge(rows_land, 16 * 7)
            pe.transpose(pm[:, 0:P], rowsA, ident[:, :]).then_inc(col_tr, 1)
            pe.transpose(ptr[:, 0:32], rowsB[0:32, :], ident[0:32, 0:32]).then_inc(col_tr, 1)
            pe.wait_ge(sil_done, C + 1)
            pe.wait_ge(cols, C + 2)
            for l in range(2):
                with pe.Fori(0, MODU // 2) as i:
                    for slot in range(2):
                        pe.wait_ge(ada_land[slot], i * 16 + 16 * (l * MODU // 2 + 1))
                        pe.wait_ge(ada_ev, i * 2 + (C + l * MODU + slot - 1))
                        for m in range(4):
                            for kt in range(KD):
                                mm = pe.matmul((pm, ptr)[slot][:, NS * m:NS * m + NS], raw_gu[:, slot, kt, m * P:m * P + P],
                                               sil[:, :, kt], start=kt == 0, stop=kt == KD - 1)
                        mm.then_inc(ada_mm, 1)

            def three(dst, a, b, first, last):
                pe.matmul(dst, a[0], b[0], start=first, stop=False)
                pe.matmul(dst, a[1], b[0], start=False, stop=False)
                return pe.matmul(dst, a[0], b[1], start=False, stop=last)

            def norm(k):
                pe.wait_ge(n_xn, k + (C + 1))
                for q in range(4):
                    for kk in range(2):
                        for tt in range(TT):
                            kt = 2 * q + kk
                            mm = pe.transpose(py[:, q, kk * T + tt * P:kk * T + tt * P + P],
                                              xn[:, tt, kt * P:kt * P + P], ident[:, :])
                    mm.then_inc(n_tr, 1)

            def wcols(u, kt, a, z):
                return hi_gu[:, u.slot, kt, a:z], lo_gu[:, u.slot, kt, a:z]

            def project_T(u, n):
                pe.wait_ge(gu_lo, u.n * 2 + (C + 2))
                for half in range(2):
                    pe.wait_ge(k_ev, n * 2 + (C + half - 1))
                    for m in (2 * half, 2 * half + 1):
                        for kt in range(KD):
                            mm = three(pg[:, half, (m % 2) * T:(m % 2) * T + T], wcols(u, kt, m * P, m * P + P),
                                       (a_hi[:, kt, :], a_lo[:, kt, :]), kt == 0, kt == KD - 1)
                    mm.then_inc(gu_used if half else k_mm, 1)

            def project_rows(u, nh):
                pe.wait_ge(gu_lo, u.n * 2 + (C + 2))
                for tt in range(TT):
                    for kt in range(KD):
                        mm = three(py[:, 2 * tt + nh, :], (a_hi[:, kt, tt * P:tt * P + P], a_lo[:, kt, tt * P:tt * P + P]),
                                   wcols(u, kt, 0, UC), kt == 0, kt == KD - 1)
                mm.then_inc(gu_used, 1)

            def gate_rows(k):
                pe.wait_ge(g_dg, k + (C + 1))
                for nh in range(2):
                    mm = pe.matmul(pg[:, nh, :], ones[:, :], diag[:, nh * 512:nh * 512 + 512], start=True, stop=True)
                mm.then_inc(g_mm, 1)

            def swiglu(steps, tiles, q0, gu, du, yb, done_h=None):
                def up(u, st_, q, part):
                    b = part if tiles == 2 else st_ % 2
                    if part == 0 or tiles == 2:
                        pe.wait_ge(f_h, q(C) if tiles == 2 else q(C - 1))
                    if part == 0:
                        pe.wait_ge(gu_lo, u.n * 2 + (C + 2 if tiles == 2 else C + 1))
                    elif tiles == 1:
                        pe.wait_ge(gu_lo, u.n * 2 + (C + 2))
                    for kt in range(KD) if tiles == 2 else range(4 * part, 4 * part + 4):
                        mm = three(pg[:, b, :], tuple(x_[:, kt, part * P:part * P + P] if tiles == 2 else x_[:, kt, :] for x_ in acts),
                                   wcols(u, kt, 0, 2 * FS), kt == 0, kt == KD - 1)
                    if part == 1:
                        mm.then_inc(gu_used, 1)

                acts = (a_hi, a_lo) if tiles == 2 else (ag_hi, ag_lo)

                def step(st_, i, ahead_, ahead):
                    q = lambda n: (q0 + (st_ + n)) if i is None else (i * 2 + q0 + (st_ + n))
                    if ahead:
                        up(gu(st_ + 1, it0(i)), st_ + 1, lambda n: q(n + 1), 0)
                    pe.wait_ge(f_h, q(C + 1))
                    if st_ == 0 and done_h:
                        pe.wait_ge(*done_h)
                    pe.wait_ge(f_lo, q(C))
                    for f in range(2):
                        for t in range(tiles):
                            mm = pe.transpose(ptr[:, (f * tiles + t) * P:(f * tiles + t) * P + P],
                                              hnat[:, t, f * P:f * P + P], ident[:, :])
                    mm.then_inc(f_tr, 1)
                    if ahead:
                        up(gu(st_ + 1, it0(i)), st_ + 1, lambda n: q(n + 1), 1)
                    u = du(st_, it0(i))
                    pe.wait_ge(f_lo, q(C + 1))
                    pe.wait_ge(d_lo, u.n + (C + 1))
                    for t in range(tiles):
                        for nh in range(2):
                            for f in range(2):
                                mm = three(py[:, yb + 2 * t + nh, :], (hT_hi[:, f, t * P:t * P + P], hT_lo[:, f, t * P:t * P + P]),
                                           (hi_d[:, u.slot, f, nh * 512:nh * 512 + 512], lo_d[:, u.slot, f, nh * 512:nh * 512 + 512]),
                                           st_ == 0 and f == 0, st_ == steps - 1 and i is None and f == 1)
                    mm.then_inc(d_used, 1)

                for part in range(2):
                    up(gu(0, 0), 0, lambda n: q0 + n, part)
                run_steps(pe, steps, step)

            with pe.Fori(0, NS) as s:
                norm(s * 2)
                pe.wait_ge(n_lo, s * 8 + (C + 4))
                for k in range(4):
                    project_T(gu0(s, k), s * 4 + k)
                pe.wait_ge(m_diff, s + (C + 1))
                pe.wait_ge(cst_land, 32)
                for g in range(4):
                    mm = pe.matmul(pg[:, g // 2, (g % 2) * T:(g % 2) * T + T], poolw[:, g, :], scr[:, 12 + g, :],
                                   start=True, stop=True)
                mm.then_inc(m_pool, 1)
                pe.wait_ge(m_lo, s + (C + 1))
                for k in range(2):
                    project_rows(gu0(s, 4 + k), k)
                gate_rows(s * 2)
                norm(s * 2 + 1)
                gate_rows(s * 2 + 1)
                pe.wait_ge(n_lo, s * 8 + (C + 8))
                pe.wait_ge(g_ev, s * 2 + (C + 2))
                swiglu(STEPS0, TT, s * STEPS0, lambda k, i: gu0(s, 6 + k, i), lambda k, i: d0(s, k, i), 0)

            norm(NORM_CTX)
            pe.wait_ge(n_lo, C + 4 * (NORM_CTX + 1))
            for u in range(2):
                project_T(gu1(u), T_L1 + u)
            for nh in range(2):
                project_rows(gu1(2 + nh), nh)
            pe.wait_ge(v_ev, C + 1)
            norm(NORM_LAT)
            pe.wait_ge(n_lo, C + 4 * (NORM_LAT + 1))
            for u in range(4):
                project_T(gu1(4 + u), T_L1 + 2 + u)
            for nh in range(2):
                project_rows(gu1(8 + nh), nh)
            pe.wait_ge(v_ev, C + 2)
            pe.wait_ge(k_ev, C + 2 * (T_L1 + 6))

            with pe.Fori(0, HEADS // 4) as i:
                for b in range(2):
                    def score(it):
                        x_ = i * 8 + (C + 4 * b + it)
                        if it == 0:
                            pe.wait_ge(t_cur, i * 2 + (C + b + 1))
                        pe.wait_ge(t_s, x_ - 1)
                        par, qt = it // 2, it % 2
                        rows = slice(HD * par, HD * par + HD)
                        pe.matmul(pg[:, it % 2, :], q_cur[rows, b, qt * P:qt * P + P], k_cur[rows, b, :],
                                  start=True, stop=True).then_inc(t_qk, 1)

                    def turn(it):
                        x_ = i * 8 + (C + 4 * b + it)
                        pe.wait_ge(t_e, x_ + 1)
                        pe.wait_ge(t_pt, x_)
                        for kt in range(4):
                            mm = pe.transpose(ptr[:, kt * P:kt * P + P], prob[:, it % 2, kt * P:kt * P + P], ident[:, :])
                        mm.then_inc(t_tr, 1)

                    def weigh(it):
                        x_ = i * 8 + (C + 4 * b + it)
                        pe.wait_ge(t_pt, x_ + 1)
                        pe.wait_ge(t_o, x_ - 1)
                        col = i * (4 * HD) + (2 * b + it // 2) * HD
                        for kt in range(4):
                            mm = pe.matmul(py[:, it, 0:HD], probT[:, it % 2, kt * P:kt * P + P],
                                           v_all[:, kt, bass.ds(col, HD)], start=kt == 0, stop=kt == 3)
                        mm.then_inc(t_pv, 1)

                    score(0)
                    score(1)
                    turn(0)
                    score(2)
                    turn(1)
                    weigh(0)
                    score(3)
                    turn(2)
                    weigh(1)
                    turn(3)
                    weigh(2)
                    weigh(3)
            pe.wait_ge(t_o, C + 2 * HEADS)
            for q in range(4):
                for kk in range(2):
                    for tt in range(TT):
                        kt = 2 * q + kk
                        mm = pe.transpose(py[:, q, kk * T + tt * P:kk * T + tt * P + P], o_nat[:, tt, kt * P:kt * P + P], ident[:, :])
                mm.then_inc(o_tr, 1)
            pe.wait_ge(o_lo, C + 4)
            for k in range(2):
                project_rows(gu1(10 + k), k)
            gate_rows(RES_ATT)
            norm(NORM_FFN)

            pe.wait_ge(n_a, C + 4 * (NORM_FFN + 1))
            for tt in range(TT):
                for kt in range(KD):
                    mm = pe.matmul(pm[:, tt * NE:tt * NE + NE], aT[:, kt, tt * P:tt * P + P], wr[:, kt, :],
                                   start=kt == 0, stop=kt == KD - 1)
            mm.then_inc(r_lg, 1)
            pe.wait_ge(r_mask, C + 1)
            for dst, terms in ((32, ((tri, 0),)), (40, ((ones, 0), (tri, 1))), (48, ((ones, 0), (ones, 1)))):
                for n, (m_, tt) in enumerate(terms):
                    mm = pe.matmul(pm[:, dst:dst + NE], m_[:, :], route[:, tt, :], start=n == 0, stop=n == len(terms) - 1)
            mm.then_inc(r_pos, 1)
            pe.wait_ge(r_jobs, C + 1)
            over = pe.value_load(jint[0:1, 3:4], min_val=0, max_val=OVER)
            with pe.Fori(0, over + NE) as j:
                q0 = j * STEPSE + D_MOE
                pe.wait_ge(j_pick, j + (C + 1))
                pe.wait_ge(j_acc, j * 2 + C)
                for kt in range(KD):
                    for tt in range(TT):
                        mm = pe.matmul(py[:, kt // 4, (kt % 4) * P:(kt % 4) * P + P], xn[:, tt, kt * P:kt * P + P],
                                       pick[:, tt, :], start=tt == 0, stop=tt == TT - 1)
                mm.then_inc(j_gat, 1)
                pe.wait_ge(f_lo, q0 + C)
                for tt in range(TT):
                    mm = pe.transpose(ptr[:, tt * P:tt * P + P], pickg[:, tt, :], ident[:, :])
                mm.then_inc(j_bt, 1)
                pe.wait_ge(j_lo, j + (C + 1))
                pe.wait_ge(j_ysb, j + C)
                swiglu(STEPSE, 1, q0, lambda k, i: gu1(k, j, i), lambda k, i: d1(j, k, i), 2, (j_back, j + (C + 1)))
                pe.wait_ge(j_ysb, j + (C + 1))
                for tt in range(TT):
                    if tt:
                        pe.wait_ge(j_acc, j * 2 + (C + 1))
                    for nh in range(2):
                        mm = pe.matmul(py[:, nh, :], back[:, tt, :], ysb[:, nh * 512:nh * 512 + 512], start=True, stop=True)
                    mm.then_inc(j_comb, 1)
            gate_rows(RES_MOE)


_INS = ['x', 'c', 'ctx', 'c_ctx', 'w_mod', 'b_mod', 'g_mix', 'g_ffn', 'g_final', 'w_in_ab', 'conv_w', 'pool_w',
        'pool_scale', 'w_out_ab', 'w_ff_gate', 'w_ff_up', 'w_ff_down', 'w_qkv', 'rpb', 'w_out_na', 'w_router',
        'we_gate', 'we_up', 'we_down']


def kernel(**inputs):
    import numpy as _np
    import concourse.bacc as _bacc
    from concourse.bass_utils import run_bass_kernel_spmd as _run

    nc = _bacc.Bacc("TRN2", target_bir_lowering=False, num_devices=1)
    arrays, args = {}, []
    for name in _INS:
        a = _np.ascontiguousarray(inputs[name])
        arrays[f"in_{name}_dram"] = a
        args.append(nc.dram_tensor(f"in_{name}_dram", a.shape, mybir.dt.from_np(a.dtype), kind="ExternalInput").ap())
    args.append(nc.dram_tensor("out_0_dram", (1, T, D), F32, kind="ExternalOutput").ap())
    backbone(nc, *args)
    r = _run(nc, [arrays], core_ids=[0])
    return r.results[0]["out_0_dram"]
```

```python
from contextlib import ExitStack

import concourse.bass as bass
from concourse import mybir

F32 = mybir.dt.float32
F32R = mybir.dt.float32r
I32 = mybir.dt.int32
ALU = mybir.AluOpType
ACT = mybir.ActivationFunctionType
AXX = mybir.AxisListType.X

P = 128
D = 1024
KD = D // P
T = 256
TT = T // P
NS = 2
UC = 512
FS = 256
EPS = 1e-6
GRID = 64
HEADS, HD = 16, 64
WINR, WINC = 8, 16
DFF, DFE, NE, TOPK = 2816, 3584, 8, 2
STEPS0 = DFF // FS
STEPSE = DFE // FS
CAP = P
OVER = (TOPK * T) // (CAP + 1)
JOBS = NE + OVER
ZW = GRID * (GRID + 1)
NDR = 2 * WINR - 1
NDC = 2 * WINC - 1
C = 3
MODU = NS * 6 * D // UC
WINDOWS = (2, 4, 8, 16)
MIX_ORDER = (3, 1, 2, 0)

GU_STREAM = 4 + 2 + STEPS0
GU_L1 = MODU + NS * GU_STREAM
GU_MOE = GU_L1 + 4 + 6 + 2
D_MOE = NS * STEPS0
SLOT_STREAM = (GU_STREAM - GU_STREAM // 2, GU_STREAM // 2)
DSLOT_STREAM = (STEPS0 - STEPS0 // 2, STEPS0 // 2)


def it0(i):
    return 0 if i is None else i


class Unit:

    def __init__(self, slot, n, uses, follows_same_slot):
        self.slot, self.n, self.uses = slot, n, uses
        self.before = n if follows_same_slot else n - 1


def gu_mod(k, i=0):
    return Unit(k % 2, i * 2 + k, i + (k // 2 + 1), False)


def gu0(s, k, i=0):
    return Unit(k % 2, s * GU_STREAM + i * 2 + (MODU + k),
                s * SLOT_STREAM[k % 2] + i + (MODU // 2 + k // 2 + 1), k == 0)


def gu1(k, j=None, i=0):
    if j is None:
        return Unit(k % 2, GU_L1 + k, MODU // 2 + NS * SLOT_STREAM[k % 2] + k // 2 + 1, k == 0)
    base = GU_MOE - GU_L1
    return Unit(k % 2, j * STEPSE + i * 2 + (GU_MOE + k),
                j * (STEPSE // 2) + i + (MODU // 2 + NS * SLOT_STREAM[k % 2] + base // 2 + k // 2 + 1), False)


def d0(s, k, i=0):
    return Unit(k % 2, s * STEPS0 + i * 2 + k, s * DSLOT_STREAM[k % 2] + i + (k // 2 + 1), k == 0)


def d1(j, k, i=0):
    slot = (k + 1) % 2
    return Unit(slot, j * STEPSE + i * 2 + (D_MOE + k),
                j * (STEPSE // 2) + i + (NS * DSLOT_STREAM[slot] + k // 2 + 1), False)


def backbone(nc, x, c, ctx_in, c_ctx, w_mod, b_mod, g_mix, g_ffn, g_final, w_in, conv_w, pool_w,
             pool_scale, w_out, w_gate, w_up, w_down, w_qkv, rpb, w_na, w_router, we_gate, we_up,
             we_down, out):
    stack = ExitStack()
    with stack:
        def sb(name, shape, dt=F32):
            return stack.enter_context(nc.sbuf_tensor(name, shape, dt))

        def ps(name, shape):
            return stack.enter_context(nc.psum_tensor(name, shape, F32))

        owned = {"act": [], "dve": [], "pe": [], "pool": []}

        def sem(name, owner=None):
            s = stack.enter_context(nc.semaphore(name))
            if owner:
                owned[owner].append(s)
            return s

        raw_gu = sb("raw_gu", [P, 2, KD, UC])
        hi_gu = sb("hi_gu", [P, 2, KD, UC], F32R)
        lo_gu = sb("lo_gu", [P, 2, KD, UC], F32R)
        raw_d = sb("raw_d", [P, 2, 2, D])
        hi_d = sb("hi_d", [P, 2, 2, D], F32R)
        lo_d = sb("lo_d", [P, 2, 2, D], F32R)
        h_all = sb("h_all", [P, NS, TT, D])
        scr = sb("scr", [P, 2 * KD, T])
        a_hi = sb("a_hi", [P, KD, T], F32R)
        a_lo = sb("a_lo", [P, KD, T], F32R)
        hT_hi = sb("hT_hi", [P, 2, T], F32R)
        hT_lo = sb("hT_lo", [P, 2, T], F32R)
        hnat = sb("hnat", [P, TT, FS])
        sg = sb("sg", [P, TT, FS])
        ident = sb("ident", [P, P])
        ones = sb("ones", [P, P])
        tri = sb("tri", [P, P])
        iota = sb("iota", [P, P])
        colsA = sb("colsA", [P, P])
        colsB = sb("colsB", [P, 32])
        sil = sb("sil", [P, NS, KD])
        modT = sb("modT", [P, 2, 6, KD, NS])
        gsT = sb("gsT", [P, 2, 2, KD, NS])
        wmask = sb("wmask", [P, GRID])
        edge = sb("edge", [P, 4, 16])
        poolw = sb("poolw", [P, 4, P])
        st = sb("st", [P, 24])
        wr = sb("wr", [P, KD, NE])
        low8 = sb("low8", [P, NE, NE])
        tables = poolw[:, 2:4, :].rearrange("p g c -> p (g c)")
        route = tables[:, 0:48].rearrange("p (a e) -> p a e", a=6)
        jobs = tables[:, 48:48 + 6 * JOBS].rearrange("p (a e) -> p a e", a=6)
        sel = tables[:, 128:128 + OVER * NE].rearrange("p (a e) -> p a e", a=OVER)
        cmp8 = tables[:, 160:160 + NE * NE].rearrange("p (a e) -> p a e", a=NE)
        small = sb("small", [P, 8, NE])
        gcol = small[:, 6, :]
        jint = sb("jint", [P, 4], I32)

        xn = scr[:, 0:KD, :].rearrange("p k t -> p (k t)").rearrange("p (a d) -> p a d", a=TT)
        aT = scr[:, KD:2 * KD, :]
        aT_flat = aT.rearrange("p k t -> p (k t)")
        grow = aT_flat[:, 0:D]
        q_all = aT
        k_lat = scr[:, 0:KD, :]
        k_ctx = h_all[:, 0, :, :].rearrange("p a d -> p (a d)").rearrange("p (k t) -> p k t", k=KD)
        v_all = raw_d[:, :, :, :].rearrange("p a b d -> p (a b) d")
        sl0 = raw_gu[:, 0, :, :].rearrange("p k n -> p (k n)")
        sl1 = raw_gu[:, 1, :, :].rearrange("p k n -> p (k n)")
        bias = sl0[:, 0:2048].rearrange("p (b i n) -> p b i n", b=2, i=4)
        prob = sl0[:, 2048:3072].rearrange("p (b n) -> p b n", b=2)
        probT = sl0[:, 3072:4096].rearrange("p (b n) -> p b n", b=2)
        o_nat = sl1[:, 0:2048].rearrange("p (a d) -> p a d", a=TT)
        q_cur = sl1[:, 2048:2560].rearrange("p (b n) -> p b n", b=2)
        k_cur = sl1[:, 2560:3584].rearrange("p (b n) -> p b n", b=2)
        xg = aT_flat[:, 0:KD * P].rearrange("p (k t) -> p k t", k=KD)
        ysb = aT_flat[:, D:2 * D]
        acc = h_all[:, 0, :, :]
        pick = hnat[:, 1, :].rearrange("p (a s) -> p a s", a=TT)
        pickg = sg[:, 1, :].rearrange("p (a s) -> p a s", a=TT)
        back = poolw[:, 0:2, :]
        ag_hi = a_hi[:, 0:KD // 2, :].rearrange("p k t -> p (k t)").rearrange("p (k t) -> p k t", k=KD)
        ag_lo = a_lo[:, 0:KD // 2, :].rearrange("p k t -> p (k t)").rearrange("p (k t) -> p k t", k=KD)
        zpad = hnat[0:120, 0, 0:2 * (GRID + 1)].rearrange("p (t w) -> p t w", t=2)
        zrep = raw_d[0:120, :, :, :].rearrange("p a b d -> p (a b d)")[:, 0:ZW // 2]
        iota_i = sg[:, 0, 0:P].bitcast(I32)
        sil4 = a_hi[:, 0, 0:4 * KD].rearrange("p (k m) -> p k m", m=4)
        mod_rows = aT_flat[0:4, 0:2 * UC].rearrange("p (b n) -> p b n", b=2)
        fold = small[0:4, 0, 0:2]
        rowsA = scr[:, 0, 0:P]
        rowsB = scr[:, 1, 0:P]

        pg = ps("pg", [P, 2, 512])
        turn_mix = ps("turn_mix", [P, 2, 512])
        ptr, pm = turn_mix[:, 0, :], turn_mix[:, 1, :]
        py = ps("py", [P, 4, 512])

        zed = nc.dram_tensor("skewed_bias", [HEADS * NDR, ZW], F32, kind="Internal").ap()

        x_land = sem("x_land"); rows_land = sem("rows_land"); cst_land = sem("cst_land")
        rpb_land = sem("rpb_land"); z_land = sem("z_land"); bias_land = [sem("bias_land0"), sem("bias_land1")]
        gu_land = [[sem(f"gu_land{slot}{half}") for half in range(2)] for slot in range(2)]
        d_land = [sem("d_land0"), sem("d_land1")]
        gf_land = sem("gf_land"); out_land = sem("out_land")
        consts = sem("consts"); act_pace = sem("act_pace"); p_self = sem("p_self")
        col_tr = sem("col_tr", "pe"); cols = sem("cols", "dve"); sil_done = sem("sil_done", "act"); sil_lo = sem("sil_lo", "dve")
        ada_row = sem("ada_row", "act"); ada_mm = sem("ada_mm", "pe"); ada_ev = sem("ada_ev", "dve")
        gu_hi = sem("gu_hi", "act"); gu_lo = sem("gu_lo", "dve"); gu_used = sem("gu_used", "pe")
        d_hi = sem("d_hi", "act"); d_lo = sem("d_lo", "dve"); d_used = sem("d_used", "pe")
        n_ss = sem("n_ss", "act"); n_ms = sem("n_ms", "dve"); n_sq = sem("n_sq", "act")
        n_xn = sem("n_xn", "dve"); n_tr = sem("n_tr", "pe"); n_a = sem("n_a", "dve")
        n_hi = sem("n_hi", "act"); n_lo = sem("n_lo", "dve")
        k_mm = sem("k_mm", "pe"); k_ev = sem("k_ev", "act")
        m_diff = sem("m_diff", "dve"); m_pool = sem("m_pool", "pe"); m_y = sem("m_y", "dve")
        m_hi = sem("m_hi", "act"); m_lo = sem("m_lo", "dve")
        g_dg = sem("g_dg", "dve"); g_mm = sem("g_mm", "pe"); g_ev = sem("g_ev", "act")
        res = sem("res", "dve"); y_tile = sem("y_tile", "pe")
        f_sil = sem("f_sil", "act"); f_h = sem("f_h", "dve")
        f_tr = sem("f_tr", "pe"); f_hi = sem("f_hi", "act"); f_lo = sem("f_lo", "dve")
        v_ev = sem("v_ev", "act")
        t_cur = sem("t_cur", "act"); t_qk = sem("t_qk", "pe"); t_s = sem("t_s", "dve")
        t_e = sem("t_e", "act"); t_tr = sem("t_tr", "pe"); t_pt = sem("t_pt", "act")
        t_pv = sem("t_pv", "pe"); t_o = sem("t_o", "dve"); t_bias = sem("t_bias", "pool")
        o_tr = sem("o_tr", "pe"); o_hi = sem("o_hi", "act"); o_lo = sem("o_lo", "dve")
        r_lg = sem("r_lg", "pe"); r_mx = sem("r_mx", "dve"); r_ex = sem("r_ex", "act")
        r_mask = sem("r_mask", "dve"); r_pos = sem("r_pos", "pe"); r_jobs = sem("r_jobs", "dve")
        j_pick = sem("j_pick", "dve"); j_gat = sem("j_gat", "pe"); j_xg = sem("j_xg", "dve")
        j_hi = sem("j_hi", "act"); j_lo = sem("j_lo", "dve"); j_bt = sem("j_bt", "pe")
        j_back = sem("j_back", "dve"); j_ysb = sem("j_ysb", "act")
        j_comb = sem("j_comb", "pe"); j_acc = sem("j_acc", "dve")
        fin = sem("fin", "dve")

        NORM_CTX, NORM_LAT, NORM_FFN, NORM_OUT = 4, 5, 6, 7
        RES_ATT, RES_MOE = 4, 5
        T_L1 = NS * 4

        def run_steps(eng, steps, step, more=False):
            step(0, None, True, True)
            loops = (steps - 2 if more else steps - 3) // 2
            with eng.Fori(0, loops) as i:
                for n in (1, 2):
                    step(n, i, True, True)
            for n in range(1 + 2 * loops, steps):
                step(n, None, more or n + 2 < steps, more or n + 1 < steps)

        def run_modulation(eng, step):
            for k in (0, 1):
                step(k, None)
            with eng.Fori(0, (MODU - 4) // 2) as i:
                for k in (2, 3):
                    step(k, i)
            for k in range(MODU - 2, MODU + 2):
                step(k, None)

        def credits(eng, name):
            for s_ in owned[name]:
                eng.sem_inc(s_, C)

        block = stack.enter_context(nc.Block())

        @block.sync
        def _(sp):
            for s, src in ((0, ctx_in), (1, x)):
                sp.dma_start(h_all[:, s, :, :], src[0].rearrange("(a p) d -> p a d", p=P)).then_inc(x_land, 16)
            rows = [(rowsA[0:96, :], b_mod.rearrange("l (m p) -> (l m) p", p=P)),
                    (rowsA[96:112, :], g_mix.rearrange("l (m p) -> (l m) p", p=P)),
                    (rowsA[112:128, :], g_ffn.rearrange("l (m p) -> (l m) p", p=P)),
                    (rowsB[0:12, :], conv_w[0].rearrange("k (m p) -> (k m) p", p=P)),
                    (rowsB[12:16, :], pool_scale[0].rearrange("(m p) -> m p", p=P)),
                    (rowsB[16:24, :], c_ctx.rearrange("(m p) -> m p", p=P)),
                    (rowsB[24:32, :], c[0].rearrange("(m p) -> m p", p=P))]
            for dst, src in rows:
                sp.dma_start(dst, src).then_inc(rows_land, 16)

            def load_gu(u, quarters):
                for half in range(2):
                    if isinstance(u.before, int) and u.before < 1:
                        pass
                    else:
                        sp.wait_ge(gu_lo, u.before * 2 + (C + half - 1))
                    for dst, src in quarters[half]:
                        sp.dma_start(dst, src).then_inc(gu_land[u.slot][half], 16)

            def load_cols(u, v):
                load_gu(u, [[(raw_gu[:, u.slot, k:k + 2, :], v[:, k:k + 2, :]) for k in (4 * half, 4 * half + 2)]
                            for half in range(2)])

            def cols_of(w, unit):
                return w[0].rearrange("(k p) n -> p k n", p=P)[:, :, unit * UC:(unit + 1) * UC]

            wm = [w_mod[l].rearrange("(k p) (j c) -> j p k c", p=P, c=UC) for l in range(2)]
            for k in range(2):
                load_cols(gu_mod(k), wm[0][k])
            sp.dma_start(poolw[:, :, :], pool_w[0].rearrange("g c d -> c g d")).then_inc(cst_land, 16)
            sp.dma_start(wr[:, :, :], w_router[0].rearrange("(k p) e -> p k e", p=P)).then_inc(cst_land, 16)
            for l in range(2):
                with sp.Fori(1 - l, MODU // 4) as i:
                    for k in range(2):
                        load_cols(gu_mod(k + l * MODU // 2, i), wm[l][i * 2 + k])
            sp.wait_ge(z_land, 64)

            def load_step(u, du, g_src, u_src, d_src):
                load_gu(u, [[(raw_gu[:, u.slot, 4 * half:4 * half + 4, c_:c_ + FS], src[:, 4 * half:4 * half + 4, :])
                             for c_, src in ((0, g_src), (FS, u_src))] for half in range(2)])
                sp.wait_ge(d_lo, du.before + C)
                sp.dma_start(raw_d[:, du.slot, :, :], d_src).then_inc(d_land[du.slot], 16)

            gw = w_gate[0].rearrange("(k p) (j c) -> j p k c", p=P, c=FS)
            uw = w_up[0].rearrange("(k p) (j c) -> j p k c", p=P, c=FS)
            dw = w_down[0].rearrange("(j f p) n -> j p f n", p=P, f=2)
            with sp.Fori(0, NS) as s:
                for k, unit in enumerate(MIX_ORDER):
                    load_cols(gu0(s, k), cols_of(w_in, unit))
                for k in range(2):
                    load_cols(gu0(s, 4 + k), cols_of(w_out, k))
                load_step(gu0(s, 6), d0(s, 0), gw[0], uw[0], dw[0])
                with sp.Fori(0, (STEPS0 - 1) // 2) as i:
                    for k in (1, 2):
                        load_step(gu0(s, 6 + k, i), d0(s, k, i), gw[i * 2 + k], uw[i * 2 + k], dw[i * 2 + k])
            for n, unit in enumerate((2, 3, 4, 5, 0, 1, 2, 3, 4, 5)):
                load_cols(gu1(n), cols_of(w_qkv, unit))

            zv = zed[:, WINC - 1:WINC - 1 + GRID * GRID].rearrange("r (j k) -> j r k", k=GRID)

            def load_bias(b, i=None):
                for par in range(2):
                    for qt in range(TT):
                        for r2 in range(2):
                            row = (2 * b + par) * NDR + WINR - 1 - (2 * qt + r2)
                            rows4 = zv[:, row:row + 4, :] if i is None else zv[:, bass.ds(i * (4 * NDR) + row, 4), :]
                            sp.dma_start(bias[64 * r2:64 * r2 + 64, b, 2 * par + qt, :]
                                         .rearrange("p (r k) -> p r k", k=GRID), rows4).then_inc(bias_land[b], 16)

            sp.wait_ge(gu_lo, C + 2 * (GU_L1 + 10))
            for b in range(2):
                load_bias(b)
            with sp.Fori(1, HEADS // 4) as i:
                for b in range(2):
                    sp.wait_ge(t_s, i * 8 + (C + 4 * b - 4))
                    load_bias(b, i)
            sp.wait_ge(o_tr, C + 4)
            for n in (10, 11):
                load_cols(gu1(n), cols_of(w_na, n - 10))

            ge = we_gate[0].rearrange("e (k p) (j c) -> e j p k c", p=P, c=FS)
            ue = we_up[0].rearrange("e (k p) (j c) -> e j p k c", p=P, c=FS)
            de = we_down[0].rearrange("e (j f p) n -> e j p f n", p=P, f=2)

            def load_expert(j, e):
                load_step(gu1(0, j), d1(j, 0), ge[e, 0], ue[e, 0], de[e, 0])
                with sp.Fori(0, (STEPSE - 1) // 2) as i:
                    for k in (1, 2):
                        load_step(gu1(k, j, i), d1(j, k, i), ge[e, i * 2 + k], ue[e, i * 2 + k], de[e, i * 2 + k])
                k = STEPSE - 1
                load_step(gu1(k, j), d1(j, k), ge[e, k], ue[e, k], de[e, k])

            with sp.Fori(0, NE) as j:
                load_expert(j, j)
            sp.wait_ge(r_jobs, C + 1)
            over = sp.value_load(jint[0:1, 3:4], min_val=0, max_val=OVER)
            with sp.If(over > 0):
                with sp.Fori(0, over) as r:
                    e = sp.value_load(jint[0:1, bass.ds(r, 1)], min_val=0, max_val=NE - 1)
                    load_expert(r + NE, e)
            sp.wait_ge(g_dg, C + 6)
            gfin = sl0[:, 0:D]
            sp.dma_start(gfin, g_final.rearrange("(o d) -> o d", o=1).to_broadcast([P, D])).then_inc(gf_land, 16)
            for tt in range(TT):
                sp.wait_ge(fin, C + tt + 1)
                sp.dma_start(out[0].rearrange("(a p) d -> p a d", p=P)[:, tt, :], xn[:, tt, :]).then_inc(out_land, 16)
            sp.wait_ge(out_land, 16 * TT)

        @block.gpsimd
        def _(pool):
            credits(pool, "pool")
            pool.memset(ident[:, :], 0.0).then_inc(p_self, 1)
            pool.memset(ones[:, :], 1.0).then_inc(p_self, 1)
            pool.memset(tri[:, :], 1.0).then_inc(p_self, 1)
            pool.memset(wmask[:, :], 1.0).then_inc(p_self, 1)
            pool.memset(zpad[:, :, :], 0.0).then_inc(p_self, 1)
            pool.wait_ge(p_self, 5)
            pool.affine_select(out=ident[:, :], in_=ident[:, :], compare_op=ALU.not_equal, fill=1.0,
                               base=0, pattern=[[-1, P]], channel_multiplier=1).then_inc(consts, 1)
            pool.affine_select(out=tri[:, :], in_=tri[:, :], compare_op=ALU.is_gt, fill=0.0,
                               base=0, pattern=[[1, P]], channel_multiplier=-1).then_inc(consts, 1)
            pool.iota(iota_i[:, :], pattern=[[1, P]], base=0, channel_multiplier=0).then_inc(consts, 1)
            n = 5
            for r in range(2):
                lo, hi = 64 * r, 64 * r + 64
                for base, mult, step, cols_ in ((WINC // 2, -1, 1, (0, GRID - WINC)),
                                                (WINC // 2 - 1, 1, -1, (WINC, GRID))):
                    a, z = cols_
                    pool.wait_ge(p_self, n)
                    pool.affine_select(out=wmask[lo:hi, a:z], in_=wmask[lo:hi, a:z], compare_op=ALU.is_ge,
                                       fill=0.0, base=base + step * a, pattern=[[step, z - a]],
                                       channel_multiplier=mult).then_inc(p_self, 1)
                    n += 1
            pool.wait_ge(p_self, n)
            pool.tensor_scalar(wmask[:, :], wmask[:, :], -1.0, 1e30, ALU.add, ALU.mult).then_inc(p_self, 1)
            n += 1
            pool.wait_ge(p_self, n)
            for t in range(2):
                pool.dma_start(zpad[0:120, t, 0:NDC], rpb[0].rearrange("h a b -> (h a) b")[120 * t:120 * t + 120, :])\
                    .then_inc(rpb_land, 16)
            pool.wait_ge(rpb_land, 32)
            for t in range(2):
                for q in range(2):
                    if 2 * t + q:
                        pool.wait_ge(z_land, 16 * (2 * t + q))
                    half = ZW // 2
                    pool.tensor_copy(zrep.rearrange("p (j w) -> p j w", w=GRID + 1),
                                     zpad[0:120, t:t + 1, :].to_broadcast([120, GRID // 2, GRID + 1])).then_inc(p_self, 1)
                    n += 1
                    pool.wait_ge(p_self, n)
                    pool.dma_start(zed[120 * t:120 * t + 120, q * half:(q + 1) * half], zrep).then_inc(z_land, 16)
            with pool.Fori(0, HEADS // 4) as i:
                for b in range(2):
                    pool.wait_ge(bias_land[b], i * 128 + 128)
                    v = bias[:, b, :, :].rearrange("p i (r k) -> p (i r) k", k=GRID)
                    pool.tensor_tensor(v, v, wmask[:, None, :].to_broadcast([P, 16, GRID]), ALU.add).then_inc(t_bias, 1)

        @block.scalar
        def _(act):
            credits(act, "act")

            def hi_half(u, h):
                act.wait_ge(gu_land[u.slot][h], u.uses * 32)
                if h == 0:
                    act.wait_ge(gu_used, u.before + C)
                act.activation(hi_gu[:, u.slot, 4 * h:4 * h + 4, :], raw_gu[:, u.slot, 4 * h:4 * h + 4, :],
                               ACT.Copy).then_inc(gu_hi, 1)

            def hi(u):
                hi_half(u, 0)
                hi_half(u, 1)

            def hi_down(u):
                act.wait_ge(d_land[u.slot], u.uses * 16)
                act.wait_ge(d_used, u.before + C)
                act.activation(hi_d[:, u.slot, :, :], raw_d[:, u.slot, :, :], ACT.Copy).then_inc(d_hi, 1)

            def norm_stats(k, h, residuals, x_rows):
                act.wait_ge(x_land, 32)
                for tt in range(TT):
                    act.wait_ge(res, residuals * 2 + (C + tt - 1))
                    act.sem_inc(act_pace, 1)
                    act.activation(xn[:, tt, :], x_rows(tt), ACT.Square, accum_out=st[:, tt:tt + 1]).then_inc(n_ss, 1)
                act.wait_ge(n_ms, h)
                act.activation(st[:, 4:6], st[:, 2:4], ACT.Sqrt).then_inc(n_sq, 1)

            def norm(k, s, residuals):
                norm_stats(k, k + (C + 1), residuals, lambda tt: h_all[:, s, tt, :])
                for q in range(4):
                    act.wait_ge(n_a, k * 4 + (C + q + 1))
                    act.activation(a_hi[:, 2 * q:2 * q + 2, :], aT[:, 2 * q:2 * q + 2, :], ACT.Copy).then_inc(n_hi, 1)

            def evac_T(u, n, half, dst):
                if half:
                    act.wait_ge(gu_used, u.n + (C + 1))
                else:
                    act.wait_ge(k_mm, n + (C + 1))
                act.activation(dst, pg[:, half, :], ACT.Copy).then_inc(k_ev, 1)

            def gate_row(k):
                act.wait_ge(g_mm, k + (C + 1))
                act.activation(grow, turn_mix[:, :, :].rearrange("p a n -> p (a n)"), ACT.Copy).then_inc(g_ev, 1)

            def swiglu(steps, tiles, q0, gu, du, more=None):
                def step(st_, i, ahead, ahead_d):
                    q = lambda n: (q0 + (st_ + n)) if i is None else (i * 2 + q0 + (st_ + n))
                    act.wait_ge(gu_used, gu(st_, it0(i)).n + (C + 1))
                    act.wait_ge(f_h, q(C))
                    for t in range(tiles):
                        b = t if tiles == 2 else st_ % 2
                        ins = act.activation(sg[:, t, :], pg[:, b, 0:FS], ACT.Silu)
                    ins.then_inc(f_sil, 1)
                    if ahead:
                        hi_half(gu(st_ + 2, it0(i)), 0)
                    last = more and st_ == steps - 1
                    if ahead_d and not last:
                        hi_down(du(st_ + 1, it0(i)))
                    act.wait_ge(f_tr, q(C + 1))
                    act.wait_ge(d_used, q(C))
                    n = tiles * P
                    act.activation(hT_hi[:, :, 0:n], ptr[:, 0:2 * n].rearrange("p (f t) -> p f t", f=2),
                                   ACT.Copy).then_inc(f_hi, 1)
                    if last:
                        more()
                    elif ahead:
                        hi_half(gu(st_ + 2, it0(i)), 1)
                run_steps(act, steps, step, more)

            act.wait_ge(cols, C + 2)
            act.activation(sil[:, :, :], colsB[:, 16:32].rearrange("p (s k) -> p s k", s=NS), ACT.Silu).then_inc(sil_done, 1)
            act.wait_ge(sil_done, C + 1)
            act.activation(sil4[:, :, 0:NS], sil[:, :, :].rearrange("p s k -> p k s"), ACT.Copy).then_inc(sil_done, 1)

            def mod_step(k, i):
                if k < MODU:
                    hi(gu_mod(k, it0(i)))
                if 1 <= k <= MODU:
                    n = it0(i) * 2 + (k - 1)
                    b = (k - 1) % 2
                    act.wait_ge(gu_used, n + (C + 1))
                    act.wait_ge(ada_mm, n + (C - 1))
                    act.activation(mod_rows[:, b, :], pg[0:4, b, :], ACT.Copy).then_inc(ada_row, 1)
            run_modulation(act, mod_step)

            with act.Fori(0, NS) as s:
                hi(gu0(s, 0))
                hi(gu0(s, 1))
                norm(s * 2, s, s * 2)
                for k, unit in enumerate(MIX_ORDER):
                    if k == 0:
                        act.wait_ge(n_lo, s * 8 + (C + 4))
                    for half in range(2):
                        m = 4 * unit + 2 * half
                        evac_T(gu0(s, k), s * 4 + k, half, scr[:, m:m + 2, :].rearrange("p m t -> p (m t)"))
                    if k < 3:
                        hi(gu0(s, k + 2))
                for n, m in enumerate((4, 0)):
                    act.wait_ge(m_y, s * 2 + (C + n + 1))
                    act.activation(a_hi[:, m:m + 4, :], scr[:, m:m + 4, :], ACT.Copy).then_inc(m_hi, 1)
                hi(gu0(s, 5))
                gate_row(s * 2)
                hi(gu0(s, 6))
                norm(s * 2 + 1, s, s * 2 + 1)
                hi(gu0(s, 7))
                hi_down(d0(s, 0))
                act.wait_ge(n_lo, s * 8 + (C + 8))
                gate_row(s * 2 + 1)
                swiglu(STEPS0, TT, s * STEPS0, lambda k, i: gu0(s, 6 + k, i), lambda k, i: d0(s, k, i))

            hi(gu1(0))
            hi(gu1(1))
            norm(NORM_CTX, 0, 4)
            for u in range(2):
                for half in range(2):
                    evac_T(gu1(u), T_L1 + u, half, k_ctx[:, 4 * u + 2 * half:4 * u + 2 * half + 2, :].rearrange("p m t -> p (m t)"))
                hi(gu1(u + 2))

            def evac_v(u, tile0):
                act.wait_ge(gu_used, C + u.n + 1)
                act.activation(v_all[:, tile0:tile0 + 2, :].rearrange("p a d -> p (a d)"),
                               py[:, :, :].rearrange("p a n -> p (a n)"), ACT.Copy).then_inc(v_ev, 1)

            act.wait_ge(d_lo, C + D_MOE)
            evac_v(gu1(3), 2)
            hi(gu1(4))
            hi(gu1(5))
            norm(NORM_LAT, 1, 4)
            act.wait_ge(n_lo, C + 4 * (NORM_LAT + 1))
            for u in range(4):
                dst = (q_all, k_lat)[u // 2]
                for half in range(2):
                    m = 4 * (u % 2) + 2 * half
                    evac_T(gu1(4 + u), T_L1 + 2 + u, half, dst[:, m:m + 2, :].rearrange("p m t -> p (m t)"))
                hi(gu1(u + 6))
            evac_v(gu1(9), 0)
            act.wait_ge(gu_lo, C + 2 * (GU_L1 + 10))

            with act.Fori(0, HEADS // 4) as i:
                for b in range(2):
                    act.wait_ge(t_qk, i * 8 + (C + 4 * b))
                    act.wait_ge(k_ev, C + 2 * (T_L1 + 6))
                    act.sem_inc(act_pace, 1)
                    act.activation(q_cur[:, b, :], q_all[:, bass.ds(i * 2 + b, 1), :].rearrange("p o t -> p (o t)"), ACT.Copy)
                    act.activation(k_cur[:, b, 0:T], k_lat[:, bass.ds(i * 2 + b, 1), :].rearrange("p o t -> p (o t)"), ACT.Copy)
                    act.activation(k_cur[:, b, T:2 * T], k_ctx[:, bass.ds(i * 2 + b, 1), :].rearrange("p o t -> p (o t)"), ACT.Copy).then_inc(t_cur, 1)

                    def exps(it):
                        act.wait_ge(t_s, i * 8 + (C + 4 * b + it + 1))
                        act.activation(prob[:, it % 2, :], prob[:, it % 2, :], ACT.Exp, bias=st[:, 20 + it:21 + it],
                                       accum_out=st[:, 12 + it:13 + it]).then_inc(t_e, 1)

                    def turned(it):
                        act.wait_ge(t_tr, i * 8 + (C + 4 * b + it + 1))
                        act.wait_ge(t_pv, i * 8 + (C + 4 * b + it - 1))
                        act.activation(probT[:, it % 2, :], ptr[:, :], ACT.Copy).then_inc(t_pt, 1)

                    exps(0)
                    for it in range(1, 4):
                        exps(it)
                        turned(it - 1)
                    turned(3)
            for q in range(4):
                act.wait_ge(o_tr, C + q + 1)
                act.activation(a_hi[:, 2 * q:2 * q + 2, :].rearrange("p k t -> p (k t)"), py[:, q, :], ACT.Copy).then_inc(o_hi, 1)
            hi(gu1(10))
            hi(gu1(11))
            gate_row(RES_ATT)
            norm(NORM_FFN, 1, RES_ATT + 1)
            act.wait_ge(r_mx, C + 1)
            for tt in range(TT):
                act.activation(small[:, 2 + tt, :], small[:, tt, :], ACT.Exp, bias=st[:, 10 + tt:11 + tt]).then_inc(r_ex, 1)
            for k in range(2):
                hi(gu1(k, 0))
            hi_down(d1(0, 0))

            def gathered(j):
                for h in range(2):
                    act.wait_ge(j_xg, j * 2 + (C + h + 1))
                    act.activation(ag_hi[:, 4 * h:4 * h + 4, :], xg[:, 4 * h:4 * h + 4, :], ACT.Copy).then_inc(j_hi, 1)

            act.wait_ge(r_jobs, C + 1)
            over = act.value_load(jint[0:1, 3:4], min_val=0, max_val=OVER)
            gathered(0)

            def result(j):
                act.wait_ge(d_used, j * STEPSE + (D_MOE + STEPSE + C))
                act.wait_ge(j_comb, j * 2 + C)
                act.activation(ysb, py[:, 2:4, :].rearrange("p a n -> p (a n)"), ACT.Copy).then_inc(j_ysb, 1)

            def job(j, follows):
                def more():
                    gathered(j + 1)
                    hi_down(d1(j, STEPSE))
                    result(j)
                    hi_half(gu1(STEPSE + 1, j), 1)
                swiglu(STEPSE, 1, j * STEPSE + D_MOE, lambda k, i: gu1(k, j, i), lambda k, i: d1(j, k, i),
                       more if follows else None)
                if not follows:
                    result(j)

            with act.Fori(0, over + (NE - 1)) as j:
                job(j, True)
            job(over + (NE - 1), False)
            gate_row(RES_MOE)
            norm_stats(NORM_OUT, C + NORM_OUT + 1, RES_MOE + 1, lambda tt: h_all[:, 1, tt, :])

        @block.vector
        def _(dve):
            credits(dve, "dve")
            dve.memset(low8[:, :, :], 0.0)
            dve.memset(edge[:, :, :], 1.0)
            dve.drain()
            for e in range(1, NE):
                dve.memset(low8[:, e, 0:e], 1.0)
            for g, w in enumerate(WINDOWS):
                for t in range(w // 2):
                    dve.memset(edge[:, g, t:t + 1], w / (t + w // 2))
                for t in range(w - 1 - w // 2):
                    dve.memset(edge[:, g, 15 - t:16 - t], w / (t + 1 + w // 2))
            dve.wait_ge(consts, 3)
            dve.tensor_copy(iota[:, :], iota_i[:, :])
            for n, (dst, rows_) in enumerate(((colsA, P), (colsB, 32))):
                dve.wait_ge(col_tr, C + n + 1)
                dve.tensor_copy(dst[:, :], (pm, ptr)[n][:, 0:rows_]).then_inc(cols, 1)

            def lo_half(u, h):
                dve.wait_ge(gu_hi, u.n * 2 + (C + h + 1))
                k = slice(4 * h, 4 * h + 4)
                dve.tensor_tensor(lo_gu[:, u.slot, k, :], raw_gu[:, u.slot, k, :],
                                  hi_gu[:, u.slot, k, :].bitcast(F32), ALU.subtract).then_inc(gu_lo, 1)

            def lo(u):
                lo_half(u, 0)
                lo_half(u, 1)

            def lo_down(u):
                dve.wait_ge(d_hi, u.n + (C + 1))
                dve.tensor_tensor(lo_d[:, u.slot, :, :], raw_d[:, u.slot, :, :], hi_d[:, u.slot, :, :].bitcast(F32),
                                  ALU.subtract).then_inc(d_lo, 1)

            def rstd(k):
                dve.wait_ge(n_ss, k * 2 + (C + 2))
                dve.tensor_scalar(st[:, 2:4], st[:, 0:2], 1.0 / D, EPS, ALU.mult, ALU.add).then_inc(n_ms, 1)
                dve.wait_ge(n_sq, k + (C + 1))
                dve.reciprocal(st[:, 6:8], st[:, 4:6])
                dve.drain()
                dve.tensor_tensor(st[:, 8:10], st[:, 6:8], st[:, 6:8], ALU.mult)
                dve.drain()
                dve.tensor_tensor(st[:, 8:10], st[:, 8:10], st[:, 2:4], ALU.mult)
                dve.drain()
                dve.tensor_scalar(st[:, 8:10], st[:, 8:10], -0.5, 1.5, ALU.mult, ALU.add)
                dve.drain()
                dve.tensor_tensor(st[:, 6:8], st[:, 6:8], st[:, 8:10], ALU.mult)
                dve.drain()

            def modulate(dst, src, l, half, kt, s):
                gs = gsT[:, l, half, kt, s:s + 1] if isinstance(s, int) else gsT[:, l, half, kt, bass.ds(s, 1)]
                sh = modT[:, l, 3 * half, kt, s:s + 1] if isinstance(s, int) else modT[:, l, 3 * half, kt, bass.ds(s, 1)]
                return dve.tensor_scalar(dst, src, gs, sh, ALU.mult, ALU.add)

            def norm(k, l, half, s):
                rstd(k)
                for tt in range(TT):
                    dve.tensor_scalar(xn[:, tt, :], h_all[:, s, tt, :], st[:, 6 + tt:7 + tt], None, ALU.mult).then_inc(n_xn, 1)
                for q in range(5):
                    if q < 4:
                        dve.wait_ge(n_tr, k * 4 + (C + q + 1))
                        for kk in range(2):
                            ins = modulate(aT[:, 2 * q + kk, :], py[:, q, kk * T:kk * T + T], l, half, 2 * q + kk, s)
                        ins.then_inc(n_a, 1)
                    if q:
                        dve.wait_ge(n_hi, k * 4 + (C + q))
                        v = slice(2 * q - 2, 2 * q)
                        dve.tensor_tensor(a_lo[:, v, :], aT[:, v, :], a_hi[:, v, :].bitcast(F32), ALU.subtract).then_inc(n_lo, 1)

            def gate_col(l, half, s):
                col = modT[:, l, 3 * half + 2, :, s:s + 1] if isinstance(s, int) else modT[:, l, 3 * half + 2, :, bass.ds(s, 1)]
                dve.tensor_copy(gcol[:, :, None], col).then_inc(g_dg, 1)

            def residual(k, s, y=None, done=None):
                dve.wait_ge(g_ev, k + (C + 1))
                for tt in range(TT):
                    if done:
                        dve.wait_ge(*((y_tile, k + (C + 1)) if tt == 0 else done))
                    src = py[:, 2 * tt:2 * tt + 2, :].rearrange("p a n -> p (a n)") if y is None else y[:, tt, :]
                    dve.tensor_tensor(xn[:, tt, :], src, grow, ALU.mult)
                    dve.drain()
                    dve.tensor_tensor(h_all[:, s, tt, :], h_all[:, s, tt, :], xn[:, tt, :], ALU.add).then_inc(res, 1)

            def swiglu(steps, tiles, q0, gu, du, more=None):
                def step(st_, i, ahead, ahead_d):
                    q = lambda n: (q0 + (st_ + n)) if i is None else (i * 2 + q0 + (st_ + n))
                    dve.wait_ge(f_sil, q(C + 1))
                    dve.wait_ge(f_tr, q(C))
                    for t in range(tiles):
                        b = t if tiles == 2 else st_ % 2
                        ins = dve.tensor_tensor(hnat[:, t, :], pg[:, b, FS:2 * FS], sg[:, t, :], ALU.mult)
                    ins.then_inc(f_h, 1)
                    if ahead:
                        lo_half(gu(st_ + 2, it0(i)), 0)
                    last = more and st_ == steps - 1
                    if ahead_d and not last:
                        lo_down(du(st_ + 1, it0(i)))
                    dve.wait_ge(f_hi, q(C + 1))
                    n = tiles * P
                    dve.tensor_tensor(hT_lo[:, :, 0:n], ptr[:, 0:2 * n].rearrange("p (f t) -> p f t", f=2),
                                      hT_hi[:, :, 0:n].bitcast(F32), ALU.subtract).then_inc(f_lo, 1)
                    if last:
                        more()
                    elif ahead:
                        lo_half(gu(st_ + 2, it0(i)), 1)
                run_steps(dve, steps, step, more)

            dve.tensor_tensor(fold, ident[0:4, 0:2], ident[0:4, 2:4], ALU.add)
            dve.wait_ge(sil_done, C + 2)
            dve.tensor_tensor(sil4[:, :, NS:2 * NS], sil[:, :, :].rearrange("p s k -> p k s"),
                              sil4[:, :, 0:NS].bitcast(F32), ALU.subtract)
            dve.drain().then_inc(sil_lo, 1)
            mv = modT[:, :, :, :, :].rearrange("p l i k s -> p (l i k) s")

            def mod_step(k, i):
                if k < MODU:
                    lo(gu_mod(k, it0(i)))
                if k >= 2:
                    dve.wait_ge(ada_mm, it0(i) * 2 + (C + k - 1))
                    m4 = it0(i) * 8 + 4 * (k - 2)
                    dve.tensor_tensor(mv[:, bass.ds(m4, 4), :], (pm, ptr)[k % 2][:, 0:8].rearrange("p (m s) -> p m s", s=NS),
                                      colsA[:, bass.ds(m4, 4)][:, :, None].to_broadcast([P, 4, NS]), ALU.add).then_inc(ada_ev, 1)
            run_modulation(dve, mod_step)
            dve.drain()
            for l in range(2):
                for half in range(2):
                    g = colsA[:, 96 + 16 * half + 8 * l:96 + 16 * half + 8 * l + 8]
                    ins = dve.scalar_tensor_tensor(out=gsT[:, l, half, :, :], in0=modT[:, l, 3 * half + 1, :, :], scalar=1.0,
                                                   in1=g[:, :, None].to_broadcast([P, KD, NS]), op0=ALU.add, op1=ALU.mult)
            dve.drain()
            dve.wait_ge(z_land, 64)

            with dve.Fori(0, NS) as s:
                lo(gu0(s, 0))
                lo(gu0(s, 1))
                gate_col(0, 0, s)
                norm(s * 2, 0, 0, s)
                padA = hnat[:, :, :].rearrange("p a n -> p (a n)")
                padB = sg[:, :, :].rearrange("p a n -> p (a n)")
                for g, w in enumerate(WINDOWS):
                    if g:
                        dve.drain()
                    if g == 2:
                        lo(gu0(s, 2))
                    if g % 2 == 0:
                        dve.wait_ge(k_ev, s * 8 + (C + 1 + g // 2))
                    dve.memset(padA[:, 0:16], 0.0)
                    dve.memset(padA[:, 16 + T:32 + T], 0.0)
                    dve.tensor_copy(padA[:, 16:16 + T], scr[:, 12 + g, :])
                    dve.drain()
                    src, dst, n, back_, fwd = padA, padB, 1, 1, 0
                    lo_, hi_ = 0, T + 32
                    while n < w:
                        lo_, hi_ = lo_ + back_, hi_ - fwd
                        dve.tensor_tensor(dst[:, lo_:hi_], src[:, lo_ - back_:hi_ - back_], src[:, lo_ + fwd:hi_ + fwd], ALU.add)
                        dve.drain()
                        src, dst, n = dst, src, 2 * n
                        back_ = fwd = n // 2
                    for a, e in ((16, 0), (16 + T - 8, 8)):
                        dve.tensor_tensor(src[:, a:a + 8], src[:, a:a + 8], edge[:, g, e:e + 8], ALU.mult)
                    dve.drain()
                    ins = dve.scalar_tensor_tensor(out=scr[:, 12 + g, :], in0=src[:, 16:16 + T], scalar=1.0 / w,
                                                   in1=scr[:, 12 + g, :], op0=ALU.mult, op1=ALU.subtract)
                ins.then_inc(m_diff, 1)
                lo(gu0(s, 3))
                dve.wait_ge(k_ev, s * 8 + (C + 6))
                dve.tensor_tensor(scr[:, 4:8, :], scr[:, 4:8, :], scr[:, 8:12, :], ALU.mult)
                dve.drain()
                for m in range(4):
                    dve.tensor_scalar(scr[:, 8 + m, :], scr[:, 4 + m, :], colsB[:, 4 + m:5 + m], None, ALU.mult)
                dve.drain()
                lo(gu0(s, 4))
                for m in range(4):
                    dve.scalar_tensor_tensor(out=scr[:, 8 + m, 1:T], in0=scr[:, 4 + m, 0:T - 1], scalar=colsB[:, m:m + 1],
                                             in1=scr[:, 8 + m, 1:T], op0=ALU.mult, op1=ALU.add)
                dve.drain()
                for m in range(4):
                    dve.scalar_tensor_tensor(out=scr[:, 8 + m, 0:T - 1], in0=scr[:, 4 + m, 1:T], scalar=colsB[:, 8 + m:9 + m],
                                             in1=scr[:, 8 + m, 0:T - 1], op0=ALU.mult, op1=ALU.add)
                dve.drain()
                dve.wait_ge(m_pool, s + (C + 1))
                for g in range(4):
                    ins = dve.tensor_scalar(scr[:, 4 + g, :], py[:, g // 2, (g % 2) * T:(g % 2) * T + T],
                                            colsB[:, 12 + g:13 + g], None, ALU.mult)
                ins.then_inc(m_y, 1)
                dve.wait_ge(k_ev, s * 8 + (C + 8))
                dve.tensor_tensor(scr[:, 0:4, :], scr[:, 0:4, :], scr[:, 8:12, :], ALU.mult).then_inc(m_y, 1)
                for n, m in enumerate((4, 0)):
                    dve.wait_ge(m_hi, s * 2 + (C + n + 1))
                    dve.tensor_tensor(a_lo[:, m:m + 4, :], scr[:, m:m + 4, :], a_hi[:, m:m + 4, :].bitcast(F32),
                                      ALU.subtract).then_inc(m_lo, 1)
                lo(gu0(s, 5))
                lo(gu0(s, 6))
                residual(s * 2, s, done=(gu_used, gu0(s, 5).n + (C + 1)))
                gate_col(0, 1, s)
                norm(s * 2 + 1, 0, 1, s)
                lo(gu0(s, 7))
                lo_down(d0(s, 0))
                swiglu(STEPS0, TT, s * STEPS0, lambda k, i: gu0(s, 6 + k, i), lambda k, i: d0(s, k, i))
                residual(s * 2 + 1, s, done=(d_used, s * STEPS0 + (STEPS0 + C)))

            lo(gu1(0))
            lo(gu1(1))
            norm(NORM_CTX, 1, 0, 0)
            for n in range(2, 6):
                lo(gu1(n))
            norm(NORM_LAT, 1, 0, 1)
            for n in range(6, 10):
                lo(gu1(n))

            with dve.Fori(0, HEADS // 4) as i:
                for b in range(2):
                    def scores(it):
                        x_ = i * 8 + (C + 4 * b + it)
                        dve.wait_ge(t_qk, x_ + 1)
                        dve.wait_ge(t_tr, x_ - 1)
                        p_ = prob[:, it % 2, :]
                        dve.scalar_tensor_tensor(out=p_[:, 0:T], in0=pg[:, it % 2, 0:T], scalar=HD ** -0.5,
                                                 in1=bias[:, b, it, :], op0=ALU.mult, op1=ALU.add)
                        dve.tensor_scalar(p_[:, T:2 * T], pg[:, it % 2, T:2 * T], HD ** -0.5, None, ALU.mult)
                        dve.drain()
                        dve.tensor_reduce(st[:, 20 + it:21 + it], p_, AXX, ALU.max)
                        dve.drain()
                        dve.tensor_scalar(st[:, 20 + it:21 + it], st[:, 20 + it:21 + it], -1.0, None, ALU.mult).then_inc(t_s, 1)

                    def outs(it):
                        dve.wait_ge(t_pv, i * 8 + (C + 4 * b + it + 1))
                        dve.reciprocal(st[:, 16 + it:17 + it], st[:, 12 + it:13 + it])
                        dve.drain()
                        col = i * (4 * HD) + (2 * b + it // 2) * HD
                        dve.tensor_scalar(o_nat[:, it % 2, bass.ds(col, HD)], py[:, it, 0:HD], st[:, 16 + it:17 + it],
                                          None, ALU.mult).then_inc(t_o, 1)

                    dve.wait_ge(t_bias, i * 2 + (C + b + 1))
                    scores(0)
                    scores(1)
                    scores(2)
                    outs(0)
                    scores(3)
                    for it in range(1, 4):
                        outs(it)
            for q in range(4):
                dve.wait_ge(o_hi, C + q + 1)
                dve.tensor_tensor(a_lo[:, 2 * q:2 * q + 2, :].rearrange("p k t -> p (k t)"), py[:, q, :],
                                  a_hi[:, 2 * q:2 * q + 2, :].rearrange("p k t -> p (k t)").bitcast(F32), ALU.subtract).then_inc(o_lo, 1)
            gate_col(1, 0, 1)
            lo(gu1(10))
            lo(gu1(11))
            residual(RES_ATT, 1, done=(gu_used, C + gu1(11).n + 1))
            norm(NORM_FFN, 1, 1, 1)

            dve.wait_ge(r_lg, C + 1)
            dve.tensor_copy(small[:, 0:2, :], pm[:, 0:2 * NE].rearrange("p (a e) -> p a e", a=TT))
            dve.memset(acc[:, :, :], 0.0)
            dve.drain()
            dve.tensor_reduce(st[:, 8:10], small[:, 0:2, :], AXX, ALU.max)
            dve.drain()
            dve.tensor_scalar(st[:, 10:12], st[:, 8:10], -1.0, None, ALU.mult).then_inc(r_mx, 1)
            for tt in range(TT):
                l_ = small[:, tt, :]
                other = l_[:, None, :].to_broadcast([P, NE, NE])
                own = l_[:, :, None].to_broadcast([P, NE, NE])
                dve.tensor_tensor(cmp8, other, own, ALU.is_equal)
                dve.drain()
                dve.tensor_tensor(cmp8, cmp8, low8[:, :, :], ALU.mult)
                dve.drain()
                dve.tensor_reduce(small[:, 4, :], cmp8, AXX, ALU.add)
                dve.drain()
                dve.tensor_tensor(cmp8, other, own, ALU.is_gt)
                dve.drain()
                dve.tensor_reduce(small[:, 5, :], cmp8, AXX, ALU.add)
                dve.drain()
                dve.tensor_tensor(small[:, 4, :], small[:, 4, :], small[:, 5, :], ALU.add)
                dve.drain()
                ins = dve.tensor_scalar(route[:, tt, :], small[:, 4, :], TOPK - 0.5, None, ALU.is_lt)
                dve.drain()
            dve.drain().then_inc(r_mask, 1)
            dve.wait_ge(r_ex, C + 2)
            for tt in range(TT):
                dve.tensor_tensor(small[:, 2 + tt, :], small[:, 2 + tt, :], route[:, tt, :], ALU.mult)
            dve.drain()
            dve.tensor_reduce(st[:, 12:14], small[:, 2:4, :], AXX, ALU.add)
            dve.drain()
            dve.reciprocal(st[:, 14:16], st[:, 12:14])
            dve.drain()
            for tt in range(TT):
                dve.tensor_scalar(route[:, 4 + tt, :], small[:, 2 + tt, :], st[:, 14 + tt:15 + tt], None, ALU.mult)
            dve.wait_ge(r_pos, C + 1)
            dve.tensor_copy(route[:, 2:4, :], pm[:, 32:48].rearrange("p (a e) -> p a e", a=TT))
            dve.tensor_scalar(small[:, 4, :], pm[:, 48:56], CAP + 0.5, None, ALU.is_gt)
            dve.drain()
            dve.tensor_tensor(cmp8, small[:, 4, :][:, None, :].to_broadcast([P, NE, NE]), low8[:, :, :], ALU.mult)
            dve.drain()
            dve.tensor_reduce(small[:, 5, :], cmp8, AXX, ALU.add)
            dve.tensor_reduce(st[:, 16:17], small[:, 4, :], AXX, ALU.add)
            dve.drain()
            for r in range(OVER):
                dve.scalar_tensor_tensor(out=sel[:, r, :], in0=small[:, 5, :], scalar=float(r), in1=small[:, 4, :],
                                         op0=ALU.is_equal, op1=ALU.mult)
            dve.tensor_copy(jobs[:, :, 0:NE], route)
            dve.drain()
            for r in range(OVER):
                dve.tensor_tensor(cmp8[:, 0:6, :], route, sel[:, r, :][:, None, :].to_broadcast([P, 6, NE]), ALU.mult)
                dve.drain()
                dve.tensor_reduce(jobs[:, :, NE + r], cmp8[:, 0:6, :], AXX, ALU.add)
                dve.drain()
                dve.tensor_scalar(jobs[:, 2:4, NE + r], jobs[:, 2:4, NE + r], -float(CAP), None, ALU.add)
            dve.tensor_tensor(cmp8[:, 0:OVER, :], sel, iota[:, 0:NE][:, None, :].to_broadcast([P, OVER, NE]), ALU.mult)
            dve.drain()
            dve.tensor_reduce(st[:, 17:17 + OVER], cmp8[:, 0:OVER, :], AXX, ALU.add)
            dve.drain()
            dve.tensor_copy(jint[:, 0:OVER], st[:, 17:17 + OVER])
            dve.tensor_copy(jint[:, 3:4], st[:, 16:17])
            dve.drain().then_inc(r_jobs, 1)
            dve.wait_ge(r_jobs, C + 1)
            over = dve.value_load(jint[0:1, 3:4], min_val=0, max_val=OVER)

            def picks(j, first=False):
                if not first:
                    dve.wait_ge(j_gat, j * 2 + C)
                    dve.wait_ge(j_bt, j + C)
                for tt in range(TT):
                    dve.tensor_scalar(pick[:, tt, :], iota[:, :], jobs[:, 2 + tt, bass.ds(j, 1)],
                                      jobs[:, tt, bass.ds(j, 1)], ALU.is_equal, ALU.mult)
                dve.drain()
                for tt in range(TT):
                    ins = dve.tensor_scalar(pickg[:, tt, :], pick[:, tt, :], jobs[:, 4 + tt, bass.ds(j, 1)], None, ALU.mult)
                ins.then_inc(j_pick, 1)

            def gathered(j):
                for h in range(2):
                    dve.wait_ge(j_gat, j * 2 + (C + h + 1))
                    for kt in range(4 * h, 4 * h + 4):
                        ins = modulate(xg[:, kt, :], py[:, h, (kt % 4) * P:(kt % 4) * P + P], 1, 1, kt, 1)
                    ins.then_inc(j_xg, 1)
                for h in range(2):
                    dve.wait_ge(j_hi, j * 2 + (C + h + 1))
                    v = slice(4 * h, 4 * h + 4)
                    dve.tensor_tensor(ag_lo[:, v, :], xg[:, v, :], ag_hi[:, v, :].bitcast(F32), ALU.subtract).then_inc(j_lo, 1)

            def gates_back(j):
                dve.wait_ge(j_bt, j + (C + 1))
                dve.tensor_copy(back, ptr[:, 0:T].rearrange("p (a t) -> p a t", a=TT)).then_inc(j_back, 1)

            def accumulate(j, tt):
                dve.wait_ge(j_comb, j * 2 + (C + tt + 1))
                dve.tensor_tensor(acc[:, tt, :], acc[:, tt, :], py[:, 0:2, :].rearrange("p a n -> p (a n)"), ALU.add).then_inc(j_acc, 1)

            picks(0, True)
            for k in range(2):
                lo(gu1(k, 0))
            lo_down(d1(0, 0))
            gathered(0)
            gates_back(0)

            def job(j, follows):
                def more():
                    gathered(j + 1)
                    lo_down(d1(j, STEPSE))
                    accumulate(j, 0)
                    lo_half(gu1(STEPSE + 1, j), 1)
                    accumulate(j, 1)
                    gates_back(j + 1)
                if follows:
                    picks(j + 1)
                swiglu(STEPSE, 1, j * STEPSE + D_MOE, lambda k, i: gu1(k, j, i), lambda k, i: d1(j, k, i),
                       more if follows else None)
                if not follows:
                    for tt in range(TT):
                        accumulate(j, tt)

            with dve.Fori(0, over + (NE - 1)) as j:
                job(j, True)
            job(over + (NE - 1), False)
            dve.drain()
            gate_col(1, 1, 1)
            residual(RES_MOE, 1, acc)
            rstd(NORM_OUT)
            dve.wait_ge(gf_land, 16)
            for tt in range(TT):
                dve.scalar_tensor_tensor(out=xn[:, tt, :], in0=h_all[:, 1, tt, :], scalar=st[:, 6 + tt:7 + tt],
                                         in1=sl0[:, 0:D], op0=ALU.mult, op1=ALU.mult).then_inc(fin, 1)

        @block.tensor
        def _(pe):
            credits(pe, "pe")
            pe.wait_ge(consts, 3)
            pe.wait_ge(rows_land, 16 * 7)
            pe.transpose(pm[:, 0:P], rowsA, ident[:, :]).then_inc(col_tr, 1)
            pe.transpose(ptr[:, 0:32], rowsB[0:32, :], ident[0:32, 0:32]).then_inc(col_tr, 1)
            pe.wait_ge(sil_lo, C + 1)

            def mod_step(k, i):
                n = it0(i) * 2 + k
                if k < MODU:
                    pe.wait_ge(gu_lo, n * 2 + (C + 2))
                    if k >= 2:
                        pe.wait_ge(ada_row, n + (C - 1))
                    for kt in range(KD):
                        for part in (hi_gu, lo_gu):
                            mm = pe.matmul(pg[0:4, k % 2, :], sil4[:, kt, :], part[:, k % 2, kt, :],
                                           start=kt == 0 and part is hi_gu, stop=kt == KD - 1 and part is lo_gu)
                    mm.then_inc(gu_used, 1)
                if 1 <= k <= MODU:
                    b = (k - 1) % 2
                    pe.wait_ge(ada_row, n + C)
                    pe.wait_ge(ada_ev, n + (C - 2))
                    for m in range(4):
                        mm = pe.matmul((pm, ptr)[b][:, NS * m:NS * m + NS], mod_rows[:, b, m * P:m * P + P], fold,
                                       start=True, stop=True)
                    mm.then_inc(ada_mm, 1)
            run_modulation(pe, mod_step)

            def three(dst, a, b, first, last):
                pe.matmul(dst, a[0], b[0], start=first, stop=False)
                pe.matmul(dst, a[1], b[0], start=False, stop=False)
                return pe.matmul(dst, a[0], b[1], start=False, stop=last)

            def norm(k):
                for tt in range(TT):
                    pe.wait_ge(n_xn, k * 2 + (C + tt + 1))
                    for q in range(4):
                        for kk in range(2):
                            kt = 2 * q + kk
                            mm = pe.transpose(py[:, q, kk * T + tt * P:kk * T + tt * P + P],
                                              xn[:, tt, kt * P:kt * P + P], ident[:, :])
                        if tt:
                            mm.then_inc(n_tr, 1)

            def wait_a(k, kt):
                if k is not None and kt % 2 == 0:
                    pe.wait_ge(n_lo, k * 4 + (C + kt // 2 + 1))

            def wcols(u, kt, a, z):
                return hi_gu[:, u.slot, kt, a:z], lo_gu[:, u.slot, kt, a:z]

            def project_T(u, n, k=None):
                pe.wait_ge(gu_lo, u.n * 2 + (C + 2))
                for half in range(2):
                    pe.wait_ge(k_ev, n * 2 + (C + half - 1))
                    for m in (2 * half, 2 * half + 1):
                        for kt in range(KD):
                            wait_a(k if m == 0 else None, kt)
                            mm = three(pg[:, half, (m % 2) * T:(m % 2) * T + T], wcols(u, kt, m * P, m * P + P),
                                       (a_hi[:, kt, :], a_lo[:, kt, :]), kt == 0, kt == KD - 1)
                    mm.then_inc(gu_used if half else k_mm, 1)

            def project_rows(u, nh, order=range(KD), halves=None, tile_done=False):
                pe.wait_ge(gu_lo, u.n * 2 + (C + 2))
                for tt in range(TT):
                    for n, kt in enumerate(order):
                        if halves and tt == 0 and n % 4 == 0:
                            pe.wait_ge(halves[0], halves[1] + n // 4)
                        mm = three(py[:, 2 * tt + nh, :], (a_hi[:, kt, tt * P:tt * P + P], a_lo[:, kt, tt * P:tt * P + P]),
                                   wcols(u, kt, 0, UC), n == 0, n == KD - 1)
                    if tile_done and tt == 0:
                        mm.then_inc(y_tile, 1)
                mm.then_inc(gu_used, 1)

            def gate_rows(k):
                pe.wait_ge(g_dg, k + (C + 1))
                for kt in range(KD):
                    mm = pe.matmul(turn_mix[:, kt // 4, (kt % 4) * P:(kt % 4) * P + P], gcol[:, kt:kt + 1].to_broadcast([P, P]),
                                   ident[:, :], start=True, stop=True)
                mm.then_inc(g_mm, 1)

            def products(tiles, u, b, part, k=None):
                acts = (a_hi, a_lo) if tiles == 2 else (ag_hi, ag_lo)
                for kt in range(KD) if tiles == 2 else range(4 * part, 4 * part + 4):
                    wait_a(k, kt)
                    mm = three(pg[:, b, :], tuple(x_[:, kt, part * P:part * P + P] if tiles == 2 else x_[:, kt, :] for x_ in acts),
                               wcols(u, kt, 0, 2 * FS), kt == 0, kt == KD - 1)
                return mm

            def swiglu(steps, tiles, q0, gu, du, yb, done_h=None, before_down=None, a_norm=None):
                def up(u, st_, q, part, k=None):
                    b = part if tiles == 2 else st_ % 2
                    if part == 0 or tiles == 2:
                        pe.wait_ge(f_h, q(C) if tiles == 2 else q(C - 1))
                    if part == 0:
                        pe.wait_ge(gu_lo, u.n * 2 + (C + 2 if tiles == 2 else C + 1))
                    elif tiles == 1:
                        pe.wait_ge(gu_lo, u.n * 2 + (C + 2))
                    mm = products(tiles, u, b, part, k)
                    if part == 1:
                        mm.then_inc(gu_used, 1)

                def step(st_, i, ahead_, ahead):
                    q = lambda n: (q0 + (st_ + n)) if i is None else (i * 2 + q0 + (st_ + n))
                    if ahead:
                        up(gu(st_ + 1, it0(i)), st_ + 1, lambda n: q(n + 1), 0)
                    pe.wait_ge(f_h, q(C + 1))
                    if st_ == 0 and done_h:
                        pe.wait_ge(*done_h)
                    pe.wait_ge(f_lo, q(C))
                    for f in range(2):
                        for t in range(tiles):
                            mm = pe.transpose(ptr[:, (f * tiles + t) * P:(f * tiles + t) * P + P],
                                              hnat[:, t, f * P:f * P + P], ident[:, :])
                    mm.then_inc(f_tr, 1)
                    if st_ == steps - 1 and before_down:
                        before_down()
                    if ahead:
                        up(gu(st_ + 1, it0(i)), st_ + 1, lambda n: q(n + 1), 1)
                    u = du(st_, it0(i))
                    pe.wait_ge(f_lo, q(C + 1))
                    pe.wait_ge(d_lo, u.n + (C + 1))
                    for t in range(tiles):
                        for nh in range(2):
                            for f in range(2):
                                mm = three(py[:, yb + 2 * t + nh, :], (hT_hi[:, f, t * P:t * P + P], hT_lo[:, f, t * P:t * P + P]),
                                           (hi_d[:, u.slot, f, nh * 512:nh * 512 + 512], lo_d[:, u.slot, f, nh * 512:nh * 512 + 512]),
                                           st_ == 0 and f == 0, st_ == steps - 1 and i is None and f == 1)
                        if tiles == 2 and t == 0 and st_ == steps - 1 and i is None:
                            mm.then_inc(y_tile, 1)
                    mm.then_inc(d_used, 1)

                if tiles == 2:
                    for part in range(2):
                        up(gu(0, 0), 0, lambda n: q0 + n, part, a_norm if part == 0 else None)
                run_steps(pe, steps, step)

            with pe.Fori(0, NS) as s:
                norm(s * 2)
                for k in range(3):
                    project_T(gu0(s, k), s * 4 + k, s * 2 if k == 0 else None)
                pe.wait_ge(m_diff, s + (C + 1))
                pe.wait_ge(cst_land, 32)
                for g in range(4):
                    mm = pe.matmul(py[:, g // 2, (g % 2) * T:(g % 2) * T + T], poolw[:, g, :], scr[:, 12 + g, :],
                                   start=True, stop=True)
                mm.then_inc(m_pool, 1)
                project_T(gu0(s, 3), s * 4 + 3)
                gate_rows(s * 2)
                project_rows(gu0(s, 4), 0, (4, 5, 6, 7, 0, 1, 2, 3), (m_lo, s * 2 + (C + 1)))
                project_rows(gu0(s, 5), 1, tile_done=True)
                norm(s * 2 + 1)
                gate_rows(s * 2 + 1)
                swiglu(STEPS0, TT, s * STEPS0, lambda k, i: gu0(s, 6 + k, i), lambda k, i: d0(s, k, i), 0,
                       (g_ev, s * 2 + (C + 2)), a_norm=s * 2 + 1)

            norm(NORM_CTX)
            for u in range(2):
                project_T(gu1(u), T_L1 + u, None if u else NORM_CTX)
            for nh in range(2):
                project_rows(gu1(2 + nh), nh)
            pe.wait_ge(v_ev, C + 1)
            norm(NORM_LAT)
            for u in range(4):
                project_T(gu1(4 + u), T_L1 + 2 + u, None if u else NORM_LAT)
            for nh in range(2):
                project_rows(gu1(8 + nh), nh)
            pe.wait_ge(v_ev, C + 2)
            pe.wait_ge(k_ev, C + 2 * (T_L1 + 6))

            with pe.Fori(0, HEADS // 4) as i:
                for b in range(2):
                    def score(it):
                        x_ = i * 8 + (C + 4 * b + it)
                        if it == 0:
                            pe.wait_ge(t_cur, i * 2 + (C + b + 1))
                        pe.wait_ge(t_s, x_ - 1)
                        par, qt = it // 2, it % 2
                        rows = slice(HD * par, HD * par + HD)
                        pe.matmul(pg[:, it % 2, :], q_cur[rows, b, qt * P:qt * P + P], k_cur[rows, b, :],
                                  start=True, stop=True).then_inc(t_qk, 1)

                    def turn(it):
                        x_ = i * 8 + (C + 4 * b + it)
                        pe.wait_ge(t_e, x_ + 1)
                        pe.wait_ge(t_pt, x_)
                        for kt in range(4):
                            mm = pe.transpose(ptr[:, kt * P:kt * P + P], prob[:, it % 2, kt * P:kt * P + P], ident[:, :])
                        mm.then_inc(t_tr, 1)

                    def weigh(it):
                        x_ = i * 8 + (C + 4 * b + it)
                        pe.wait_ge(t_pt, x_ + 1)
                        pe.wait_ge(t_o, x_ - 1)
                        col = i * (4 * HD) + (2 * b + it // 2) * HD
                        for kt in range(4):
                            mm = pe.matmul(py[:, it, 0:HD], probT[:, it % 2, kt * P:kt * P + P],
                                           v_all[:, kt, bass.ds(col, HD)], start=kt == 0, stop=kt == 3)
                        mm.then_inc(t_pv, 1)

                    score(0)
                    score(1)
                    turn(0)
                    score(2)
                    turn(1)
                    weigh(0)
                    score(3)
                    turn(2)
                    weigh(1)
                    turn(3)
                    weigh(2)
                    weigh(3)
            pe.wait_ge(t_o, C + 2 * HEADS)
            for q in range(4):
                for kk in range(2):
                    for tt in range(TT):
                        kt = 2 * q + kk
                        mm = pe.transpose(py[:, q, kk * T + tt * P:kk * T + tt * P + P], o_nat[:, tt, kt * P:kt * P + P], ident[:, :])
                mm.then_inc(o_tr, 1)
            gate_rows(RES_ATT)
            pe.wait_ge(o_lo, C + 4)
            for k in range(2):
                project_rows(gu1(10 + k), k, tile_done=k == 1)
            norm(NORM_FFN)

            pe.wait_ge(n_a, C + 4 * (NORM_FFN + 1))
            for tt in range(TT):
                for kt in range(KD):
                    mm = pe.matmul(pm[:, tt * NE:tt * NE + NE], aT[:, kt, tt * P:tt * P + P], wr[:, kt, :],
                                   start=kt == 0, stop=kt == KD - 1)
            mm.then_inc(r_lg, 1)
            pe.wait_ge(r_mask, C + 1)
            for dst, terms in ((32, ((tri, 0),)), (40, ((ones, 0), (tri, 1))), (48, ((ones, 0), (ones, 1)))):
                for n, (m_, tt) in enumerate(terms):
                    mm = pe.matmul(pm[:, dst:dst + NE], m_[:, :], route[:, tt, :], start=n == 0, stop=n == len(terms) - 1)
            mm.then_inc(r_pos, 1)
            pe.wait_ge(r_jobs, C + 1)
            over = pe.value_load(jint[0:1, 3:4], min_val=0, max_val=OVER)

            def gather(j):
                pe.wait_ge(j_pick, j + (C + 1))
                for h in range(2):
                    for kt in range(4 * h, 4 * h + 4):
                        for tt in range(TT):
                            mm = pe.matmul(py[:, h, (kt % 4) * P:(kt % 4) * P + P], xn[:, tt, kt * P:kt * P + P],
                                           pick[:, tt, :], start=tt == 0, stop=tt == TT - 1)
                    mm.then_inc(j_gat, 1)

            def first_up(j, part):
                q0 = j * STEPSE + D_MOE
                if part == 0:
                    pe.wait_ge(f_h, q0 + (C - 1))
                u = gu1(0, j)
                pe.wait_ge(gu_lo, u.n * 2 + (C + part + 1))
                pe.wait_ge(j_lo, j * 2 + (C + part + 1))
                mm = products(1, u, 0, part)
                if part == 1:
                    mm.then_inc(gu_used, 1)

            def gates_back(j):
                pe.wait_ge(f_lo, j * STEPSE + (D_MOE + C))
                for tt in range(TT):
                    mm = pe.transpose(ptr[:, tt * P:tt * P + P], pickg[:, tt, :], ident[:, :])
                mm.then_inc(j_bt, 1)

            def combine(j, tt):
                if tt == 0:
                    pe.wait_ge(j_ysb, j + (C + 1))
                else:
                    pe.wait_ge(j_acc, j * 2 + (C + 1))
                for nh in range(2):
                    mm = pe.matmul(py[:, nh, :], back[:, tt, :], ysb[:, nh * 512:nh * 512 + 512], start=True, stop=True)
                mm.then_inc(j_comb, 1)

            gather(0)
            for part in range(2):
                first_up(0, part)
            gates_back(0)

            def job(j, follows):
                def gather_next():
                    pe.wait_ge(j_acc, j * 2 + C)
                    gather(j + 1)
                swiglu(STEPSE, 1, j * STEPSE + D_MOE, lambda k, i: gu1(k, j, i), lambda k, i: d1(j, k, i), 2,
                       (j_back, j + (C + 1)), gather_next if follows else None)
                if follows:
                    first_up(j + 1, 0)
                    pe.wait_ge(j_xg, j * 2 + (C + 4))
                combine(j, 0)
                if follows:
                    first_up(j + 1, 1)
                combine(j, 1)
                if follows:
                    gates_back(j + 1)

            with pe.Fori(0, over + (NE - 1)) as j:
                job(j, True)
            job(over + (NE - 1), False)
            gate_rows(RES_MOE)


_INS = ['x', 'c', 'ctx', 'c_ctx', 'w_mod', 'b_mod', 'g_mix', 'g_ffn', 'g_final', 'w_in_ab', 'conv_w', 'pool_w',
        'pool_scale', 'w_out_ab', 'w_ff_gate', 'w_ff_up', 'w_ff_down', 'w_qkv', 'rpb', 'w_out_na', 'w_router',
        'we_gate', 'we_up', 'we_down']


def kernel(**inputs):
    import numpy as _np
    import concourse.bacc as _bacc
    from concourse.bass_utils import run_bass_kernel_spmd as _run

    nc = _bacc.Bacc("TRN2", target_bir_lowering=False, num_devices=1)
    arrays, args = {}, []
    for name in _INS:
        a = _np.ascontiguousarray(inputs[name])
        arrays[f"in_{name}_dram"] = a
        args.append(nc.dram_tensor(f"in_{name}_dram", a.shape, mybir.dt.from_np(a.dtype), kind="ExternalInput").ap())
    args.append(nc.dram_tensor("out_0_dram", (1, T, D), F32, kind="ExternalOutput").ap())
    backbone(nc, *args)
    r = _run(nc, [arrays], core_ids=[0])
    return r.results[0]["out_0_dram"]
```

```python
from contextlib import ExitStack

import concourse.bass as bass
from concourse import mybir

F32 = mybir.dt.float32
F32R = mybir.dt.float32r
I32 = mybir.dt.int32
ALU = mybir.AluOpType
ACT = mybir.ActivationFunctionType
AXX = mybir.AxisListType.X

P = 128
D = 1024
KD = D // P
T = 256
TT = T // P
NS = 2
UC = 512
FS = 256
EPS = 1e-6
GRID = 64
HEADS, HD = 16, 64
WINR, WINC = 8, 16
DFF, DFE, NE, TOPK = 2816, 3584, 8, 2
STEPS0 = DFF // FS
STEPSE = DFE // FS
CAP = P
OVER = (TOPK * T) // (CAP + 1)
JOBS = NE + OVER
ZW = GRID * (GRID + 1)
NDR = 2 * WINR - 1
NDC = 2 * WINC - 1
C = 3
MODU = NS * 6 * D // UC
WINDOWS = (2, 4, 8, 16)
MIX_ORDER = (3, 1, 2, 0)

GU_STREAM = 4 + 2 + STEPS0
GU_L1 = MODU + NS * GU_STREAM
GU_MOE = GU_L1 + 4 + 6 + 2
D_MOE = NS * STEPS0
SLOT_STREAM = (GU_STREAM - GU_STREAM // 2, GU_STREAM // 2)
DSLOT_STREAM = (STEPS0 - STEPS0 // 2, STEPS0 // 2)


def it0(i):
    return 0 if i is None else i


class Unit:

    def __init__(self, slot, n, uses, follows_same_slot):
        self.slot, self.n, self.uses = slot, n, uses
        self.before = n if follows_same_slot else n - 1


def gu_mod(k, i=0):
    return Unit(k % 2, i * 2 + k, i + (k // 2 + 1), False)


def gu0(s, k, i=0):
    return Unit(k % 2, s * GU_STREAM + i * 2 + (MODU + k),
                s * SLOT_STREAM[k % 2] + i + (MODU // 2 + k // 2 + 1), k == 0)


def gu1(k, j=None, i=0):
    if j is None:
        return Unit(k % 2, GU_L1 + k, MODU // 2 + NS * SLOT_STREAM[k % 2] + k // 2 + 1, k == 0)
    base = GU_MOE - GU_L1
    return Unit(k % 2, j * STEPSE + i * 2 + (GU_MOE + k),
                j * (STEPSE // 2) + i + (MODU // 2 + NS * SLOT_STREAM[k % 2] + base // 2 + k // 2 + 1), False)


def d0(s, k, i=0):
    return Unit(k % 2, s * STEPS0 + i * 2 + k, s * DSLOT_STREAM[k % 2] + i + (k // 2 + 1), k == 0)


def d1(j, k, i=0):
    slot = (k + 1) % 2
    return Unit(slot, j * STEPSE + i * 2 + (D_MOE + k),
                j * (STEPSE // 2) + i + (NS * DSLOT_STREAM[slot] + k // 2 + 1), False)


def backbone(nc, x, c, ctx_in, c_ctx, w_mod, b_mod, g_mix, g_ffn, g_final, w_in, conv_w, pool_w,
             pool_scale, w_out, w_gate, w_up, w_down, w_qkv, rpb, w_na, w_router, we_gate, we_up,
             we_down, out):
    stack = ExitStack()
    with stack:
        def sb(name, shape, dt=F32):
            return stack.enter_context(nc.sbuf_tensor(name, shape, dt))

        def ps(name, shape):
            return stack.enter_context(nc.psum_tensor(name, shape, F32))

        owned = {"act": [], "dve": [], "pe": [], "pool": []}

        def sem(name, owner=None):
            s = stack.enter_context(nc.semaphore(name))
            if owner:
                owned[owner].append(s)
            return s

        raw_gu = sb("raw_gu", [P, 2, KD, UC])
        hi_gu = sb("hi_gu", [P, 2, KD, UC], F32R)
        lo_gu = sb("lo_gu", [P, 2, KD, UC], F32R)
        raw_d = sb("raw_d", [P, 2, 2, D])
        hi_d = sb("hi_d", [P, 2, 2, D], F32R)
        lo_d = sb("lo_d", [P, 2, 2, D], F32R)
        h_all = sb("h_all", [P, NS, TT, D])
        scr = sb("scr", [P, 2 * KD, T])
        a_hi = sb("a_hi", [P, KD, T], F32R)
        a_lo = sb("a_lo", [P, KD, T], F32R)
        hT = sb("hT", [P, 2, 2, T], F32R)
        hidden = sb("hidden", [P, 2, TT, FS])
        hT_hi, hT_lo = hT[:, 0, :, :], hT[:, 1, :, :]
        hnat, sg = hidden[:, 0, :, :], hidden[:, 1, :, :]
        ident = sb("ident", [P, P])
        ones = sb("ones", [P, P])
        tri = sb("tri", [P, P])
        iota = sb("iota", [P, P])
        colsA = sb("colsA", [P, P])
        colsB = sb("colsB", [P, 32])
        sil = sb("sil", [P, NS, KD])
        modT = sb("modT", [P, 2, 6, KD, NS])
        gsT = sb("gsT", [P, 2, 2, KD, NS])
        wmask = sb("wmask", [P, GRID])
        edge = sb("edge", [P, 4, 16])
        poolw = sb("poolw", [P, 4, P])
        st = sb("st", [P, 24])
        wr = sb("wr", [P, KD, NE])
        low8 = sb("low8", [P, NE, NE])
        tables = poolw[:, 2:4, :].rearrange("p g c -> p (g c)")
        route = tables[:, 0:48].rearrange("p (a e) -> p a e", a=6)
        jobs = tables[:, 48:48 + 6 * JOBS].rearrange("p (a e) -> p a e", a=6)
        sel = tables[:, 128:128 + OVER * NE].rearrange("p (a e) -> p a e", a=OVER)
        cmp8 = tables[:, 160:160 + NE * NE].rearrange("p (a e) -> p a e", a=NE)
        small = sb("small", [P, 8, NE])
        gcol = small[:, 6, :]
        jint = sb("jint", [P, 4], I32)

        xn = scr[:, 0:KD, :].rearrange("p k t -> p (k t)").rearrange("p (a d) -> p a d", a=TT)
        aT = scr[:, KD:2 * KD, :]
        aT_flat = aT.rearrange("p k t -> p (k t)")
        grow = aT_flat[:, 0:D]
        q_all = aT
        k_lat = scr[:, 0:KD, :]
        k_ctx = h_all[:, 0, :, :].rearrange("p a d -> p (a d)").rearrange("p (k t) -> p k t", k=KD)
        v_all = raw_d[:, :, :, :].rearrange("p a b d -> p (a b) d")
        gfin = raw_gu[:, 0, 0:2, :].rearrange("p k n -> p (k n)")
        sl0 = raw_gu[:, 0, :, :].rearrange("p k n -> p (k n)")
        sl1 = raw_gu[:, 1, :, :].rearrange("p k n -> p (k n)")
        bias = (hidden[:, :, :, :].rearrange("p a t f -> p (a t) f"),
                sl0[:, 0:1024].rearrange("p (i n) -> p i n", i=4))
        prob = sl0[:, 2048:3072].rearrange("p (b n) -> p b n", b=2)
        probT = sl0[:, 3072:4096].rearrange("p (b n) -> p b n", b=2)
        o_nat = sl1[:, 0:2048].rearrange("p (a d) -> p a d", a=TT)
        q_cur = sl1[:, 2048:2560].rearrange("p (b n) -> p b n", b=2)
        k_cur = sl1[:, 2560:3584].rearrange("p (b n) -> p b n", b=2)
        xg = aT_flat[:, 0:KD * P].rearrange("p (k t) -> p k t", k=KD)
        ysb = aT_flat[:, D:2 * D]
        acc = h_all[:, 0, :, :]
        pick = hnat[:, 1, :].rearrange("p (a s) -> p a s", a=TT)
        pickg = sg[:, 1, :].rearrange("p (a s) -> p a s", a=TT)
        back = poolw[:, 0:2, :]
        ag_hi = a_hi[:, 0:KD // 2, :].rearrange("p k t -> p (k t)").rearrange("p (k t) -> p k t", k=KD)
        ag_lo = a_lo[:, 0:KD // 2, :].rearrange("p k t -> p (k t)").rearrange("p (k t) -> p k t", k=KD)
        zwords = raw_d[0:120, :, :, :].rearrange("p a b d -> p (a b d)")
        zrep, zpad = zwords[:, 0:ZW // 2], zwords[:, ZW // 2:ZW // 2 + 2 * (GRID + 1)].rearrange("p (t w) -> p t w", t=2)
        iota_i = sg[:, 0, 0:P].bitcast(I32)
        sil4 = a_hi[:, 0, 0:4 * KD].rearrange("p (k m) -> p k m", m=4)
        mod_rows = aT_flat[0:4, 0:2 * UC].rearrange("p (b n) -> p b n", b=2)
        fold = small[0:4, 0, 0:2]
        rowsA = scr[:, 0, 0:P]
        rowsB = scr[:, 1, 0:P]

        pg = ps("pg", [P, 2, 512])
        turn_mix = ps("turn_mix", [P, 2, 512])
        ptr, pm = turn_mix[:, 0, :], turn_mix[:, 1, :]
        py = ps("py", [P, 4, 512])

        zed = nc.dram_tensor("skewed_bias", [HEADS * NDR, ZW], F32, kind="Internal").ap()

        x_land = sem("x_land"); rows_land = sem("rows_land"); cst_land = sem("cst_land")
        rpb_land = sem("rpb_land"); z_land = sem("z_land"); bias_land = [sem("bias_land0"), sem("bias_land1")]
        gu_land = [[sem(f"gu_land{slot}{half}") for half in range(2)] for slot in range(2)]
        d_land = [sem("d_land0"), sem("d_land1")]
        gf_land = sem("gf_land"); out_land = sem("out_land")
        consts = sem("consts"); act_pace = sem("act_pace"); p_self = sem("p_self")
        col_tr = sem("col_tr", "pe"); cols = sem("cols", "dve"); sil_done = sem("sil_done", "act"); sil_lo = sem("sil_lo", "dve")
        ada_row = sem("ada_row", "act"); ada_mm = sem("ada_mm", "pe"); ada_ev = sem("ada_ev", "dve")
        gu_hi = sem("gu_hi", "act"); gu_lo = sem("gu_lo", "dve"); gu_used = sem("gu_used", "pe")
        d_hi = sem("d_hi", "act"); d_lo = sem("d_lo", "dve"); d_used = sem("d_used", "pe")
        n_ss = sem("n_ss", "act"); n_ms = sem("n_ms", "dve"); n_sq = sem("n_sq", "act")
        n_xn = sem("n_xn", "dve"); n_tr = sem("n_tr", "pe"); n_a = sem("n_a", "dve")
        n_hi = sem("n_hi", "act"); n_lo = sem("n_lo", "dve")
        k_mm = sem("k_mm", "pe"); k_ev = sem("k_ev", "act")
        m_diff = sem("m_diff", "dve"); m_pool = sem("m_pool", "pe"); m_y = sem("m_y", "dve")
        m_hi = sem("m_hi", "act"); m_lo = sem("m_lo", "dve")
        g_dg = sem("g_dg", "dve"); g_mm = sem("g_mm", "pe"); g_ev = sem("g_ev", "act")
        res = sem("res", "dve"); y_tile = sem("y_tile", "pe")
        f_sil = sem("f_sil", "act"); f_h = sem("f_h", "dve")
        f_tr = sem("f_tr", "pe"); f_hi = sem("f_hi", "act"); f_lo = sem("f_lo", "dve")
        v_ev = sem("v_ev", "act")
        t_cur = sem("t_cur", "act"); t_qk = sem("t_qk", "pe"); t_s = sem("t_s", "dve")
        t_e = sem("t_e", "act"); t_tr = sem("t_tr", "pe"); t_pt = sem("t_pt", "act")
        t_pv = sem("t_pv", "pe"); t_o = sem("t_o", "dve"); t_bias = sem("t_bias", "pool")
        o_tr = sem("o_tr", "pe"); o_hi = sem("o_hi", "act"); o_lo = sem("o_lo", "dve")
        r_lg = sem("r_lg", "pe"); r_mx = sem("r_mx", "dve"); r_ex = sem("r_ex", "act")
        r_mask = sem("r_mask", "dve"); r_pos = sem("r_pos", "pe"); r_jobs = sem("r_jobs", "dve")
        j_pick = sem("j_pick", "dve"); j_gat = sem("j_gat", "pe"); j_xg = sem("j_xg", "dve")
        j_hi = sem("j_hi", "act"); j_lo = sem("j_lo", "dve"); j_bt = sem("j_bt", "pe")
        j_back = sem("j_back", "dve"); j_ysb = sem("j_ysb", "act")
        j_comb = sem("j_comb", "pe"); j_acc = sem("j_acc", "dve")
        fin = sem("fin", "dve")

        NORM_CTX, NORM_LAT, NORM_FFN, NORM_OUT = 4, 5, 6, 7
        RES_ATT, RES_MOE = 4, 5
        T_L1 = NS * 4

        def run_steps(eng, steps, step, more=False):
            step(0, None, True, True)
            loops = (steps - 2 if more else steps - 3) // 2
            with eng.Fori(0, loops) as i:
                for n in (1, 2):
                    step(n, i, True, True)
            for n in range(1 + 2 * loops, steps):
                step(n, None, more or n + 2 < steps, more or n + 1 < steps)

        def run_modulation(eng, step):
            for k in (0, 1):
                step(k, None)
            with eng.Fori(0, (MODU - 4) // 2) as i:
                for k in (2, 3):
                    step(k, i)
            for k in range(MODU - 2, MODU + 2):
                step(k, None)

        def run_pairs(eng, pair):
            with eng.Fori(0, HEADS // 4 - 1) as i:
                for b in range(2):
                    pair(i, b, True)
            for b in range(2):
                pair(HEADS // 4 - 1, b, b == 0)

        def credits(eng, name):
            for s_ in owned[name]:
                eng.sem_inc(s_, C)

        block = stack.enter_context(nc.Block())

        @block.sync
        def _(sp):
            for s, src in ((0, ctx_in), (1, x)):
                sp.dma_start(h_all[:, s, :, :], src[0].rearrange("(a p) d -> p a d", p=P)).then_inc(x_land, 16)
            rows = [(rowsA[0:96, :], b_mod.rearrange("l (m p) -> (l m) p", p=P)),
                    (rowsA[96:112, :], g_mix.rearrange("l (m p) -> (l m) p", p=P)),
                    (rowsA[112:128, :], g_ffn.rearrange("l (m p) -> (l m) p", p=P)),
                    (rowsB[0:12, :], conv_w[0].rearrange("k (m p) -> (k m) p", p=P)),
                    (rowsB[12:16, :], pool_scale[0].rearrange("(m p) -> m p", p=P)),
                    (rowsB[16:24, :], c_ctx.rearrange("(m p) -> m p", p=P)),
                    (rowsB[24:32, :], c[0].rearrange("(m p) -> m p", p=P))]
            for dst, src in rows:
                sp.dma_start(dst, src).then_inc(rows_land, 16)

            def load_gu(u, quarters):
                for half in range(2):
                    if isinstance(u.before, int) and u.before < 1:
                        pass
                    else:
                        sp.wait_ge(gu_lo, u.before * 2 + (C + half - 1))
                    for dst, src in quarters[half]:
                        sp.dma_start(dst, src).then_inc(gu_land[u.slot][half], 16)

            def load_cols(u, v):
                load_gu(u, [[(raw_gu[:, u.slot, k:k + 2, :], v[:, k:k + 2, :]) for k in (4 * half, 4 * half + 2)]
                            for half in range(2)])

            def cols_of(w, unit):
                return w[0].rearrange("(k p) n -> p k n", p=P)[:, :, unit * UC:(unit + 1) * UC]

            wm = [w_mod[l].rearrange("(k p) (j c) -> j p k c", p=P, c=UC) for l in range(2)]
            for k in range(2):
                load_cols(gu_mod(k), wm[0][k])
            sp.dma_start(poolw[:, :, :], pool_w[0].rearrange("g c d -> c g d")).then_inc(cst_land, 16)
            sp.dma_start(wr[:, :, :], w_router[0].rearrange("(k p) e -> p k e", p=P)).then_inc(cst_land, 16)
            for l in range(2):
                with sp.Fori(1 - l, MODU // 4) as i:
                    for k in range(2):
                        load_cols(gu_mod(k + l * MODU // 2, i), wm[l][i * 2 + k])

            def load_step(u, du, g_src, u_src, d_src):
                load_gu(u, [[(raw_gu[:, u.slot, 4 * half:4 * half + 4, c_:c_ + FS], src[:, 4 * half:4 * half + 4, :])
                             for c_, src in ((0, g_src), (FS, u_src))] for half in range(2)])
                sp.wait_ge(d_lo, du.before + C)
                sp.dma_start(raw_d[:, du.slot, :, :], d_src).then_inc(d_land[du.slot], 16)

            gw = w_gate[0].rearrange("(k p) (j c) -> j p k c", p=P, c=FS)
            uw = w_up[0].rearrange("(k p) (j c) -> j p k c", p=P, c=FS)
            dw = w_down[0].rearrange("(j f p) n -> j p f n", p=P, f=2)
            with sp.Fori(0, NS) as s:
                for k, unit in enumerate(MIX_ORDER):
                    load_cols(gu0(s, k), cols_of(w_in, unit))
                for k in range(2):
                    load_cols(gu0(s, 4 + k), cols_of(w_out, k))
                sp.wait_ge(z_land, 64)
                load_step(gu0(s, 6), d0(s, 0), gw[0], uw[0], dw[0])
                with sp.Fori(0, (STEPS0 - 1) // 2) as i:
                    for k in (1, 2):
                        load_step(gu0(s, 6 + k, i), d0(s, k, i), gw[i * 2 + k], uw[i * 2 + k], dw[i * 2 + k])
            for n, unit in enumerate((2, 3, 4, 5, 0, 1, 2, 3, 4, 5)):
                load_cols(gu1(n), cols_of(w_qkv, unit))

            zv = zed[:, WINC - 1:WINC - 1 + GRID * GRID].rearrange("r (j k) -> j r k", k=GRID)

            def load_bias(b, i=None):
                for par in range(2):
                    for qt in range(TT):
                        for r2 in range(2):
                            row = (2 * b + par) * NDR + WINR - 1 - (2 * qt + r2)
                            rows4 = zv[:, row:row + 4, :] if i is None else zv[:, bass.ds(i * (4 * NDR) + row, 4), :]
                            sp.dma_start(bias[b][64 * r2:64 * r2 + 64, 2 * par + qt, :]
                                         .rearrange("p (r k) -> p r k", k=GRID), rows4).then_inc(bias_land[b], 16)

            sp.wait_ge(res, C + 8)
            for b in range(2):
                if b:
                    sp.wait_ge(gu_lo, C + 2 * (GU_L1 + 10))
                load_bias(b)
            with sp.Fori(1, HEADS // 4) as i:
                for b in range(2):
                    sp.wait_ge(t_s, i * 8 + (C + 4 * b - 4))
                    load_bias(b, i)

            for n, spent in ((10, (t_pv, C + 2 * HEADS)), (11, (o_tr, C + 4))):
                sp.wait_ge(*spent)
                load_cols(gu1(n), cols_of(w_na, n - 10))

            ge = we_gate[0].rearrange("e (k p) (j c) -> e j p k c", p=P, c=FS)
            ue = we_up[0].rearrange("e (k p) (j c) -> e j p k c", p=P, c=FS)
            de = we_down[0].rearrange("e (j f p) n -> e j p f n", p=P, f=2)

            def load_expert(j, e):
                load_step(gu1(0, j), d1(j, 0), ge[e, 0], ue[e, 0], de[e, 0])
                with sp.Fori(0, (STEPSE - 1) // 2) as i:
                    for k in (1, 2):
                        load_step(gu1(k, j, i), d1(j, k, i), ge[e, i * 2 + k], ue[e, i * 2 + k], de[e, i * 2 + k])
                k = STEPSE - 1
                load_step(gu1(k, j), d1(j, k), ge[e, k], ue[e, k], de[e, k])

            with sp.Fori(0, NE) as j:
                load_expert(j, j)
            sp.wait_ge(r_jobs, C + 1)
            over = sp.value_load(jint[0:1, 3:4], min_val=0, max_val=OVER)
            with sp.If(over > 0):
                with sp.Fori(0, over) as r:
                    e = sp.value_load(jint[0:1, bass.ds(r, 1)], min_val=0, max_val=NE - 1)
                    load_expert(r + NE, e)
            sp.wait_ge(g_dg, C + 6)
            sp.dma_start(gfin, g_final.rearrange("(o d) -> o d", o=1).to_broadcast([P, D])).then_inc(gf_land, 16)
            for tt in range(TT):
                sp.wait_ge(fin, C + tt + 1)
                sp.dma_start(out[0].rearrange("(a p) d -> p a d", p=P)[:, tt, :], xn[:, tt, :]).then_inc(out_land, 16)
            sp.wait_ge(out_land, 16 * TT)

        @block.gpsimd
        def _(pool):
            credits(pool, "pool")
            pool.memset(ident[:, :], 0.0).then_inc(p_self, 1)
            pool.memset(ones[:, :], 1.0).then_inc(p_self, 1)
            pool.memset(tri[:, :], 1.0).then_inc(p_self, 1)
            pool.memset(wmask[:, :], 1.0).then_inc(p_self, 1)
            pool.memset(zpad[:, :, :], 0.0).then_inc(p_self, 1)
            pool.wait_ge(p_self, 5)
            pool.affine_select(out=ident[:, :], in_=ident[:, :], compare_op=ALU.not_equal, fill=1.0,
                               base=0, pattern=[[-1, P]], channel_multiplier=1).then_inc(consts, 1)
            pool.affine_select(out=tri[:, :], in_=tri[:, :], compare_op=ALU.is_gt, fill=0.0,
                               base=0, pattern=[[1, P]], channel_multiplier=-1).then_inc(consts, 1)
            pool.iota(iota_i[:, :], pattern=[[1, P]], base=0, channel_multiplier=0).then_inc(consts, 1)
            n = 5
            for r in range(2):
                lo, hi = 64 * r, 64 * r + 64
                for base, mult, step, cols_ in ((WINC // 2, -1, 1, (0, GRID - WINC)),
                                                (WINC // 2 - 1, 1, -1, (WINC, GRID))):
                    a, z = cols_
                    pool.wait_ge(p_self, n)
                    pool.affine_select(out=wmask[lo:hi, a:z], in_=wmask[lo:hi, a:z], compare_op=ALU.is_ge,
                                       fill=0.0, base=base + step * a, pattern=[[step, z - a]],
                                       channel_multiplier=mult).then_inc(p_self, 1)
                    n += 1
            pool.wait_ge(p_self, n)
            pool.tensor_scalar(wmask[:, :], wmask[:, :], -1.0, 1e30, ALU.add, ALU.mult).then_inc(p_self, 1)
            n += 1
            pool.wait_ge(p_self, n)
            for t in range(2):
                pool.dma_start(zpad[0:120, t, 0:NDC], rpb[0].rearrange("h a b -> (h a) b")[120 * t:120 * t + 120, :])\
                    .then_inc(rpb_land, 16)
            pool.wait_ge(rpb_land, 32)
            pool.wait_ge(gu_hi, C + 2 * MODU)
            for t in range(2):
                for q in range(2):
                    if 2 * t + q:
                        pool.wait_ge(z_land, 16 * (2 * t + q))
                    half = ZW // 2
                    pool.tensor_copy(zrep.rearrange("p (j w) -> p j w", w=GRID + 1),
                                     zpad[0:120, t:t + 1, :].to_broadcast([120, GRID // 2, GRID + 1])).then_inc(p_self, 1)
                    n += 1
                    pool.wait_ge(p_self, n)
                    pool.dma_start(zed[120 * t:120 * t + 120, q * half:(q + 1) * half], zrep).then_inc(z_land, 16)
            with pool.Fori(0, HEADS // 4) as i:
                for b in range(2):
                    pool.wait_ge(bias_land[b], i * 128 + 128)
                    v = bias[b].rearrange("p i (r k) -> p (i r) k", k=GRID)
                    pool.tensor_tensor(v, v, wmask[:, None, :].to_broadcast([P, 16, GRID]), ALU.add).then_inc(t_bias, 1)

        @block.scalar
        def _(act):
            credits(act, "act")

            def hi_half(u, h):
                act.wait_ge(gu_land[u.slot][h], u.uses * 32)
                if h == 0:
                    act.wait_ge(gu_used, u.before + C)
                act.activation(hi_gu[:, u.slot, 4 * h:4 * h + 4, :], raw_gu[:, u.slot, 4 * h:4 * h + 4, :],
                               ACT.Copy).then_inc(gu_hi, 1)

            def hi(u):
                hi_half(u, 0)
                hi_half(u, 1)

            def hi_down(u):
                act.wait_ge(d_land[u.slot], u.uses * 16)
                act.wait_ge(d_used, u.before + C)
                act.activation(hi_d[:, u.slot, :, :], raw_d[:, u.slot, :, :], ACT.Copy).then_inc(d_hi, 1)

            def norm_stats(k, h, residuals, x_rows):
                act.wait_ge(x_land, 32)
                for tt in range(TT):
                    act.wait_ge(res, residuals * 2 + (C + tt - 1))
                    act.sem_inc(act_pace, 1)
                    act.activation(xn[:, tt, :], x_rows(tt), ACT.Square, accum_out=st[:, tt:tt + 1]).then_inc(n_ss, 1)
                act.wait_ge(n_ms, h)
                act.activation(st[:, 4:6], st[:, 2:4], ACT.Sqrt).then_inc(n_sq, 1)

            def stream_stats(k, s, residuals):
                norm_stats(k, k + (C + 1), residuals, lambda tt: h_all[:, s, tt, :])

            def norm(k, s, residuals):
                stream_stats(k, s, residuals)
                norm_hi(k)

            def norm_hi(k):
                for q in range(4):
                    act.wait_ge(n_a, k * 4 + (C + q + 1))
                    act.activation(a_hi[:, 2 * q:2 * q + 2, :], aT[:, 2 * q:2 * q + 2, :], ACT.Copy).then_inc(n_hi, 1)

            def evac_T(u, n, half, dst):
                if half:
                    act.wait_ge(gu_used, u.n + (C + 1))
                else:
                    act.wait_ge(k_mm, n + (C + 1))
                act.activation(dst, pg[:, half, :], ACT.Copy).then_inc(k_ev, 1)

            def gate_row(k):
                act.wait_ge(g_mm, k + (C + 1))
                act.activation(grow, turn_mix[:, :, :].rearrange("p a n -> p (a n)"), ACT.Copy).then_inc(g_ev, 1)

            def swiglu(steps, tiles, q0, gu, du, more=None):
                def step(st_, i, ahead, ahead_d):
                    q = lambda n: (q0 + (st_ + n)) if i is None else (i * 2 + q0 + (st_ + n))
                    act.wait_ge(gu_used, gu(st_, it0(i)).n + (C + 1))
                    act.wait_ge(f_h, q(C))
                    for t in range(tiles):
                        b = t if tiles == 2 else st_ % 2
                        ins = act.activation(sg[:, t, :], pg[:, b, 0:FS], ACT.Silu)
                    ins.then_inc(f_sil, 1)
                    if ahead:
                        hi_half(gu(st_ + 2, it0(i)), 0)
                    last = more and st_ == steps - 1
                    if ahead_d and not last:
                        hi_down(du(st_ + 1, it0(i)))
                    act.wait_ge(f_tr, q(C + 1))
                    act.wait_ge(d_used, q(C))
                    n = tiles * P
                    act.activation(hT_hi[:, :, 0:n], ptr[:, 0:2 * n].rearrange("p (f t) -> p f t", f=2),
                                   ACT.Copy).then_inc(f_hi, 1)
                    if last:
                        more()
                    elif ahead:
                        hi_half(gu(st_ + 2, it0(i)), 1)
                run_steps(act, steps, step, more)

            act.wait_ge(cols, C + 2)
            act.activation(sil[:, :, :], colsB[:, 16:32].rearrange("p (s k) -> p s k", s=NS), ACT.Silu).then_inc(sil_done, 1)
            act.wait_ge(sil_done, C + 1)
            act.activation(sil4[:, :, 0:NS], sil[:, :, :].rearrange("p s k -> p k s"), ACT.Copy).then_inc(sil_done, 1)

            stream_stats(0, 0, 0)

            def mod_step(k, i):
                if k < MODU:
                    hi(gu_mod(k, it0(i)))
                if 1 <= k <= MODU:
                    n = it0(i) * 2 + (k - 1)
                    b = (k - 1) % 2
                    act.wait_ge(gu_used, n + (C + 1))
                    act.wait_ge(ada_mm, n + (C - 1))
                    act.activation(mod_rows[:, b, :], pg[0:4, b, :], ACT.Copy).then_inc(ada_row, 1)
            run_modulation(act, mod_step)

            hi(gu0(0, 0))
            with act.Fori(0, NS) as s:
                norm_hi(s * 2)
                hi(gu0(s, 1))
                for k, unit in enumerate(MIX_ORDER):
                    if k == 0:
                        act.wait_ge(n_lo, s * 8 + (C + 4))
                    for half in range(2):
                        m = 4 * unit + 2 * half
                        evac_T(gu0(s, k), s * 4 + k, half, scr[:, m:m + 2, :].rearrange("p m t -> p (m t)"))
                    if k < 3:
                        hi(gu0(s, k + 2))
                for n, m in enumerate((4, 0)):
                    act.wait_ge(m_y, s * 2 + (C + n + 1))
                    act.activation(a_hi[:, m:m + 4, :], scr[:, m:m + 4, :], ACT.Copy).then_inc(m_hi, 1)
                hi(gu0(s, 5))
                gate_row(s * 2)
                hi(gu0(s, 6))
                norm(s * 2 + 1, s, s * 2 + 1)
                hi(gu0(s, 7))
                hi_down(d0(s, 0))
                act.wait_ge(n_lo, s * 8 + (C + 8))
                gate_row(s * 2 + 1)
                stream_stats(s * 2 + 2, 1 - s, s * 2 + 1)
                swiglu(STEPS0, TT, s * STEPS0, lambda k, i: gu0(s, 6 + k, i), lambda k, i: d0(s, k, i))
                hi(gu0(s + 1, 0))

            norm_hi(NORM_CTX)
            hi(gu1(1))
            for u in range(2):
                for half in range(2):
                    evac_T(gu1(u), T_L1 + u, half, k_ctx[:, 4 * u + 2 * half:4 * u + 2 * half + 2, :].rearrange("p m t -> p (m t)"))
                hi(gu1(u + 2))
                if u == 0:
                    norm_stats(NORM_LAT, C + NORM_LAT + 1, 4, lambda tt: h_all[:, 1, tt, :])
            hi(gu1(4))

            def evac_v(u, tile0):
                act.wait_ge(gu_used, C + u.n + 1)
                act.activation(v_all[:, tile0:tile0 + 2, :].rearrange("p a d -> p (a d)"),
                               py[:, :, :].rearrange("p a n -> p (a n)"), ACT.Copy).then_inc(v_ev, 1)

            act.wait_ge(d_lo, C + D_MOE)
            act.wait_ge(gu_used, C + gu1(3).n + 1)
            norm_hi(NORM_LAT)
            evac_v(gu1(3), 2)
            hi(gu1(5))
            act.wait_ge(n_lo, C + 4 * (NORM_LAT + 1))
            for u in range(4):
                dst = (q_all, k_lat)[u // 2]
                for half in range(2):
                    m = 4 * (u % 2) + 2 * half
                    evac_T(gu1(4 + u), T_L1 + 2 + u, half, dst[:, m:m + 2, :].rearrange("p m t -> p (m t)"))
                hi(gu1(u + 6))
            evac_v(gu1(9), 0)
            act.wait_ge(gu_lo, C + 2 * (GU_L1 + 10))

            def current(i, b):
                if not isinstance(i, int) or i or b:
                    act.wait_ge(t_qk, i * 8 + (C + 4 * b - 4))
                act.wait_ge(k_ev, C + 2 * (T_L1 + 6))
                act.sem_inc(act_pace, 1)
                pair, b2 = bass.ds(i * 2 + b, 1), b % 2
                act.activation(q_cur[:, b2, :], q_all[:, pair, :].rearrange("p o t -> p (o t)"), ACT.Copy)
                act.activation(k_cur[:, b2, 0:T], k_lat[:, pair, :].rearrange("p o t -> p (o t)"), ACT.Copy)
                act.activation(k_cur[:, b2, T:2 * T], k_ctx[:, pair, :].rearrange("p o t -> p (o t)"), ACT.Copy).then_inc(t_cur, 1)

            def exps(i, it):
                act.wait_ge(t_s, i * 8 + (C + it + 1))
                act.activation(prob[:, it % 2, :], prob[:, it % 2, :], ACT.Exp, bias=st[:, 20 + it % 4:21 + it % 4],
                               accum_out=st[:, 12 + it % 4:13 + it % 4]).then_inc(t_e, 1)

            def turned(i, it):
                act.wait_ge(t_tr, i * 8 + (C + it + 1))
                act.wait_ge(t_pv, i * 8 + (C + it - 1))
                act.activation(probT[:, it % 2, :], ptr, ACT.Copy).then_inc(t_pt, 1)

            def pair(i, b, follows):
                n = 4 * b
                exps(i, n + 1)
                turned(i, n)
                if follows:
                    current(i, b + 1)
                exps(i, n + 2)
                turned(i, n + 1)
                exps(i, n + 3)
                turned(i, n + 2)
                if follows:
                    exps(i, n + 4)
                turned(i, n + 3)

            current(0, 0)
            exps(0, 0)
            run_pairs(act, pair)
            for q in range(4):
                act.wait_ge(o_tr, C + q + 1)
                act.activation(a_hi[:, 2 * q:2 * q + 2, :].rearrange("p k t -> p (k t)"), py[:, q, :], ACT.Copy).then_inc(o_hi, 1)
            hi(gu1(10))
            hi(gu1(11))
            gate_row(RES_ATT)
            norm(NORM_FFN, 1, RES_ATT + 1)
            hi(gu1(0, 0))
            act.wait_ge(r_mx, C + 1)
            for tt in range(TT):
                act.activation(small[:, 2 + tt, :], small[:, tt, :], ACT.Exp, bias=st[:, 10 + tt:11 + tt]).then_inc(r_ex, 1)
            hi(gu1(1, 0))
            hi_down(d1(0, 0))

            def gathered(j):
                for h in range(2):
                    act.wait_ge(j_xg, j * 2 + (C + h + 1))
                    act.activation(ag_hi[:, 4 * h:4 * h + 4, :], xg[:, 4 * h:4 * h + 4, :], ACT.Copy).then_inc(j_hi, 1)

            act.wait_ge(r_jobs, C + 1)
            over = act.value_load(jint[0:1, 3:4], min_val=0, max_val=OVER)
            gathered(0)

            def result(j):
                act.wait_ge(d_used, j * STEPSE + (D_MOE + STEPSE + C))
                act.wait_ge(j_comb, j * 2 + C)
                act.activation(ysb, py[:, 2:4, :].rearrange("p a n -> p (a n)"), ACT.Copy).then_inc(j_ysb, 1)

            def job(j, follows):
                def more():
                    gathered(j + 1)
                    hi_down(d1(j, STEPSE))
                    result(j)
                    hi_half(gu1(STEPSE + 1, j), 1)
                swiglu(STEPSE, 1, j * STEPSE + D_MOE, lambda k, i: gu1(k, j, i), lambda k, i: d1(j, k, i),
                       more if follows else None)
                if not follows:
                    result(j)

            with act.Fori(0, over + (NE - 1)) as j:
                job(j, True)
            job(over + (NE - 1), False)
            gate_row(RES_MOE)
            norm_stats(NORM_OUT, C + NORM_OUT + 1, RES_MOE + 1, lambda tt: h_all[:, 1, tt, :])

        @block.vector
        def _(dve):
            credits(dve, "dve")
            dve.memset(low8[:, :, :], 0.0)
            dve.memset(edge[:, :, :], 1.0)
            dve.drain()
            for e in range(1, NE):
                dve.memset(low8[:, e, 0:e], 1.0)
            for g, w in enumerate(WINDOWS):
                for t in range(w // 2):
                    dve.memset(edge[:, g, t:t + 1], w / (t + w // 2))
                for t in range(w - 1 - w // 2):
                    dve.memset(edge[:, g, 15 - t:16 - t], w / (t + 1 + w // 2))
            dve.wait_ge(consts, 3)
            dve.tensor_copy(iota[:, :], iota_i[:, :])
            for n, (dst, rows_) in enumerate(((colsA, P), (colsB, 32))):
                dve.wait_ge(col_tr, C + n + 1)
                dve.tensor_copy(dst[:, :], (pm, ptr)[n][:, 0:rows_]).then_inc(cols, 1)

            def lo_half(u, h):
                dve.wait_ge(gu_hi, u.n * 2 + (C + h + 1))
                k = slice(4 * h, 4 * h + 4)
                dve.tensor_tensor(lo_gu[:, u.slot, k, :], raw_gu[:, u.slot, k, :],
                                  hi_gu[:, u.slot, k, :].bitcast(F32), ALU.subtract).then_inc(gu_lo, 1)

            def lo(u):
                lo_half(u, 0)
                lo_half(u, 1)

            def lo_down(u):
                dve.wait_ge(d_hi, u.n + (C + 1))
                dve.tensor_tensor(lo_d[:, u.slot, :, :], raw_d[:, u.slot, :, :], hi_d[:, u.slot, :, :].bitcast(F32),
                                  ALU.subtract).then_inc(d_lo, 1)

            def rstd(k):
                dve.wait_ge(n_ss, k * 2 + (C + 2))
                dve.tensor_scalar(st[:, 2:4], st[:, 0:2], 1.0 / D, EPS, ALU.mult, ALU.add).then_inc(n_ms, 1)
                dve.wait_ge(n_sq, k + (C + 1))
                dve.reciprocal(st[:, 6:8], st[:, 4:6])
                dve.drain()
                dve.tensor_tensor(st[:, 8:10], st[:, 6:8], st[:, 6:8], ALU.mult)
                dve.drain()
                dve.tensor_tensor(st[:, 8:10], st[:, 8:10], st[:, 2:4], ALU.mult)
                dve.drain()
                dve.tensor_scalar(st[:, 8:10], st[:, 8:10], -0.5, 1.5, ALU.mult, ALU.add)
                dve.drain()
                dve.tensor_tensor(st[:, 6:8], st[:, 6:8], st[:, 8:10], ALU.mult)
                dve.drain()

            def modulate(dst, src, l, half, kt, s):
                gs = gsT[:, l, half, kt, s:s + 1] if isinstance(s, int) else gsT[:, l, half, kt, bass.ds(s, 1)]
                sh = modT[:, l, 3 * half, kt, s:s + 1] if isinstance(s, int) else modT[:, l, 3 * half, kt, bass.ds(s, 1)]
                return dve.tensor_scalar(dst, src, gs, sh, ALU.mult, ALU.add)

            def norm(k, l, half, s):
                norm_rows(k, s)
                norm_cols(k, l, half, s, [py[:, q, :] for q in range(4)])

            def norm_rows(k, s):
                rstd(k)
                for tt in range(TT):
                    dve.tensor_scalar(xn[:, tt, :], h_all[:, s, tt, :], st[:, 6 + tt:7 + tt], None, ALU.mult).then_inc(n_xn, 1)

            def norm_cols(k, l, half, s, banks, between=None):
                for q in range(8 if between else 5):
                    if q < 4:
                        dve.wait_ge(n_tr, k * 4 + (C + q + 1))
                        for kk in range(2):
                            ins = modulate(aT[:, 2 * q + kk, :], banks[q][:, kk * T:kk * T + T], l, half, 2 * q + kk, s)
                        ins.then_inc(n_a, 1)
                    if between:
                        if q == 3:
                            between()
                        q -= 3
                    if q > 0:
                        dve.wait_ge(n_hi, k * 4 + (C + q))
                        v = slice(2 * q - 2, 2 * q)
                        dve.tensor_tensor(a_lo[:, v, :], aT[:, v, :], a_hi[:, v, :].bitcast(F32), ALU.subtract).then_inc(n_lo, 1)

            def gate_col(l, half, s):
                col = modT[:, l, 3 * half + 2, :, s:s + 1] if isinstance(s, int) else modT[:, l, 3 * half + 2, :, bass.ds(s, 1)]
                dve.tensor_copy(gcol[:, :, None], col).then_inc(g_dg, 1)

            def residual(k, s, y=None, done=None):
                dve.wait_ge(g_ev, k + (C + 1))
                for tt in range(TT):
                    if done:
                        dve.wait_ge(*((y_tile, k + (C + 1)) if tt == 0 else done))
                    src = py[:, 2 * tt:2 * tt + 2, :].rearrange("p a n -> p (a n)") if y is None else y[:, tt, :]
                    dve.tensor_tensor(xn[:, tt, :], src, grow, ALU.mult)
                    dve.drain()
                    dve.tensor_tensor(h_all[:, s, tt, :], h_all[:, s, tt, :], xn[:, tt, :], ALU.add).then_inc(res, 1)

            def swiglu(steps, tiles, q0, gu, du, more=None):
                def step(st_, i, ahead, ahead_d):
                    q = lambda n: (q0 + (st_ + n)) if i is None else (i * 2 + q0 + (st_ + n))
                    dve.wait_ge(f_sil, q(C + 1))
                    dve.wait_ge(f_tr, q(C))
                    for t in range(tiles):
                        b = t if tiles == 2 else st_ % 2
                        ins = dve.tensor_tensor(hnat[:, t, :], pg[:, b, FS:2 * FS], sg[:, t, :], ALU.mult)
                    ins.then_inc(f_h, 1)
                    if ahead:
                        lo_half(gu(st_ + 2, it0(i)), 0)
                    last = more and st_ == steps - 1
                    if ahead_d and not last:
                        lo_down(du(st_ + 1, it0(i)))
                    dve.wait_ge(f_hi, q(C + 1))
                    n = tiles * P
                    dve.tensor_tensor(hT_lo[:, :, 0:n], ptr[:, 0:2 * n].rearrange("p (f t) -> p f t", f=2),
                                      hT_hi[:, :, 0:n].bitcast(F32), ALU.subtract).then_inc(f_lo, 1)
                    if last:
                        more()
                    elif ahead:
                        lo_half(gu(st_ + 2, it0(i)), 1)
                run_steps(dve, steps, step, more)

            dve.tensor_tensor(fold, ident[0:4, 0:2], ident[0:4, 2:4], ALU.add)
            dve.wait_ge(sil_done, C + 2)
            dve.tensor_tensor(sil4[:, :, NS:2 * NS], sil[:, :, :].rearrange("p s k -> p k s"),
                              sil4[:, :, 0:NS].bitcast(F32), ALU.subtract)
            dve.drain().then_inc(sil_lo, 1)
            norm_rows(0, 0)
            mv = modT[:, :, :, :, :].rearrange("p l i k s -> p (l i k) s")

            def mod_step(k, i):
                if k < MODU:
                    lo(gu_mod(k, it0(i)))
                if k >= 2:
                    dve.wait_ge(ada_mm, it0(i) * 2 + (C + k - 1))
                    m4 = it0(i) * 8 + 4 * (k - 2)
                    dve.tensor_tensor(mv[:, bass.ds(m4, 4), :], (pm, ptr)[k % 2][:, 0:8].rearrange("p (m s) -> p m s", s=NS),
                                      colsA[:, bass.ds(m4, 4)][:, :, None].to_broadcast([P, 4, NS]), ALU.add).then_inc(ada_ev, 1)
            run_modulation(dve, mod_step)
            dve.drain()
            for l in range(2):
                for half in range(2):
                    g = colsA[:, 96 + 16 * half + 8 * l:96 + 16 * half + 8 * l + 8]
                    ins = dve.scalar_tensor_tensor(out=gsT[:, l, half, :, :], in0=modT[:, l, 3 * half + 1, :, :], scalar=1.0,
                                                   in1=g[:, :, None].to_broadcast([P, KD, NS]), op0=ALU.add, op1=ALU.mult)
            dve.drain()

            turned_early = (pg[:, 0, :], pg[:, 1, :], ptr, pm)
            lo(gu0(0, 0))
            with dve.Fori(0, NS) as s:
                gate_col(0, 0, s)
                norm_cols(s * 2, 0, 0, s, turned_early)
                lo(gu0(s, 1))
                padA = hnat[:, :, :].rearrange("p a n -> p (a n)")
                padB = sg[:, :, :].rearrange("p a n -> p (a n)")
                for g, w in enumerate(WINDOWS):
                    if g:
                        dve.drain()
                    if g == 2:
                        lo(gu0(s, 2))
                    if g % 2 == 0:
                        dve.wait_ge(k_ev, s * 8 + (C + 1 + g // 2))
                    dve.memset(padA[:, 0:16], 0.0)
                    dve.memset(padA[:, 16 + T:32 + T], 0.0)
                    dve.tensor_copy(padA[:, 16:16 + T], scr[:, 12 + g, :])
                    dve.drain()
                    src, dst, n, back_, fwd = padA, padB, 1, 1, 0
                    lo_, hi_ = 0, T + 32
                    while n < w:
                        lo_, hi_ = lo_ + back_, hi_ - fwd
                        dve.tensor_tensor(dst[:, lo_:hi_], src[:, lo_ - back_:hi_ - back_], src[:, lo_ + fwd:hi_ + fwd], ALU.add)
                        dve.drain()
                        src, dst, n = dst, src, 2 * n
                        back_ = fwd = n // 2
                    for a, e in ((16, 0), (16 + T - 8, 8)):
                        dve.tensor_tensor(src[:, a:a + 8], src[:, a:a + 8], edge[:, g, e:e + 8], ALU.mult)
                    dve.drain()
                    ins = dve.scalar_tensor_tensor(out=scr[:, 12 + g, :], in0=src[:, 16:16 + T], scalar=1.0 / w,
                                                   in1=scr[:, 12 + g, :], op0=ALU.mult, op1=ALU.subtract)
                ins.then_inc(m_diff, 1)
                lo(gu0(s, 3))
                dve.wait_ge(k_ev, s * 8 + (C + 6))
                dve.tensor_tensor(scr[:, 4:8, :], scr[:, 4:8, :], scr[:, 8:12, :], ALU.mult)
                dve.drain()
                for m in range(4):
                    dve.tensor_scalar(scr[:, 8 + m, :], scr[:, 4 + m, :], colsB[:, 4 + m:5 + m], None, ALU.mult)
                dve.drain()
                lo(gu0(s, 4))
                for m in range(4):
                    dve.scalar_tensor_tensor(out=scr[:, 8 + m, 1:T], in0=scr[:, 4 + m, 0:T - 1], scalar=colsB[:, m:m + 1],
                                             in1=scr[:, 8 + m, 1:T], op0=ALU.mult, op1=ALU.add)
                dve.drain()
                for m in range(4):
                    dve.scalar_tensor_tensor(out=scr[:, 8 + m, 0:T - 1], in0=scr[:, 4 + m, 1:T], scalar=colsB[:, 8 + m:9 + m],
                                             in1=scr[:, 8 + m, 0:T - 1], op0=ALU.mult, op1=ALU.add)
                dve.drain()
                dve.wait_ge(m_pool, s + (C + 1))
                for g in range(4):
                    ins = dve.tensor_scalar(scr[:, 4 + g, :], py[:, g // 2, (g % 2) * T:(g % 2) * T + T],
                                            colsB[:, 12 + g:13 + g], None, ALU.mult)
                ins.then_inc(m_y, 1)
                dve.wait_ge(k_ev, s * 8 + (C + 8))
                dve.tensor_tensor(scr[:, 0:4, :], scr[:, 0:4, :], scr[:, 8:12, :], ALU.mult).then_inc(m_y, 1)
                for n, m in enumerate((4, 0)):
                    dve.wait_ge(m_hi, s * 2 + (C + n + 1))
                    dve.tensor_tensor(a_lo[:, m:m + 4, :], scr[:, m:m + 4, :], a_hi[:, m:m + 4, :].bitcast(F32),
                                      ALU.subtract).then_inc(m_lo, 1)
                lo(gu0(s, 5))
                lo(gu0(s, 6))
                residual(s * 2, s, done=(gu_used, gu0(s, 5).n + (C + 1)))
                gate_col(0, 1, s)
                norm(s * 2 + 1, 0, 1, s)
                lo(gu0(s, 7))
                lo_down(d0(s, 0))
                norm_rows(s * 2 + 2, 1 - s)
                swiglu(STEPS0, TT, s * STEPS0, lambda k, i: gu0(s, 6 + k, i), lambda k, i: d0(s, k, i))
                lo(gu0(s + 1, 0))
                residual(s * 2 + 1, s, done=(d_used, s * STEPS0 + (STEPS0 + C)))

            norm_cols(NORM_CTX, 1, 0, 0, turned_early)
            lo(gu1(1))
            lo(gu1(2))
            norm_rows(NORM_LAT, 1)
            lo(gu1(3))
            norm_cols(NORM_LAT, 1, 0, 1, turned_early, lambda: lo(gu1(4)))
            for n in range(5, 10):
                lo(gu1(n))

            def scores(i, it):
                b, n = it // 4 % 2, it % 4
                if n == 0:
                    dve.wait_ge(t_bias, i * 2 + (C + it // 4 + 1))
                dve.wait_ge(t_qk, i * 8 + (C + it + 1))
                dve.wait_ge(t_tr, i * 8 + (C + it - 1))
                p_ = prob[:, it % 2, :]
                dve.scalar_tensor_tensor(out=p_[:, 0:T], in0=pg[:, it % 2, 0:T], scalar=HD ** -0.5,
                                         in1=bias[b][:, n, :], op0=ALU.mult, op1=ALU.add)
                dve.tensor_scalar(p_[:, T:2 * T], pg[:, it % 2, T:2 * T], HD ** -0.5, None, ALU.mult)
                dve.drain()
                dve.tensor_reduce(st[:, 20 + n:21 + n], p_, AXX, ALU.max)
                dve.drain()
                dve.tensor_scalar(st[:, 20 + n:21 + n], st[:, 20 + n:21 + n], -1.0, None, ALU.mult).then_inc(t_s, 1)

            def outs(i, it):
                n = it % 4
                dve.wait_ge(t_pv, i * 8 + (C + it + 1))
                dve.reciprocal(st[:, 16 + n:17 + n], st[:, 12 + n:13 + n])
                dve.drain()
                col = i * (4 * HD) + it // 2 * HD
                dve.tensor_scalar(o_nat[:, it % 2, bass.ds(col, HD)], py[:, n, 0:HD], st[:, 16 + n:17 + n],
                                  None, ALU.mult).then_inc(t_o, 1)

            def pair(i, b, follows):
                n = 4 * b
                scores(i, n + 2)
                outs(i, n)
                scores(i, n + 3)
                outs(i, n + 1)
                if follows:
                    scores(i, n + 4)
                outs(i, n + 2)
                if follows:
                    scores(i, n + 5)
                outs(i, n + 3)

            scores(0, 0)
            scores(0, 1)
            run_pairs(dve, pair)
            for q in range(4):
                dve.wait_ge(o_hi, C + q + 1)
                dve.tensor_tensor(a_lo[:, 2 * q:2 * q + 2, :].rearrange("p k t -> p (k t)"), py[:, q, :],
                                  a_hi[:, 2 * q:2 * q + 2, :].rearrange("p k t -> p (k t)").bitcast(F32), ALU.subtract).then_inc(o_lo, 1)
            gate_col(1, 0, 1)
            lo(gu1(10))
            lo(gu1(11))
            residual(RES_ATT, 1, done=(gu_used, C + gu1(11).n + 1))
            norm(NORM_FFN, 1, 1, 1)
            dve.memset(acc[:, :, :], 0.0)
            lo(gu1(0, 0))

            dve.wait_ge(r_lg, C + 1)
            dve.tensor_copy(small[:, 0:2, :], pm[:, 0:2 * NE].rearrange("p (a e) -> p a e", a=TT))
            dve.drain()
            dve.tensor_reduce(st[:, 8:10], small[:, 0:2, :], AXX, ALU.max)
            dve.drain()
            dve.tensor_scalar(st[:, 10:12], st[:, 8:10], -1.0, None, ALU.mult).then_inc(r_mx, 1)
            cmp16 = sg[:, 0, 0:TT * NE * NE].rearrange("p (a e) -> p a e", e=NE)
            for tt in range(TT):
                l_ = small[:, tt, :]
                dve.tensor_tensor(cmp16[:, tt * NE:tt * NE + NE, :], l_[:, None, :].to_broadcast([P, NE, NE]),
                                  l_[:, :, None].to_broadcast([P, NE, NE]), ALU.is_equal)
            dve.drain()
            for tt in range(TT):
                dve.tensor_tensor(cmp16[:, tt * NE:tt * NE + NE, :], cmp16[:, tt * NE:tt * NE + NE, :], low8[:, :, :], ALU.mult)
            dve.drain()
            rank = small[:, 4:8, :].rearrange("p a e -> p (a e)")
            dve.tensor_reduce(rank[:, 0:TT * NE], cmp16, AXX, ALU.add)
            dve.drain()
            for tt in range(TT):
                l_ = small[:, tt, :]
                dve.tensor_tensor(cmp16[:, tt * NE:tt * NE + NE, :], l_[:, None, :].to_broadcast([P, NE, NE]),
                                  l_[:, :, None].to_broadcast([P, NE, NE]), ALU.is_gt)
            dve.drain()
            dve.tensor_reduce(rank[:, TT * NE:2 * TT * NE], cmp16, AXX, ALU.add)
            dve.drain()
            dve.tensor_tensor(small[:, 4:6, :], small[:, 4:6, :], small[:, 6:8, :], ALU.add)
            dve.drain()
            dve.tensor_scalar(route[:, 0:TT, :], small[:, 4:6, :], TOPK - 0.5, None, ALU.is_lt)
            dve.drain().then_inc(r_mask, 1)
            dve.wait_ge(r_ex, C + 2)
            for tt in range(TT):
                dve.tensor_tensor(small[:, 2 + tt, :], small[:, 2 + tt, :], route[:, tt, :], ALU.mult)
            dve.drain()
            dve.tensor_reduce(st[:, 12:14], small[:, 2:4, :], AXX, ALU.add)
            dve.drain()
            dve.reciprocal(st[:, 14:16], st[:, 12:14])
            dve.drain()
            for tt in range(TT):
                dve.tensor_scalar(route[:, 4 + tt, :], small[:, 2 + tt, :], st[:, 14 + tt:15 + tt], None, ALU.mult)
            dve.wait_ge(r_pos, C + 1)
            dve.tensor_copy(route[:, 2:4, :], pm[:, 32:48].rearrange("p (a e) -> p a e", a=TT))
            dve.tensor_scalar(small[:, 4, :], pm[:, 48:56], CAP + 0.5, None, ALU.is_gt)
            dve.drain()
            dve.tensor_tensor(cmp8, small[:, 4, :][:, None, :].to_broadcast([P, NE, NE]), low8[:, :, :], ALU.mult)
            dve.drain()
            dve.tensor_reduce(small[:, 5, :], cmp8, AXX, ALU.add)
            dve.tensor_reduce(st[:, 16:17], small[:, 4, :], AXX, ALU.add)
            dve.drain()
            for r in range(OVER):
                dve.scalar_tensor_tensor(out=sel[:, r, :], in0=small[:, 5, :], scalar=float(r), in1=small[:, 4, :],
                                         op0=ALU.is_equal, op1=ALU.mult)
            dve.tensor_copy(jobs[:, :, 0:NE], route)
            dve.drain()
            for r in range(OVER):
                dve.tensor_tensor(cmp8[:, 0:6, :], route, sel[:, r, :][:, None, :].to_broadcast([P, 6, NE]), ALU.mult)
                dve.drain()
                dve.tensor_reduce(jobs[:, :, NE + r], cmp8[:, 0:6, :], AXX, ALU.add)
                dve.drain()
                dve.tensor_scalar(jobs[:, 2:4, NE + r], jobs[:, 2:4, NE + r], -float(CAP), None, ALU.add)
            dve.tensor_tensor(cmp8[:, 0:OVER, :], sel, iota[:, 0:NE][:, None, :].to_broadcast([P, OVER, NE]), ALU.mult)
            dve.drain()
            dve.tensor_reduce(st[:, 17:17 + OVER], cmp8[:, 0:OVER, :], AXX, ALU.add)
            dve.drain()
            dve.tensor_copy(jint[:, 0:OVER], st[:, 17:17 + OVER])
            dve.tensor_copy(jint[:, 3:4], st[:, 16:17])
            dve.drain().then_inc(r_jobs, 1)
            dve.wait_ge(r_jobs, C + 1)
            over = dve.value_load(jint[0:1, 3:4], min_val=0, max_val=OVER)

            def picks(j, first=False):
                if not first:
                    dve.wait_ge(j_gat, j * 2 + C)
                    dve.wait_ge(j_bt, j + C)
                for tt in range(TT):
                    dve.tensor_scalar(pick[:, tt, :], iota[:, :], jobs[:, 2 + tt, bass.ds(j, 1)],
                                      jobs[:, tt, bass.ds(j, 1)], ALU.is_equal, ALU.mult)
                dve.drain()
                for tt in range(TT):
                    ins = dve.tensor_scalar(pickg[:, tt, :], pick[:, tt, :], jobs[:, 4 + tt, bass.ds(j, 1)], None, ALU.mult)
                ins.then_inc(j_pick, 1)

            def gathered(j):
                for h in range(2):
                    dve.wait_ge(j_gat, j * 2 + (C + h + 1))
                    for kt in range(4 * h, 4 * h + 4):
                        ins = modulate(xg[:, kt, :], py[:, h, (kt % 4) * P:(kt % 4) * P + P], 1, 1, kt, 1)
                    ins.then_inc(j_xg, 1)
                for h in range(2):
                    dve.wait_ge(j_hi, j * 2 + (C + h + 1))
                    v = slice(4 * h, 4 * h + 4)
                    dve.tensor_tensor(ag_lo[:, v, :], xg[:, v, :], ag_hi[:, v, :].bitcast(F32), ALU.subtract).then_inc(j_lo, 1)

            def gates_back(j):
                dve.wait_ge(j_bt, j + (C + 1))
                dve.tensor_copy(back, ptr[:, 0:T].rearrange("p (a t) -> p a t", a=TT)).then_inc(j_back, 1)

            def accumulate(j, tt):
                dve.wait_ge(j_comb, j * 2 + (C + tt + 1))
                dve.tensor_tensor(acc[:, tt, :], acc[:, tt, :], py[:, 0:2, :].rearrange("p a n -> p (a n)"), ALU.add).then_inc(j_acc, 1)

            picks(0, True)
            lo_half(gu1(1, 0), 0)
            gathered(0)
            gates_back(0)
            lo_half(gu1(1, 0), 1)
            lo_down(d1(0, 0))

            def job(j, follows):
                def more():
                    gathered(j + 1)
                    lo_down(d1(j, STEPSE))
                    accumulate(j, 0)
                    lo_half(gu1(STEPSE + 1, j), 1)
                    accumulate(j, 1)
                    gates_back(j + 1)
                if follows:
                    picks(j + 1)
                swiglu(STEPSE, 1, j * STEPSE + D_MOE, lambda k, i: gu1(k, j, i), lambda k, i: d1(j, k, i),
                       more if follows else None)
                if not follows:
                    for tt in range(TT):
                        accumulate(j, tt)

            with dve.Fori(0, over + (NE - 1)) as j:
                job(j, True)
            job(over + (NE - 1), False)
            dve.drain()
            gate_col(1, 1, 1)
            residual(RES_MOE, 1, acc)
            rstd(NORM_OUT)
            dve.wait_ge(gf_land, 16)
            for tt in range(TT):
                dve.scalar_tensor_tensor(out=xn[:, tt, :], in0=h_all[:, 1, tt, :], scalar=st[:, 6 + tt:7 + tt],
                                         in1=gfin, op0=ALU.mult, op1=ALU.mult).then_inc(fin, 1)

        @block.tensor
        def _(pe):
            credits(pe, "pe")
            pe.wait_ge(consts, 3)
            pe.wait_ge(rows_land, 16 * 7)
            pe.transpose(pm[:, 0:P], rowsA, ident[:, :]).then_inc(col_tr, 1)
            pe.transpose(ptr[:, 0:32], rowsB[0:32, :], ident[0:32, 0:32]).then_inc(col_tr, 1)
            pe.wait_ge(sil_lo, C + 1)

            def mod_step(k, i):
                n = it0(i) * 2 + k
                if k < MODU:
                    pe.wait_ge(gu_lo, n * 2 + (C + 2))
                    if k >= 2:
                        pe.wait_ge(ada_row, n + (C - 1))
                    for kt in range(KD):
                        for part in (hi_gu, lo_gu):
                            mm = pe.matmul(pg[0:4, k % 2, :], sil4[:, kt, :], part[:, k % 2, kt, :],
                                           start=kt == 0 and part is hi_gu, stop=kt == KD - 1 and part is lo_gu)
                    mm.then_inc(gu_used, 1)
                if 1 <= k <= MODU:
                    b = (k - 1) % 2
                    pe.wait_ge(ada_row, n + C)
                    pe.wait_ge(ada_ev, n + (C - 2))
                    for m in range(4):
                        mm = pe.matmul((pm, ptr)[b][:, NS * m:NS * m + NS], mod_rows[:, b, m * P:m * P + P], fold,
                                       start=True, stop=True)
                    mm.then_inc(ada_mm, 1)
            run_modulation(pe, mod_step)

            def three(dst, a, b, first, last):
                pe.matmul(dst, a[0], b[0], start=first, stop=False)
                pe.matmul(dst, a[1], b[0], start=False, stop=False)
                return pe.matmul(dst, a[0], b[1], start=False, stop=last)

            def norm(k, banks=tuple(py[:, q, :] for q in range(4))):
                for tt in range(TT):
                    pe.wait_ge(n_xn, k * 2 + (C + tt + 1))
                    for q in range(4):
                        for kk in range(2):
                            kt = 2 * q + kk
                            mm = pe.transpose(banks[q][:, kk * T + tt * P:kk * T + tt * P + P],
                                              xn[:, tt, kt * P:kt * P + P], ident[:, :])
                        if tt:
                            mm.then_inc(n_tr, 1)

            def wait_a(k, kt):
                if k is not None and kt % 2 == 0:
                    pe.wait_ge(n_lo, k * 4 + (C + kt // 2 + 1))

            def wcols(u, kt, a, z):
                return hi_gu[:, u.slot, kt, a:z], lo_gu[:, u.slot, kt, a:z]

            def project_T(u, n, k=None):
                pe.wait_ge(gu_lo, u.n * 2 + (C + 2))
                for half in range(2):
                    pe.wait_ge(k_ev, n * 2 + (C + half - 1))
                    for m in (2 * half, 2 * half + 1):
                        for kt in range(KD):
                            wait_a(k if m == 0 else None, kt)
                            mm = three(pg[:, half, (m % 2) * T:(m % 2) * T + T], wcols(u, kt, m * P, m * P + P),
                                       (a_hi[:, kt, :], a_lo[:, kt, :]), kt == 0, kt == KD - 1)
                    mm.then_inc(gu_used if half else k_mm, 1)

            def project_rows(u, nh, order=range(KD), halves=None, tile_done=False):
                pe.wait_ge(gu_lo, u.n * 2 + (C + 2))
                for tt in range(TT):
                    for n, kt in enumerate(order):
                        if halves and tt == 0 and n % 4 == 0:
                            pe.wait_ge(halves[0], halves[1] + n // 4)
                        mm = three(py[:, 2 * tt + nh, :], (a_hi[:, kt, tt * P:tt * P + P], a_lo[:, kt, tt * P:tt * P + P]),
                                   wcols(u, kt, 0, UC), n == 0, n == KD - 1)
                    if tile_done and tt == 0:
                        mm.then_inc(y_tile, 1)
                mm.then_inc(gu_used, 1)

            def gate_rows(k):
                pe.wait_ge(g_dg, k + (C + 1))
                for kt in range(KD):
                    mm = pe.matmul(turn_mix[:, kt // 4, (kt % 4) * P:(kt % 4) * P + P], gcol[:, kt:kt + 1].to_broadcast([P, P]),
                                   ident[:, :], start=True, stop=True)
                mm.then_inc(g_mm, 1)

            def products(tiles, u, b, part, k=None):
                acts = (a_hi, a_lo) if tiles == 2 else (ag_hi, ag_lo)
                for kt in range(KD) if tiles == 2 else range(4 * part, 4 * part + 4):
                    wait_a(k, kt)
                    mm = three(pg[:, b, :], tuple(x_[:, kt, part * P:part * P + P] if tiles == 2 else x_[:, kt, :] for x_ in acts),
                               wcols(u, kt, 0, 2 * FS), kt == 0, kt == KD - 1)
                return mm

            def swiglu(steps, tiles, q0, gu, du, yb, done_h=None, before_down=None, a_norm=None):
                def up(u, st_, q, part, k=None):
                    b = part if tiles == 2 else st_ % 2
                    if part == 0 or tiles == 2:
                        pe.wait_ge(f_h, q(C) if tiles == 2 else q(C - 1))
                    if part == 0:
                        pe.wait_ge(gu_lo, u.n * 2 + (C + 2 if tiles == 2 else C + 1))
                    elif tiles == 1:
                        pe.wait_ge(gu_lo, u.n * 2 + (C + 2))
                    mm = products(tiles, u, b, part, k)
                    if part == 1:
                        mm.then_inc(gu_used, 1)

                def step(st_, i, ahead_, ahead):
                    q = lambda n: (q0 + (st_ + n)) if i is None else (i * 2 + q0 + (st_ + n))
                    if ahead:
                        up(gu(st_ + 1, it0(i)), st_ + 1, lambda n: q(n + 1), 0)
                    pe.wait_ge(f_h, q(C + 1))
                    if st_ == 0 and done_h:
                        pe.wait_ge(*done_h)
                    pe.wait_ge(f_lo, q(C))
                    for f in range(2):
                        for t in range(tiles):
                            mm = pe.transpose(ptr[:, (f * tiles + t) * P:(f * tiles + t) * P + P],
                                              hnat[:, t, f * P:f * P + P], ident[:, :])
                    mm.then_inc(f_tr, 1)
                    if st_ == steps - 1 and before_down:
                        before_down()
                    if ahead:
                        up(gu(st_ + 1, it0(i)), st_ + 1, lambda n: q(n + 1), 1)
                    u = du(st_, it0(i))
                    pe.wait_ge(f_lo, q(C + 1))
                    pe.wait_ge(d_lo, u.n + (C + 1))
                    for t in range(tiles):
                        for nh in range(2):
                            for f in range(2):
                                mm = three(py[:, yb + 2 * t + nh, :], (hT_hi[:, f, t * P:t * P + P], hT_lo[:, f, t * P:t * P + P]),
                                           (hi_d[:, u.slot, f, nh * 512:nh * 512 + 512], lo_d[:, u.slot, f, nh * 512:nh * 512 + 512]),
                                           st_ == 0 and f == 0, st_ == steps - 1 and i is None and f == 1)
                        if tiles == 2 and t == 0 and st_ == steps - 1 and i is None:
                            mm.then_inc(y_tile, 1)
                    mm.then_inc(d_used, 1)

                if tiles == 2:
                    for part in range(2):
                        up(gu(0, 0), 0, lambda n: q0 + n, part, a_norm if part == 0 else None)
                run_steps(pe, steps, step)

            early = (pg[:, 0, :], pg[:, 1, :], ptr, pm)
            pe.wait_ge(ada_ev, C + MODU)
            norm(0, early)
            with pe.Fori(0, NS) as s:
                def turn_next():
                    pe.wait_ge(f_lo, s * STEPS0 + (C + STEPS0))
                    norm(s * 2 + 2, early)
                for k in range(3):
                    project_T(gu0(s, k), s * 4 + k, s * 2 if k == 0 else None)
                pe.wait_ge(m_diff, s + (C + 1))
                pe.wait_ge(cst_land, 32)
                for g in range(4):
                    mm = pe.matmul(py[:, g // 2, (g % 2) * T:(g % 2) * T + T], poolw[:, g, :], scr[:, 12 + g, :],
                                   start=True, stop=True)
                mm.then_inc(m_pool, 1)
                project_T(gu0(s, 3), s * 4 + 3)
                gate_rows(s * 2)
                project_rows(gu0(s, 4), 0, (4, 5, 6, 7, 0, 1, 2, 3), (m_lo, s * 2 + (C + 1)))
                project_rows(gu0(s, 5), 1, tile_done=True)
                norm(s * 2 + 1)
                gate_rows(s * 2 + 1)
                swiglu(STEPS0, TT, s * STEPS0, lambda k, i: gu0(s, 6 + k, i), lambda k, i: d0(s, k, i), 0,
                       (g_ev, s * 2 + (C + 2)), turn_next, a_norm=s * 2 + 1)

            for u in range(2):
                project_T(gu1(u), T_L1 + u, None if u else NORM_CTX)
            pe.wait_ge(k_ev, C + 2 * (T_L1 + 2))
            norm(NORM_LAT, early)
            for nh in range(2):
                project_rows(gu1(2 + nh), nh)
            for u in range(4):
                project_T(gu1(4 + u), T_L1 + 2 + u, None if u else NORM_LAT)
            pe.wait_ge(v_ev, C + 1)
            for nh in range(2):
                project_rows(gu1(8 + nh), nh)
            pe.wait_ge(v_ev, C + 2)
            pe.wait_ge(k_ev, C + 2 * (T_L1 + 6))

            def score(i, it):
                b, n = it // 4 % 2, it % 4
                if n == 0:
                    pe.wait_ge(t_cur, i * 2 + (C + it // 4 + 1))
                pe.wait_ge(t_s, i * 8 + (C + it - 1))
                rows = slice(HD * (n // 2), HD * (n // 2) + HD)
                pe.matmul(pg[:, it % 2, :], q_cur[rows, b, (it % 2) * P:(it % 2) * P + P], k_cur[rows, b, :],
                          start=True, stop=True).then_inc(t_qk, 1)

            def turn(i, it):
                pe.wait_ge(t_e, i * 8 + (C + it + 1))
                pe.wait_ge(t_pt, i * 8 + (C + it))
                for kt in range(4):
                    mm = pe.transpose(ptr[:, kt * P:kt * P + P], prob[:, it % 2, kt * P:kt * P + P], ident[:, :])
                mm.then_inc(t_tr, 1)

            def weigh(i, it):
                pe.wait_ge(t_pt, i * 8 + (C + it + 1))
                pe.wait_ge(t_o, i * 8 + (C + it - 3))
                col = i * (4 * HD) + it // 2 * HD
                for kt in range(4):
                    mm = pe.matmul(py[:, it % 4, 0:HD], probT[:, it % 2, kt * P:kt * P + P],
                                   v_all[:, kt, bass.ds(col, HD)], start=kt == 0, stop=kt == 3)
                mm.then_inc(t_pv, 1)

            def pair(i, b, follows):
                n = 4 * b
                turn(i, n)
                score(i, n + 2)
                turn(i, n + 1)
                weigh(i, n)
                score(i, n + 3)
                turn(i, n + 2)
                weigh(i, n + 1)
                if follows:
                    score(i, n + 4)
                turn(i, n + 3)
                weigh(i, n + 2)
                if follows:
                    score(i, n + 5)
                weigh(i, n + 3)

            score(0, 0)
            score(0, 1)
            run_pairs(pe, pair)
            pe.wait_ge(t_o, C + 2 * HEADS)
            for q in range(4):
                for kk in range(2):
                    for tt in range(TT):
                        kt = 2 * q + kk
                        mm = pe.transpose(py[:, q, kk * T + tt * P:kk * T + tt * P + P], o_nat[:, tt, kt * P:kt * P + P], ident[:, :])
                mm.then_inc(o_tr, 1)
            gate_rows(RES_ATT)
            pe.wait_ge(o_lo, C + 4)
            for k in range(2):
                project_rows(gu1(10 + k), k, tile_done=k == 1)
            norm(NORM_FFN)

            pe.wait_ge(n_a, C + 4 * (NORM_FFN + 1))
            for tt in range(TT):
                for kt in range(KD):
                    mm = pe.matmul(pm[:, tt * NE:tt * NE + NE], aT[:, kt, tt * P:tt * P + P], wr[:, kt, :],
                                   start=kt == 0, stop=kt == KD - 1)
            mm.then_inc(r_lg, 1)
            pe.wait_ge(r_mask, C + 1)
            for dst, terms in ((32, ((tri, 0),)), (40, ((ones, 0), (tri, 1))), (48, ((ones, 0), (ones, 1)))):
                for n, (m_, tt) in enumerate(terms):
                    mm = pe.matmul(pm[:, dst:dst + NE], m_[:, :], route[:, tt, :], start=n == 0, stop=n == len(terms) - 1)
            mm.then_inc(r_pos, 1)
            pe.wait_ge(r_jobs, C + 1)
            over = pe.value_load(jint[0:1, 3:4], min_val=0, max_val=OVER)

            def gather(j):
                pe.wait_ge(j_pick, j + (C + 1))
                for h in range(2):
                    for kt in range(4 * h, 4 * h + 4):
                        for tt in range(TT):
                            mm = pe.matmul(py[:, h, (kt % 4) * P:(kt % 4) * P + P], xn[:, tt, kt * P:kt * P + P],
                                           pick[:, tt, :], start=tt == 0, stop=tt == TT - 1)
                    mm.then_inc(j_gat, 1)

            def first_up(j, part):
                q0 = j * STEPSE + D_MOE
                if part == 0:
                    pe.wait_ge(f_h, q0 + (C - 1))
                u = gu1(0, j)
                pe.wait_ge(gu_lo, u.n * 2 + (C + part + 1))
                pe.wait_ge(j_lo, j * 2 + (C + part + 1))
                mm = products(1, u, 0, part)
                if part == 1:
                    mm.then_inc(gu_used, 1)

            def gates_back(j):
                pe.wait_ge(f_lo, j * STEPSE + (D_MOE + C))
                for tt in range(TT):
                    mm = pe.transpose(ptr[:, tt * P:tt * P + P], pickg[:, tt, :], ident[:, :])
                mm.then_inc(j_bt, 1)

            def combine(j, tt):
                if tt == 0:
                    pe.wait_ge(j_ysb, j + (C + 1))
                else:
                    pe.wait_ge(j_acc, j * 2 + (C + 1))
                for nh in range(2):
                    mm = pe.matmul(py[:, nh, :], back[:, tt, :], ysb[:, nh * 512:nh * 512 + 512], start=True, stop=True)
                mm.then_inc(j_comb, 1)

            gather(0)
            for part in range(2):
                first_up(0, part)
            gates_back(0)

            def job(j, follows):
                def gather_next():
                    pe.wait_ge(j_acc, j * 2 + C)
                    gather(j + 1)
                swiglu(STEPSE, 1, j * STEPSE + D_MOE, lambda k, i: gu1(k, j, i), lambda k, i: d1(j, k, i), 2,
                       (j_back, j + (C + 1)), gather_next if follows else None)
                if follows:
                    first_up(j + 1, 0)
                    pe.wait_ge(j_xg, j * 2 + (C + 4))
                combine(j, 0)
                if follows:
                    first_up(j + 1, 1)
                combine(j, 1)
                if follows:
                    gates_back(j + 1)

            with pe.Fori(0, over + (NE - 1)) as j:
                job(j, True)
            job(over + (NE - 1), False)
            gate_rows(RES_MOE)


_INS = ['x', 'c', 'ctx', 'c_ctx', 'w_mod', 'b_mod', 'g_mix', 'g_ffn', 'g_final', 'w_in_ab', 'conv_w', 'pool_w',
        'pool_scale', 'w_out_ab', 'w_ff_gate', 'w_ff_up', 'w_ff_down', 'w_qkv', 'rpb', 'w_out_na', 'w_router',
        'we_gate', 'we_up', 'we_down']


def kernel(**inputs):
    import numpy as _np
    import concourse.bacc as _bacc
    from concourse.bass_utils import run_bass_kernel_spmd as _run

    nc = _bacc.Bacc("TRN2", target_bir_lowering=False, num_devices=1)
    arrays, args = {}, []
    for name in _INS:
        a = _np.ascontiguousarray(inputs[name])
        arrays[f"in_{name}_dram"] = a
        args.append(nc.dram_tensor(f"in_{name}_dram", a.shape, mybir.dt.from_np(a.dtype), kind="ExternalInput").ap())
    args.append(nc.dram_tensor("out_0_dram", (1, T, D), F32, kind="ExternalOutput").ap())
    backbone(nc, *args)
    r = _run(nc, [arrays], core_ids=[0])
    return r.results[0]["out_0_dram"]
```
